# Optimizing a Trainium2 kernel written in Bass

```python
import math
import jax, jax.numpy as jnp
from jax import lax
import numpy as np

D_MODEL = 1024
BATCH = 1
SEQ = 512
DEPTH = 1

HEAD_DIM = 64
A_HEADS = 4
A_VDIM = 2 * HEAD_DIM
B_HEADS = 8
B_KV_HEADS = 2
B_WINDOW = 128
C_HEADS = 8
C_KV_HEADS = 2
CMP_BLOCK = 32
CMP_STRIDE = 16
CMP_HIDDEN = 256
SEL_BLOCK = 64
N_SELECT = 16
C_WINDOW = 512
MIX_WIDTH = B_HEADS * HEAD_DIM
N_BRANCH = 3
D_FF = 4 * D_MODEL
NUM_BUCKETS = 32
MAX_DISTANCE = 128
TOTAL_HEADS = A_HEADS + B_HEADS + C_HEADS
Q_BLOCK = 128
SEL_Q_BLOCK = 64
NEG_INF = -1e30
FORCE_BONUS = 1e4
EPS = 1e-6

SPLIT_SIZES = (
    A_HEADS * 2 * HEAD_DIM,
    A_HEADS * 2 * HEAD_DIM,
    A_HEADS * A_VDIM,
    B_HEADS * HEAD_DIM,
    B_KV_HEADS * HEAD_DIM,
    B_KV_HEADS * HEAD_DIM,
    C_HEADS * HEAD_DIM,
    6 * C_KV_HEADS * HEAD_DIM,
    C_HEADS * 3,
    N_BRANCH * D_MODEL,
)
IN_COLS = sum(SPLIT_SIZES)


def rms_norm(x, g):
    xf = x.astype(jnp.float32)
    y = xf * lax.rsqrt(jnp.mean(xf * xf, axis=-1, keepdims=True) + EPS)
    return (y * g.astype(jnp.float32)).astype(x.dtype)

def rel_bucket(dist):
    n = jnp.maximum(dist, 0)
    max_exact = NUM_BUCKETS // 2
    nf = jnp.maximum(n, 1).astype(jnp.float32)
    large = max_exact + (jnp.log(nf / max_exact) / math.log(MAX_DISTANCE / max_exact)
                         * (NUM_BUCKETS - max_exact)).astype(jnp.int32)
    large = jnp.minimum(large, NUM_BUCKETS - 1)
    return jnp.where(n < max_exact, n, large)

def diff_attention(q, k, v, lam, bias_tab):
    B, S, H, _, D = q.shape
    nb = S // Q_BLOCK
    scale = D ** -0.5
    k_pos = jnp.arange(S)
    qb = q.reshape(B, nb, Q_BLOCK, H, 2, D).transpose(1, 0, 2, 3, 4, 5)

    def block(args):
        i, qi = args
        q_pos = i * Q_BLOCK + jnp.arange(Q_BLOCK)
        dist = q_pos[:, None] - k_pos[None, :]
        mask = dist >= 0
        bias = bias_tab[rel_bucket(dist)].transpose(2, 0, 1).astype(jnp.float32)
        s = jnp.einsum('bqhcd,bkhcd->cbhqk', qi, k).astype(jnp.float32) * scale + bias
        p = jax.nn.softmax(jnp.where(mask, s, NEG_INF), axis=-1)
        w = p[0] - lam * p[1]
        return jnp.einsum('bhqk,bkhe->bqhe', w.astype(v.dtype), v)

    out = lax.map(block, (jnp.arange(nb), qb))
    return out.transpose(1, 0, 2, 3, 4).reshape(B, S, H, v.shape[-1])

def banded_attention(q, k, v, bias_tab, window, sink=None):
    B, S, H, D = q.shape
    G = k.shape[2]
    R = H // G
    nb = S // Q_BLOCK
    n_prev = -(-window // Q_BLOCK)
    kw = (n_prev + 1) * Q_BLOCK

    def band(t):
        tb = t.reshape(B, nb, Q_BLOCK, G, D)
        tb = jnp.pad(tb, ((0, 0), (n_prev, 0), (0, 0), (0, 0), (0, 0)))
        return jnp.concatenate([tb[:, j:j + nb] for j in range(n_prev + 1)], axis=2)

    kb, vb = band(k), band(v)
    qb = q.reshape(B, nb, Q_BLOCK, G, R, D)
    r = jnp.arange(Q_BLOCK)
    c = jnp.arange(kw)
    dist = n_prev * Q_BLOCK + r[:, None] - c[None, :]
    k_pos = (jnp.arange(nb)[:, None] - n_prev) * Q_BLOCK + c[None, :]
    mask = ((dist >= 0) & (dist < window))[None] & (k_pos >= 0)[:, None, :]
    bias = bias_tab[rel_bucket(dist)].reshape(Q_BLOCK, kw, G, R).transpose(2, 3, 0, 1).astype(jnp.float32)
    s = jnp.einsum('bnqgrd,bnkgd->bngrqk', qb, kb).astype(jnp.float32) * D ** -0.5 + bias
    s = jnp.where(mask[:, None, None], s, NEG_INF)
    if sink is None:
        p = jax.nn.softmax(s, axis=-1)
    else:
        sk = sink.astype(jnp.float32).reshape(G, R, 1, 1)
        m = jnp.maximum(jnp.max(s, axis=-1, keepdims=True), sk)
        e = jnp.exp(s - m)
        p = e / (jnp.sum(e, axis=-1, keepdims=True) + jnp.exp(sk - m))
    o = jnp.einsum('bngrqk,bnkgd->bnqgrd', p.astype(v.dtype), vb)
    return o.reshape(B, S, H, D)

def compress_blocks(t, pos, w1, w2):
    B, S, G, D = t.shape
    nc = (S - CMP_BLOCK) // CMP_STRIDE + 1
    idx = jnp.arange(nc)[:, None] * CMP_STRIDE + jnp.arange(CMP_BLOCK)[None, :]
    blocks = t[:, idx] + pos[None, None, :, None, :]
    flat = blocks.transpose(0, 1, 3, 2, 4).reshape(B, nc, G, CMP_BLOCK * D)
    return jax.nn.gelu(flat @ w1) @ w2

def nsa_attention(q, kc, vc, ks, vs, kw, vw, gates, bias_tab):
    B, S, H, D = q.shape
    G = ks.shape[2]
    R = H // G
    nc = kc.shape[1]
    scale = D ** -0.5
    qg = q.reshape(B, S, G, R, D)
    t_pos = jnp.arange(S)

    c_start = jnp.arange(nc) * CMP_STRIDE
    cmask = (c_start + CMP_BLOCK - 1)[None, :] <= t_pos[:, None]
    s = jnp.einsum('bsgrd,bcgd->bgrsc', qg, kc).astype(jnp.float32) * scale
    p_cmp = jnp.where(cmask, jax.nn.softmax(jnp.where(cmask, s, NEG_INF), axis=-1), 0.0)
    o_cmp = jnp.einsum('bgrsc,bcgd->bsgrd', p_cmp.astype(vc.dtype), vc).reshape(B, S, H, D)

    n_blk = S // SEL_BLOCK
    j_start = jnp.arange(n_blk) * SEL_BLOCK
    overlap = ((c_start[:, None] < j_start[None, :] + SEL_BLOCK)
               & (c_start[:, None] + CMP_BLOCK > j_start[None, :])).astype(jnp.float32)
    imp = jnp.einsum('bgrsc,cj->bgsj', p_cmp, overlap)
    cur = t_pos // SEL_BLOCK
    jj = jnp.arange(n_blk)
    valid = j_start[None, :] <= t_pos[:, None]
    forced = (jj[None, :] == 0) | (jj[None, :] == cur[:, None]) | (jj[None, :] == cur[:, None] - 1)
    score = jnp.where(valid, imp + jnp.where(forced, FORCE_BONUS, 0.0), NEG_INF)
    n_sel = min(N_SELECT, n_blk)
    _, sel_idx = lax.top_k(score, n_sel)

    kbk = ks.reshape(B, n_blk, SEL_BLOCK, G, D).transpose(0, 3, 1, 2, 4)
    vbk = vs.reshape(B, n_blk, SEL_BLOCK, G, D).transpose(0, 3, 1, 2, 4)
    nqb = S // SEL_Q_BLOCK
    qs = qg.reshape(B, nqb, SEL_Q_BLOCK, G, R, D).transpose(1, 0, 2, 3, 4, 5)
    idx_b = sel_idx.reshape(B, G, nqb, SEL_Q_BLOCK, n_sel).transpose(2, 0, 1, 3, 4)
    bi = jnp.arange(B)[:, None, None, None]
    gi = jnp.arange(G)[None, :, None, None]
    bias_g = bias_tab.reshape(NUM_BUCKETS, G, R).transpose(1, 0, 2)

    def sel_block(args):
        i, qi, ii = args
        kg = kbk[bi, gi, ii]
        vg = vbk[bi, gi, ii].reshape(B, G, SEL_Q_BLOCK, n_sel * SEL_BLOCK, D)
        q_pos = i * SEL_Q_BLOCK + jnp.arange(SEL_Q_BLOCK)
        k_pos = (ii[..., None] * SEL_BLOCK + jnp.arange(SEL_BLOCK)).reshape(B, G, SEL_Q_BLOCK, n_sel * SEL_BLOCK)
        dist = q_pos[None, None, :, None] - k_pos
        mask = dist >= 0
        bias = bias_g[gi, rel_bucket(dist)].transpose(0, 1, 4, 2, 3).astype(jnp.float32)
        s = jnp.einsum('bqgrd,bgqnkd->bgrqnk', qi, kg).reshape(B, G, R, SEL_Q_BLOCK, n_sel * SEL_BLOCK)
        s = s.astype(jnp.float32) * scale + bias
        p = jax.nn.softmax(jnp.where(mask[:, :, None], s, NEG_INF), axis=-1)
        return jnp.einsum('bgrqk,bgqkd->bqgrd', p.astype(vg.dtype), vg)

    o_sel = lax.map(sel_block, (jnp.arange(nqb), qs, idx_b))
    o_sel = o_sel.transpose(1, 0, 2, 3, 4, 5).reshape(B, S, H, D)

    o_win = banded_attention(q, kw, vw, bias_tab, C_WINDOW)

    g = jax.nn.sigmoid(gates.astype(jnp.float32)).astype(q.dtype)
    out = g[..., 0:1] * o_cmp + g[..., 1:2] * o_sel + g[..., 2:3] * o_win
    return out.reshape(B, S, H * D)

def first_inputs(seed: int = 0) -> dict:
    key = jax.random.key(seed)
    ks = jax.random.split(key, 17)

    def nrm(k, shape, scale):
        return jax.random.normal(k, shape, jnp.float32) * scale

    return {
        'x': nrm(ks[0], (BATCH, SEQ, D_MODEL), 1.0),
        'w_in': nrm(ks[1], (DEPTH, D_MODEL, IN_COLS), D_MODEL ** -0.5),
        'qk_gain': 1.0 + nrm(ks[2], (DEPTH, 8, HEAD_DIM), 0.1),
        'diff_lambda': nrm(ks[3], (DEPTH, 4, HEAD_DIM), 0.1),
        'diff_subln': 1.0 + nrm(ks[4], (DEPTH, A_VDIM), 0.1),
        'sinks': nrm(ks[5], (DEPTH, B_HEADS), 0.5),
        'cmp_pos': nrm(ks[6], (DEPTH, 2, CMP_BLOCK, HEAD_DIM), 0.5),
        'cmp_w1': nrm(ks[7], (DEPTH, 2, CMP_BLOCK * HEAD_DIM, CMP_HIDDEN), (CMP_BLOCK * HEAD_DIM) ** -0.5),
        'cmp_w2': nrm(ks[8], (DEPTH, 2, CMP_HIDDEN, HEAD_DIM), CMP_HIDDEN ** -0.5),
        'w_branch': nrm(ks[9], (DEPTH, N_BRANCH, MIX_WIDTH, D_MODEL), MIX_WIDTH ** -0.5),
        'w_out': nrm(ks[10], (DEPTH, D_MODEL, D_MODEL), D_MODEL ** -0.5),
        'norm_mix': 1.0 + nrm(ks[11], (DEPTH, D_MODEL), 0.1),
        'norm_mlp': 1.0 + nrm(ks[12], (DEPTH, D_MODEL), 0.1),
        'w_up': nrm(ks[13], (DEPTH, D_MODEL, D_FF), D_MODEL ** -0.5),
        'w_down': nrm(ks[14], (DEPTH, D_FF, D_MODEL), D_FF ** -0.5),
        'rel_bias': nrm(ks[15], (NUM_BUCKETS, TOTAL_HEADS), 0.5),
    }

def first_block(x, w_in, qk_gain, diff_lambda, diff_subln, sinks, cmp_pos, cmp_w1, cmp_w2,
              w_branch, w_out, norm_mix, norm_mlp, w_up, w_down, rel_bias):
    B, S, _ = x.shape
    points = []
    acc = 0
    for size in SPLIT_SIZES[:-1]:
        acc += size
        points.append(acc)
    bias_a = rel_bias[:, :A_HEADS]
    bias_b = rel_bias[:, A_HEADS:A_HEADS + B_HEADS]
    bias_c = rel_bias[:, A_HEADS + B_HEADS:]

    for layer in range(DEPTH):
        h = rms_norm(x, norm_mix[layer])
        proj = h @ w_in[layer]
        aq, ak, av, bq, bk, bv, cq, ckv, cg, mg = jnp.split(proj, points, axis=-1)
        gains = qk_gain[layer]

        aq = rms_norm(aq.reshape(B, S, A_HEADS, 2, HEAD_DIM), gains[0])
        ak = rms_norm(ak.reshape(B, S, A_HEADS, 2, HEAD_DIM), gains[1])
        av = av.reshape(B, S, A_HEADS, A_VDIM)
        lmb = diff_lambda[layer].astype(jnp.float32)
        lam_init = 0.8 - 0.6 * math.exp(-0.3 * layer)
        lam = jnp.exp(jnp.sum(lmb[0] * lmb[1])) - jnp.exp(jnp.sum(lmb[2] * lmb[3])) + lam_init
        oa = diff_attention(aq, ak, av, lam, bias_a)
        oa = (rms_norm(oa, diff_subln[layer]) * (1.0 - lam_init)).reshape(B, S, MIX_WIDTH)

        bq = rms_norm(bq.reshape(B, S, B_HEADS, HEAD_DIM), gains[2])
        bk = rms_norm(bk.reshape(B, S, B_KV_HEADS, HEAD_DIM), gains[3])
        bv = bv.reshape(B, S, B_KV_HEADS, HEAD_DIM)
        ob = banded_attention(bq, bk, bv, bias_b, B_WINDOW, sinks[layer]).reshape(B, S, MIX_WIDTH)

        cq = rms_norm(cq.reshape(B, S, C_HEADS, HEAD_DIM), gains[4])
        ckv = ckv.reshape(B, S, 6, C_KV_HEADS, HEAD_DIM)
        kc = rms_norm(compress_blocks(ckv[:, :, 0], cmp_pos[layer, 0], cmp_w1[layer, 0], cmp_w2[layer, 0]), gains[5])
        vc = compress_blocks(ckv[:, :, 1], cmp_pos[layer, 1], cmp_w1[layer, 1], cmp_w2[layer, 1])
        ksel = rms_norm(ckv[:, :, 2], gains[6])
        kwin = rms_norm(ckv[:, :, 4], gains[7])
        oc = nsa_attention(cq, kc, vc, ksel, ckv[:, :, 3], kwin, ckv[:, :, 5],
                           cg.reshape(B, S, C_HEADS, 3), bias_c)

        branches = jnp.stack([oa, ob, oc], axis=0)
        y = jnp.einsum('nbsm,nmd->bsnd', branches, w_branch[layer])
        gate = jax.nn.sigmoid(mg.reshape(B, S, N_BRANCH, D_MODEL).astype(jnp.float32)).astype(y.dtype)
        x = x + jnp.sum(gate * y, axis=2) @ w_out[layer]

        h = rms_norm(x, norm_mlp[layer])
        x = x + jnp.square(jax.nn.relu(h @ w_up[layer])) @ w_down[layer]
    return x


DEPTH_2 = 2

GRID_W = 64
CTX_LEN = 256
AXIS_DIM = HEAD_DIM // 2
ROPE_THETA = 10000.0
N_MOD = 6

GLA_HEADS = 4
GLA_DK = 64
GLA_DV = 128
GLA_GATE_RANK = 16
GLA_GATE_NORM = 16.0
GLA_CHUNK = 64
ATT_HEADS = 8
ATT_KV_HEADS = 2
SWA_HEADS = 16
SWA_KV_HEADS = 2
SWA_WINDOW = 128
MOE_GROUPS = 4
MOE_EXPERTS_PER_GROUP = 4
MOE_TOPK = 2
D_EXPERT = 256

EVEN_WIDTHS = (GLA_HEADS * GLA_DK, GLA_HEADS * GLA_DK, GLA_HEADS * GLA_DV, GLA_HEADS * GLA_DV,
               2 * GLA_GATE_RANK, ATT_HEADS * HEAD_DIM, ATT_KV_HEADS * HEAD_DIM, ATT_KV_HEADS * HEAD_DIM)
EVEN_IN = sum(EVEN_WIDTHS)
EVEN_MIX = GLA_HEADS * GLA_DV + ATT_HEADS * HEAD_DIM
ODD_Q = SWA_HEADS * HEAD_DIM
ODD_KV = SWA_KV_HEADS * HEAD_DIM
ODD_IN = ODD_Q + 2 * ODD_KV
ODD_MIX = ODD_Q
N_EVEN = (DEPTH_2 + 1) // 2
N_ODD = DEPTH_2 // 2


def _split(z, widths):
    return jnp.split(z, np.cumsum(widths)[:-1].tolist(), axis=-1)

def rms_norm_2(x, gain):
    xf = x.astype(jnp.float32)
    y = xf * lax.rsqrt(jnp.mean(xf * xf, axis=-1, keepdims=True) + EPS)
    return (y * gain.astype(jnp.float32)).astype(x.dtype)

def modulate(x, gain, shift, scale):
    return rms_norm_2(x, gain) * (1 + scale) + shift

def axial_rope_tables(n):
    rows = n // GRID_W
    row = jnp.repeat(jnp.arange(rows, dtype=jnp.int32), GRID_W)
    col = jnp.tile(jnp.arange(GRID_W, dtype=jnp.int32), rows)
    inv_freq = ROPE_THETA ** (-jnp.arange(0, AXIS_DIM, 2, dtype=jnp.float32) / AXIS_DIM)
    ang = jnp.stack([row[:, None] * inv_freq, col[:, None] * inv_freq], axis=1)
    return jnp.cos(ang), jnp.sin(ang)

def apply_axial_rope(x, cos, sin):
    B, n, H, _ = x.shape
    xs = x.reshape(B, n, H, 2, 2, AXIS_DIM // 2)
    x1, x2 = xs[..., 0, :], xs[..., 1, :]
    c = cos[None, :, None].astype(x.dtype)
    s = sin[None, :, None].astype(x.dtype)
    out = jnp.stack([x1 * c - x2 * s, x2 * c + x1 * s], axis=-2)
    return out.reshape(B, n, H, HEAD_DIM)

def heads(z, n_heads, gain):
    B, L, _ = z.shape
    return rms_norm_2(z.reshape(B, L, n_heads, HEAD_DIM), gain)

def group_q(q, n_kv):
    B, L, H, Dh = q.shape
    return q.reshape(B, L, n_kv, H // n_kv, Dh)

def softmax_attend(q, k, v, mask=None, sink=None):
    B, Q, KV, G, Dh = q.shape
    s = jnp.einsum('bqhgd,bkhd->bhgqk', q, k).astype(jnp.float32) * (Dh ** -0.5)
    if mask is not None:
        s = jnp.where(mask, s, -jnp.inf)
    if sink is not None:
        sink_col = jnp.broadcast_to(sink.reshape(1, KV, G, 1, 1).astype(jnp.float32), s.shape[:-1] + (1,))
        p = jax.nn.softmax(jnp.concatenate([s, sink_col], axis=-1), axis=-1)[..., :-1]
    else:
        p = jax.nn.softmax(s, axis=-1)
    o = jnp.einsum('bhgqk,bkhd->bqhgd', p.astype(v.dtype), v)
    return o.reshape(B, Q, KV * G * Dh)

def blocked_dense_attention(q, k, v):
    B, S = q.shape[:2]
    nb = S // Q_BLOCK
    qb = jnp.moveaxis(q.reshape(B, nb, Q_BLOCK, *q.shape[2:]), 1, 0)
    ob = lax.map(lambda qi: softmax_attend(qi, k, v), qb)
    return jnp.moveaxis(ob, 0, 1).reshape(B, S, -1)

def banded_window_attention(q, k, v, k_ctx, v_ctx, sink):
    B, S = q.shape[:2]
    nb = S // Q_BLOCK
    span = Q_BLOCK + 2 * SWA_WINDOW
    pad = ((0, 0), (SWA_WINDOW, SWA_WINDOW), (0, 0), (0, 0))
    kp = jnp.pad(k, pad)
    vp = jnp.pad(v, pad)
    qb = jnp.moveaxis(q.reshape(B, nb, Q_BLOCK, *q.shape[2:]), 1, 0)
    ctx_ok = jnp.ones((Q_BLOCK, k_ctx.shape[1]), dtype=bool)

    def block(args):
        qi, bi = args
        start = bi * Q_BLOCK
        kb = lax.dynamic_slice_in_dim(kp, start, span, axis=1)
        vb = lax.dynamic_slice_in_dim(vp, start, span, axis=1)
        qpos = start + jnp.arange(Q_BLOCK, dtype=jnp.int32)
        kpos = start - SWA_WINDOW + jnp.arange(span, dtype=jnp.int32)
        band = (kpos[None, :] >= 0) & (kpos[None, :] < S) & (jnp.abs(kpos[None, :] - qpos[:, None]) <= SWA_WINDOW)
        mask = jnp.concatenate([band, ctx_ok], axis=1)
        return softmax_attend(qi, jnp.concatenate([kb, k_ctx], axis=1), jnp.concatenate([vb, v_ctx], axis=1), mask, sink)

    ob = lax.map(block, (qb, jnp.arange(nb, dtype=jnp.int32)))
    return jnp.moveaxis(ob, 0, 1).reshape(B, S, -1)

def gla_chunk_scan(q, k, v, g, s0):
    B, H, L, DK = q.shape
    DV = v.shape[-1]
    n = L // GLA_CHUNK

    def chunks(t):
        return jnp.moveaxis(t.reshape(B, H, n, GLA_CHUNK, t.shape[-1]), 2, 0)

    lower_tri = jnp.tril(jnp.ones((GLA_CHUNK, GLA_CHUNK), dtype=bool))[:, :, None]

    def step(s, blk):
        qc, kc, vc, gc = blk
        b = jnp.cumsum(gc, axis=2)
        o = jnp.einsum('bhtk,bhkv->bhtv', qc * jnp.exp(b), s)
        diff = b[:, :, :, None, :] - b[:, :, None, :, :]
        decay = jnp.exp(jnp.where(lower_tri, diff, -jnp.inf))
        att = jnp.einsum('bhtk,bhsk,bhtsk->bhts', qc, kc, decay)
        o = o + jnp.einsum('bhts,bhsv->bhtv', att, vc)
        b_end = b[:, :, -1:, :]
        s = jnp.exp(b_end[:, :, 0, :, None]) * s + jnp.einsum('bhsk,bhsv->bhkv', kc * jnp.exp(b_end - b), vc)
        return s, o

    s_fin, o = lax.scan(step, s0, (chunks(q), chunks(k), chunks(v), chunks(g)))
    return jnp.moveaxis(o, 0, 2).reshape(B, H, L, DV), s_fin

def gla_inputs(q, k, v, lr, gate_w, gate_b):
    B, L, _ = q.shape

    def hd(t, d):
        return t.reshape(B, L, GLA_HEADS, d).transpose(0, 2, 1, 3).astype(jnp.float32)

    z = jnp.einsum('blzr,zrk->zblk', lr.reshape(B, L, 2, GLA_GATE_RANK), gate_w) + gate_b[:, None, None, :]
    g = jax.nn.log_sigmoid(z.astype(jnp.float32)) / GLA_GATE_NORM
    g = g.reshape(2, B, L, GLA_HEADS, GLA_DK).transpose(0, 1, 3, 2, 4)
    return hd(q, GLA_DK) * (GLA_DK ** -0.5), hd(k, GLA_DK), hd(v, GLA_DV), g

def gla_bidirectional(lat, ctx):
    ql, kl, vl, gl = lat
    qc, kc, vc, gc = ctx
    B = ql.shape[0]
    s0 = jnp.zeros((B, GLA_HEADS, GLA_DK, GLA_DV), jnp.float32)

    def rev(t):
        return jnp.flip(t, axis=2)

    oc_f, sc_f = gla_chunk_scan(qc, kc, vc, gc[0], s0)
    oc_b, sc_b = gla_chunk_scan(rev(qc), rev(kc), rev(vc), rev(gc[1]), s0)
    ol_f, _ = gla_chunk_scan(ql, kl, vl, gl[0], sc_f)
    ol_b, _ = gla_chunk_scan(rev(ql), rev(kl), rev(vl), rev(gl[1]), sc_b)
    return ol_f + rev(ol_b), oc_f + rev(oc_b)

def gla_output(o, r, gain):
    B, H, L, _ = o.shape
    o = rms_norm_2(o.transpose(0, 2, 1, 3), gain).astype(r.dtype)
    return (o * jax.nn.silu(r.reshape(B, L, H, GLA_DV))).reshape(B, L, H * GLA_DV)

def even_mixer(h_lat, h_ctx, w_in, w_out, gate_w, gate_b, gla_norm, q_norm, k_norm, cos, sin):
    B, S, _ = h_lat.shape
    Lc = h_ctx.shape[1]
    z_l = _split(h_lat @ w_in, EVEN_WIDTHS)
    z_c = _split(h_ctx @ w_in, EVEN_WIDTHS)
    o_gla_l, o_gla_c = gla_bidirectional(gla_inputs(z_l[0], z_l[1], z_l[2], z_l[4], gate_w, gate_b),
                                         gla_inputs(z_c[0], z_c[1], z_c[2], z_c[4], gate_w, gate_b))
    a_l = gla_output(o_gla_l, z_l[3], gla_norm)
    a_c = gla_output(o_gla_c, z_c[3], gla_norm)
    q_l = group_q(apply_axial_rope(heads(z_l[5], ATT_HEADS, q_norm), cos, sin), ATT_KV_HEADS)
    k_l = apply_axial_rope(heads(z_l[6], ATT_KV_HEADS, k_norm), cos, sin)
    v_l = z_l[7].reshape(B, S, ATT_KV_HEADS, HEAD_DIM)
    q_c = group_q(heads(z_c[5], ATT_HEADS, q_norm), ATT_KV_HEADS)
    k_c = heads(z_c[6], ATT_KV_HEADS, k_norm)
    v_c = z_c[7].reshape(B, Lc, ATT_KV_HEADS, HEAD_DIM)
    b_l = blocked_dense_attention(q_l, jnp.concatenate([k_l, k_c], axis=1), jnp.concatenate([v_l, v_c], axis=1))
    b_c = softmax_attend(q_c, k_c, v_c)
    return jnp.concatenate([a_l, b_l], axis=-1) @ w_out, jnp.concatenate([a_c, b_c], axis=-1) @ w_out

def odd_mixer(h_lat, h_ctx, w_in, w_out, sink, q_norm, k_norm, cos, sin, need_ctx):
    B, S, _ = h_lat.shape
    Lc = h_ctx.shape[1]
    q_l, k_l, v_l = _split(h_lat @ w_in, (ODD_Q, ODD_KV, ODD_KV))
    k_c, v_c = _split(h_ctx @ w_in[:, ODD_Q:], (ODD_KV, ODD_KV))
    q = group_q(apply_axial_rope(heads(q_l, SWA_HEADS, q_norm), cos, sin), SWA_KV_HEADS)
    k = apply_axial_rope(heads(k_l, SWA_KV_HEADS, k_norm), cos, sin)
    v = v_l.reshape(B, S, SWA_KV_HEADS, HEAD_DIM)
    kc = heads(k_c, SWA_KV_HEADS, k_norm)
    vc = v_c.reshape(B, Lc, SWA_KV_HEADS, HEAD_DIM)
    m_l = banded_window_attention(q, k, v, kc, vc, sink) @ w_out
    if not need_ctx:
        return m_l, None
    qc = group_q(heads(h_ctx @ w_in[:, :ODD_Q], SWA_HEADS, q_norm), SWA_KV_HEADS)
    return m_l, softmax_attend(qc, kc, vc, None, sink) @ w_out

def hier_moe(h, wg, bg, we, be, w_gate, w_up, w_down):
    N = h.shape[0]
    g_logits = (h @ wg + bg).astype(jnp.float32)
    g_prob = jax.nn.softmax(g_logits, axis=-1)
    g_idx = jnp.argmax(g_logits, axis=-1)
    g_weight = jnp.take_along_axis(g_prob, g_idx[:, None], axis=-1)
    e_logits = (h @ we + be).astype(jnp.float32).reshape(N, MOE_GROUPS, MOE_EXPERTS_PER_GROUP)
    e_sel = jnp.take_along_axis(e_logits, g_idx[:, None, None], axis=1)[:, 0]
    top_p, top_i = lax.top_k(jax.nn.softmax(e_sel, axis=-1), MOE_TOPK)
    top_p = top_p / jnp.sum(top_p, axis=-1, keepdims=True)
    e_weight = jnp.sum(jax.nn.one_hot(top_i, MOE_EXPERTS_PER_GROUP, dtype=jnp.float32) * top_p[..., None], axis=1)
    combine = (jax.nn.one_hot(g_idx, MOE_GROUPS, dtype=jnp.float32)[:, :, None]
               * (g_weight * e_weight)[:, None, :]).astype(h.dtype)
    out = jnp.zeros_like(h)
    for g in range(MOE_GROUPS):
        a = jnp.einsum('nd,edf->nef', h, w_gate[g])
        u = jnp.einsum('nd,edf->nef', h, w_up[g])
        hid = jax.nn.silu(a) * u * combine[:, g, :, None]
        out = out + jnp.einsum('nef,efd->nd', hid, w_down[g])
    return out

def second_inputs(seed: int = 0) -> dict:
    key = jax.random.key(seed)
    ks = iter(jax.random.split(key, 32))
    D = D_MODEL
    G, E = MOE_GROUPS, MOE_EXPERTS_PER_GROUP

    def nrm(shape, scale):
        return scale * jax.random.normal(next(ks), shape, jnp.float32)

    def gain(shape):
        return 1.0 + 0.02 * jax.random.normal(next(ks), shape, jnp.float32)

    return {
        'x': nrm((BATCH, SEQ, D), 1.0),
        'c': nrm((BATCH, D), 1.0),
        'ctx': nrm((BATCH, CTX_LEN, D), 1.0),
        'c_ctx': nrm((D,), 1.0),
        'mod_w': nrm((DEPTH_2, D, N_MOD * D), 0.5 * D ** -0.5),
        'mod_b': nrm((DEPTH_2, N_MOD * D), 0.02),
        'norm_mix': gain((DEPTH_2, D)),
        'norm_ffn': gain((DEPTH_2, D)),
        'ev_w_in': nrm((N_EVEN, D, EVEN_IN), D ** -0.5),
        'ev_w_out': nrm((N_EVEN, EVEN_MIX, D), EVEN_MIX ** -0.5),
        'gla_gate_w': nrm((N_EVEN, 2, GLA_GATE_RANK, GLA_HEADS * GLA_DK), GLA_GATE_RANK ** -0.5),
        'gla_gate_b': nrm((N_EVEN, 2, GLA_HEADS * GLA_DK), 0.1),
        'gla_out_norm': gain((N_EVEN, GLA_DV)),
        'att_q_norm': gain((N_EVEN, HEAD_DIM)),
        'att_k_norm': gain((N_EVEN, HEAD_DIM)),
        'od_w_in': nrm((N_ODD, D, ODD_IN), D ** -0.5),
        'od_w_out': nrm((N_ODD, ODD_MIX, D), ODD_MIX ** -0.5),
        'swa_sink': nrm((N_ODD, SWA_HEADS), 1.0),
        'swa_q_norm': gain((N_ODD, HEAD_DIM)),
        'swa_k_norm': gain((N_ODD, HEAD_DIM)),
        'router_group_w': nrm((DEPTH_2, D, G), D ** -0.5),
        'router_group_b': nrm((DEPTH_2, G), 0.01),
        'router_expert_w': nrm((DEPTH_2, D, G * E), D ** -0.5),
        'router_expert_b': nrm((DEPTH_2, G * E), 0.01),
        'exp_w_gate': nrm((DEPTH_2, G, E, D, D_EXPERT), D ** -0.5),
        'exp_w_up': nrm((DEPTH_2, G, E, D, D_EXPERT), D ** -0.5),
        'exp_w_down': nrm((DEPTH_2, G, E, D_EXPERT, D), D_EXPERT ** -0.5),
    }

def second_block(x, c, ctx, c_ctx, mod_w, mod_b, norm_mix, norm_ffn, ev_w_in, ev_w_out, gla_gate_w, gla_gate_b,
              gla_out_norm, att_q_norm, att_k_norm, od_w_in, od_w_out, swa_sink, swa_q_norm, swa_k_norm,
              router_group_w, router_group_b, router_expert_w, router_expert_b, exp_w_gate, exp_w_up, exp_w_down):
    B, S, D = x.shape
    cos, sin = axial_rope_tables(S)
    sc = jax.nn.silu(c)
    scc = jax.nn.silu(c_ctx)[None]
    for i in range(DEPTH_2):
        last = i == DEPTH_2 - 1
        j = i // 2
        mod_l = jnp.split((sc @ mod_w[i] + mod_b[i])[:, None, :], N_MOD, axis=-1)
        mod_c = jnp.split((scc @ mod_w[i] + mod_b[i])[:, None, :], N_MOD, axis=-1)
        h_l = modulate(x, norm_mix[i], mod_l[0], mod_l[1])
        h_c = modulate(ctx, norm_mix[i], mod_c[0], mod_c[1])
        if i % 2 == 0:
            m_l, m_c = even_mixer(h_l, h_c, ev_w_in[j], ev_w_out[j], gla_gate_w[j], gla_gate_b[j],
                                  gla_out_norm[j], att_q_norm[j], att_k_norm[j], cos, sin)
        else:
            m_l, m_c = odd_mixer(h_l, h_c, od_w_in[j], od_w_out[j], swa_sink[j], swa_q_norm[j],
                                 swa_k_norm[j], cos, sin, not last)
        x = x + mod_l[2] * m_l
        moe_p = (router_group_w[i], router_group_b[i], router_expert_w[i], router_expert_b[i],
                 exp_w_gate[i], exp_w_up[i], exp_w_down[i])
        if last:
            f_l = hier_moe(modulate(x, norm_ffn[i], mod_l[3], mod_l[4]).reshape(B * S, D), *moe_p)
            x = x + mod_l[5] * f_l.reshape(B, S, D)
        else:
            ctx = ctx + mod_c[2] * m_c
            tok = jnp.concatenate([modulate(x, norm_ffn[i], mod_l[3], mod_l[4]).reshape(B * S, D),
                                   modulate(ctx, norm_ffn[i], mod_c[3], mod_c[4]).reshape(-1, D)], axis=0)
            f = hier_moe(tok, *moe_p)
            x = x + mod_l[5] * f[:B * S].reshape(B, S, D)
            ctx = ctx + mod_c[5] * f[B * S:].reshape(ctx.shape)
    return x


def setup_inputs(seed=0):
    out = dict(first_inputs(seed))
    for name, value in second_inputs(seed + 1).items():
        if name != "x":
            out[name + "_2"] = value
    return out


def reference(
    x, w_in, qk_gain, diff_lambda, diff_subln, sinks, cmp_pos, cmp_w1, cmp_w2, w_branch, w_out,
    norm_mix, norm_mlp, w_up, w_down, rel_bias, c_2, ctx_2, c_ctx_2, mod_w_2, mod_b_2,
    norm_mix_2, norm_ffn_2, ev_w_in_2, ev_w_out_2, gla_gate_w_2, gla_gate_b_2, gla_out_norm_2,
    att_q_norm_2, att_k_norm_2, od_w_in_2, od_w_out_2, swa_sink_2, swa_q_norm_2, swa_k_norm_2,
    router_group_w_2, router_group_b_2, router_expert_w_2, router_expert_b_2, exp_w_gate_2,
    exp_w_up_2, exp_w_down_2,
):
    x = first_block(
        x, w_in, qk_gain, diff_lambda, diff_subln, sinks, cmp_pos, cmp_w1, cmp_w2, w_branch,
        w_out, norm_mix, norm_mlp, w_up, w_down, rel_bias,
    )
    return second_block(
        x, c_2, ctx_2, c_ctx_2, mod_w_2, mod_b_2, norm_mix_2, norm_ffn_2, ev_w_in_2, ev_w_out_2,
        gla_gate_w_2, gla_gate_b_2, gla_out_norm_2, att_q_norm_2, att_k_norm_2, od_w_in_2,
        od_w_out_2, swa_sink_2, swa_q_norm_2, swa_k_norm_2, router_group_w_2, router_group_b_2,
        router_expert_w_2, router_expert_b_2, exp_w_gate_2, exp_w_up_2, exp_w_down_2,
    )


_drawn_inputs = setup_inputs


def setup_inputs(seed=0):
    import zlib

    import numpy as np

    out = dict(_drawn_inputs(seed))
    spreads = {}
    factors = {'diff_lambda': 8.0,
     'sinks': 8.0,
     'ctx_2': 3.495,
     'mod_b_2': 3.599,
     'norm_mix_2': 8.0,
     'norm_ffn_2': 6.449,
     'gla_gate_b_2': 8.0,
     'gla_out_norm_2': 8.0,
     'att_q_norm_2': 8.0,
     'att_k_norm_2': 8.0,
     'swa_sink_2': 8.0,
     'swa_q_norm_2': 8.0,
     'swa_k_norm_2': 8.0,
     'router_group_b_2': 8.0,
     'router_expert_b_2': 8.0}
    for name, (base, spread) in spreads.items():
        noise = np.random.default_rng([zlib.crc32(name.encode()), seed]).standard_normal(out[name].shape)
        drawn = base * np.exp(spread * noise) if base else spread * noise
        out[name] = __import__('jax').numpy.asarray(drawn.astype(out[name].dtype))
    for name, factor in factors.items():
        out[name] = (out[name] * factor).astype(out[name].dtype)
    return out
```

```python
import math
from contextlib import ExitStack

import numpy as np
import concourse.bass as bass
from concourse import mybir

P = 128
D = 1024
KD = D // P
S = 512
CTX = 256
T = S + CTX
HD = 64
D_FF = 4096
EPS = 1e-6
NEG = -1e30
LAM_INIT = 0.8 - 0.6 * math.exp(-0.3 * 0)
NC_CMP = (S - 32) // 16 + 1
TABLE = 640
MASKED_FROM = 512
WINDOW_B = 128
N_EXP = 16
RING = 4
LAT = (0, S)
CON = (S, CTX)

F32 = mybir.dt.float32
ALU = mybir.AluOpType
ACT = mybir.ActivationFunctionType
AX = mybir.AxisListType

PARAMS = [("norm_mix", 8), ("norm_mlp", 8), ("qk_gain", 8), ("subln", 1), ("mod_b", 2 * 48), ("norm_mix_2", 16),
          ("norm_ffn_2", 16), ("gla_b", 4), ("gla_norm", 1), ("att_q", 1), ("att_k", 1), ("swa_q", 1), ("swa_k", 1),
          ("c", 16), ("sinks", 8), ("swa_sink", 16), ("router_b", 2 * 20), ("cmp_pos", 32), ("lambda", 4),
          ("valid31", 1)]
CONSTS = [("ident", P), ("ones", P), ("blocks", P), ("rot", P), ("causal_st", P), ("anti_st", P), ("cmask", 4 * NC_CMP)]


def offsets(spec):
    at, out = 0, {}
    for name, width in spec:
        out[name] = (at, at + width)
        at += width
    return out, at


PARAM_AT, N_PARAM = offsets(PARAMS)
CONST_AT, N_CONST = offsets(CONSTS)


class Flag:

    def __init__(self, nc, name):
        self.sem = nc.alloc_semaphore(name)
        self.base = 0

    def value(self, n):
        return self.base + n

    def advance(self, n):
        self.base += n


class Chain:

    def __init__(self, flag):
        self.flag = flag

    def __call__(self, eng, ins):
        ins.then_inc(self.flag.sem, 1)
        self.flag.advance(1)
        eng.wait_ge(self.flag.sem, self.flag.base)


class Core:

    def __init__(self, nc, ctx, dram):
        self.nc = nc
        self.ctx = ctx
        self.dram = dram
        sb = self.sb
        self.X = sb("X", [P, KD, T])
        self.H = sb("H", [P, KD, T])
        self.ring = sb("ring", [P, RING, 4096])
        self.par = sb("par", [P, N_PARAM])
        self.con = sb("con", [P, N_CONST])
        self.eps = sb("eps", [P, 1])
        self.mods = sb("mods", [P, 2, 48, 2])
        self.mod_gain = sb("mod_gain", [P, 2, 2, KD, 2])
        self.silu_c = sb("silu_c", [P, 16])
        self.derived = sb("derived", [P, N_DERIVED])
        self.router = sb("router", [P, 2, KD, 20])
        self.psum = ctx.enter_context(nc.psum_tensor("banks", [P, 8, 512], F32))
        self.flags = {}
        for name in ("products_done", "evacuated_v", "evacuated_s", "squared", "summed", "rooted", "normed",
                     "scored", "biased", "exped", "weighted", "turned", "copied", "attended", "emptied",
                     "v_step", "s_step", "p_step", "misc_loaded", "bias_loaded0", "bias_loaded1", "hid_ready", "gated", "silued",
                     "down_done", "added", "comb_loaded", "comb_loaded1", "out_stored", "stored", "made", "tables_stored"):
            self.flags[name] = Flag(nc, name)
        self.w_loaded = [Flag(nc, f"w_loaded{i}") for i in range(RING)]
        self.v_chain, self.s_chain, self.p_chain = (Chain(self.flags[n]) for n in ("v_step", "s_step", "p_step"))
        self.plan_list = plan_weights()
        self.plan = {name: (c, kt, n) for c, (name, kt, n) in enumerate(self.plan_list)}
        self.issued = 0
        self.used_up = {}
        self.consumed = 0

    def sb(self, name, shape):
        return self.ctx.enter_context(self.nc.sbuf_tensor(name, shape, F32))

    def bank(self, n, rows=P, cols=512, at=0):
        return self.psum[0:rows, n, at:at + cols]

    def param(self, name, a=0, n=None, rows=P):
        lo, hi = PARAM_AT[name]
        return self.par[0:rows, lo + a:hi if n is None else lo + a + n]

    def const(self, name, rows=P, at=0):
        lo, hi = CONST_AT[name]
        return self.con[at:at + rows, lo:hi]

    def chunk(self, name):
        c, kt, n = self.plan[name]
        return c, self.ring[:, c % RING, 0:kt * n].rearrange("p (k n) -> p k n", k=kt)

    def feed(self, sync, consumed):
        while self.issued < min(consumed + RING, len(self.plan_list)):
            c = self.issued
            _, kt, n = self.plan_list[c]
            if c >= RING:
                flag, value = self.used_up[c - RING]
                sync.wait_ge(flag.sem, value)
            sync.dma_start(self.ring[:, c % RING, 0:kt * n], self.dram["weights"][c, :, 0:kt * n])\
                .then_inc(self.w_loaded[c % RING].sem, 16)
            self.issued += 1

    def use_up(self, jobs):
        done = self.flags["products_done"]
        for n, job in enumerate(jobs):
            if job[1]:
                self.used_up[job[0]] = (done, done.value(n + 1))
        return self.consumed + sum(1 for j in jobs if j[1])

    def await_chunk(self, pe, c):
        pe.wait_ge(self.w_loaded[c % RING].sem, 16 * (c // RING + 1))


def products(pe, out, pairs):
    for n, (lhsT, rhs) in enumerate(pairs):
        last = pe.matmul(out, lhsT, rhs, start=n == 0, stop=n == len(pairs) - 1)
    return last


def dense(core, name, jobs, finish, both=True):
    nc, f = core.nc, core.flags
    lanes = 2 if both else 1
    used = core.use_up(jobs)

    with nc.Block(name) as block:
        @block.sync
        def _(sp):
            core.feed(sp, used)

        @block.tensor
        def _(pe):
            seen = None
            for n, (chunk, release, rows, cols, pairs) in enumerate(jobs):
                if chunk is not None and chunk != seen:
                    core.await_chunk(pe, chunk)
                    seen = chunk
                if n >= 8:
                    flag = f["evacuated_s"] if both and n % 2 else f["evacuated_v"]
                    pe.wait_ge(flag.sem, flag.value((n - 8) // lanes + 1))
                last = products(pe, core.bank(n % 8, rows, cols), pairs)
                last.then_inc(f["products_done"].sem, 1)

        @block.vector
        def _(dve):
            for n in range(0, len(jobs), lanes):
                dve.wait_ge(f["products_done"].sem, f["products_done"].value(n + 1))
                finish(dve, n, core.bank(n % 8, jobs[n][2], jobs[n][3])).then_inc(f["evacuated_v"].sem, 1)

        if both:
            @block.scalar
            def _(act):
                for n in range(1, len(jobs), 2):
                    act.wait_ge(f["products_done"].sem, f["products_done"].value(n + 1))
                    finish(act, n, core.bank(n % 8, jobs[n][2], jobs[n][3])).then_inc(f["evacuated_s"].sem, 1)

    f["products_done"].advance(len(jobs))
    f["evacuated_v"].advance((len(jobs) + lanes - 1) // lanes)
    f["evacuated_s"].advance(len(jobs) // 2 if both else 0)
    core.consumed = used


def copy_out(core, dst):
    def finish(eng, n, ps):
        if eng is core.nc.scalar:
            return eng.activation(dst(n), ps, ACT.Copy)
        return eng.tensor_copy(dst(n), ps)
    return finish


def head_normed(core, name, jobs, scratch, dest, gain, group, const, sources=None):
    nc, f = core.nc, core.flags
    squares, roots = scratch

    def tile(n):
        return sources[n] if sources else core.bank(n % 3, P, jobs[n][3])

    used = core.use_up(jobs)
    N = len(jobs)

    with nc.Block(name) as block:
        @block.sync
        def _(sp):
            core.feed(sp, used)

        @block.tensor
        def _(pe):
            seen = None
            for n in range(N + 1):
                if n < N and not sources:
                    chunk, release, rows, cols, pairs = jobs[n]
                    if chunk is not None and chunk != seen:
                        core.await_chunk(pe, chunk)
                        seen = chunk
                    if n >= 3:
                        pe.wait_ge(f["normed"].sem, f["normed"].value(n - 2))
                    last = products(pe, core.bank(n % 3, rows, cols), pairs)
                    last.then_inc(f["products_done"].sem, 1)
                if n >= 1:
                    m = n - 1
                    cols = jobs[m][3]
                    pe.wait_ge(f["squared"].sem, f["squared"].value(m + 1))
                    if m >= 2:
                        pe.wait_ge(f["rooted"].sem, f["rooted"].value(m - 1))
                    pe.matmul(core.bank(3 + m % 2, P, cols), const, squares[:, m % 2, 0:cols], start=True,
                              stop=True).then_inc(f["summed"].sem, 1)

        @block.scalar
        def _(act):
            for n in range(N + 1):
                if n < N:
                    cols = jobs[n][3]
                    if not sources:
                        act.wait_ge(f["products_done"].sem, f["products_done"].value(n + 1))
                    if n >= 2:
                        act.wait_ge(f["summed"].sem, f["summed"].value(n - 1))
                    act.activation(squares[:, n % 2, 0:cols], tile(n), ACT.Square)\
                        .then_inc(f["squared"].sem, 1)
                if n >= 1:
                    m = n - 1
                    cols = jobs[m][3]
                    act.wait_ge(f["summed"].sem, f["summed"].value(m + 1))
                    if m >= 2:
                        act.wait_ge(f["normed"].sem, f["normed"].value(m - 1))
                    r = roots[:, m % 2, 0:cols]
                    core.s_chain(act, act.activation(r, core.bank(3 + m % 2, P, cols), ACT.Ln,
                                                     bias=core.eps[:, 0:1], scale=1.0 / group))
                    act.activation(r, r, ACT.Exp, scale=-0.5).then_inc(f["rooted"].sem, 1)

        @block.vector
        def _(dve):
            for n in range(N):
                cols = jobs[n][3]
                dve.wait_ge(f["rooted"].sem, f["rooted"].value(n + 1))
                dve.scalar_tensor_tensor(out=dest(n), in0=tile(n), scalar=gain(n),
                                         in1=roots[:, n % 2, 0:cols], op0=ALU.mult, op1=ALU.mult)\
                    .then_inc(f["normed"].sem, 1)

    if not sources:
        f["products_done"].advance(N)
    for k in ("squared", "summed", "rooted", "normed"):
        f[k].advance(N)
    core.consumed = used


def normalise(core, name, parts, scale, shift=None):
    nc, f = core.nc, core.flags
    with ExitStack() as stack:
        squares = stack.enter_context(nc.sbuf_tensor(name + "_squares", [P, 2, 512], F32))
        roots = stack.enter_context(nc.sbuf_tensor(name + "_roots", [P, T], F32))
        N = KD * len(parts)
        with nc.Block(name) as block:
            @block.sync
            def _(sp):
                core.feed(sp, core.consumed)

            @block.scalar
            def _(act):
                for n in range(N):
                    (t0, tn), k = parts[n // KD], n % KD
                    if n >= 2:
                        act.wait_ge(f["summed"].sem, f["summed"].value(n - 1))
                    act.activation(squares[:, n % 2, 0:tn], core.X[:, k, t0:t0 + tn], ACT.Square)\
                        .then_inc(f["squared"].sem, 1)
                    if k == KD - 1:
                        act.wait_ge(f["summed"].sem, f["summed"].value(n + 1))
                        r = roots[:, t0:t0 + tn]
                        core.s_chain(act, act.activation(r, core.bank(n // KD, P, tn), ACT.Ln,
                                                         bias=core.eps[:, 0:1], scale=1.0 / D))
                        act.activation(r, r, ACT.Exp, scale=-0.5).then_inc(f["rooted"].sem, 1)

            @block.tensor
            def _(pe):
                for n in range(N):
                    (t0, tn), k = parts[n // KD], n % KD
                    pe.wait_ge(f["squared"].sem, f["squared"].value(n + 1))
                    pe.matmul(core.bank(n // KD, P, tn), core.const("ones"), squares[:, n % 2, 0:tn],
                              start=k == 0, stop=k == KD - 1).then_inc(f["summed"].sem, 1)

            @block.vector
            def _(dve):
                for p, (t0, tn) in enumerate(parts):
                    dve.wait_ge(f["rooted"].sem, f["rooted"].value(p + 1))
                    for k in range(KD):
                        last = dve.scalar_tensor_tensor(out=core.H[:, k, t0:t0 + tn], in0=core.X[:, k, t0:t0 + tn],
                                                        scalar=scale(k, p), in1=roots[:, t0:t0 + tn],
                                                        op0=ALU.mult, op1=ALU.mult)
                    if shift is not None:
                        core.v_chain(dve, last)
                        for k in range(KD):
                            dve.tensor_scalar(core.H[:, k, t0:t0 + tn], core.H[:, k, t0:t0 + tn], shift(k, p),
                                              None, ALU.add)
        for k, v in (("squared", N), ("summed", N), ("rooted", len(parts))):
            f[k].advance(v)


def attention(core, name, units, bias_loads=()):
    nc, f = core.nc, core.flags
    U = len(units)
    widest = max(u["width"] for u in units) + 1
    SL = 3
    groups = []
    g = 0
    for u in units:
        mine = []
        for t in range(0, len(u["v"]), 4):
            mine.append((g, t, min(4, len(u["v"]) - t)))
            g += 1
        groups.append(mine)
    evacs = [n for n, u in enumerate(units) if u["evac"]]
    score = [core.psum[:, 2 * i:2 * i + 2, :].rearrange("p a b -> p (a b)") for i in range(2)]
    ident = core.const("ident")

    with ExitStack() as stack:
        probs = stack.enter_context(nc.sbuf_tensor(name + "_probs", [P, SL, widest], F32))
        turned = stack.enter_context(nc.sbuf_tensor(name + "_turned", [P, 3, 512], F32))
        stats = stack.enter_context(nc.sbuf_tensor(name + "_stats", [P, 4, 3], F32))

        def tile_keys(u, t):
            return min(P, u["width"] - t * P)

        with nc.Block(name) as block:
            @block.sync
            def _(sp):
                if bias_loads:
                    sp.wait_ge(f["tables_stored"].sem, 32)
                for n, (dst, src, after) in enumerate(bias_loads):
                    if after is not None:
                        sp.wait_ge(f["biased"].sem, f["biased"].value(after + 1))
                    sp.dma_start(dst, src).then_inc(f[f"bias_loaded{n % 2}"].sem, 16)
                core.feed(sp, core.consumed)

            @block.tensor
            def _(pe):
                def scores(n):
                    u = units[n]
                    if n >= 2:
                        pe.wait_ge(f["exped"].sem, f["exped"].value(n - 1))
                    at = 0
                    for k in u["k"]:
                        last = pe.matmul(score[n % 2][:, at:at + k.shape[1]], u["q"], k, start=True, stop=True)
                        at += k.shape[1]
                    last.then_inc(f["scored"].sem, 1)

                def transposes(n):
                    u = units[n]
                    pe.wait_ge(f["weighted"].sem, f["weighted"].value(n + 1))
                    for g, t0, nt in groups[n]:
                        if g >= 2:
                            pe.wait_ge(f["copied"].sem, f["copied"].value(g - 1))
                        for t in range(t0, t0 + nt):
                            w = tile_keys(u, t)
                            last = pe.transpose(core.bank(4 + g % 2, w, P, (t - t0) * P),
                                                probs[:, n % SL, t * P:t * P + w], ident)
                        last.then_inc(f["turned"].sem, 1)

                def values(n):
                    u = units[n]
                    if u["first"] and u["clears"] is not None:
                        pe.wait_ge(f["emptied"].sem, f["emptied"].value(u["clears"]))
                    for g, t0, nt in groups[n]:
                        pe.wait_ge(f["copied"].sem, f["copied"].value(g + 1))
                        for t in range(t0, t0 + nt):
                            w = tile_keys(u, t)
                            last = pe.matmul(core.bank(6 + u["bank"], P, P, u["col"]), u["v"][t],
                                             turned[0:w, g % 3, (t - t0) * P:(t - t0) * P + P],
                                             start=u["first"] and t == 0,
                                             stop=u["last"] and t == len(u["v"]) - 1)
                    last.then_inc(f["attended"].sem, 1)

                for n in range(U + 3):
                    if n < U:
                        scores(n)
                    if 2 <= n < U + 2:
                        transposes(n - 2)
                    if n >= 3:
                        values(n - 3)

            @block.vector
            def _(dve):
                def soften(n):
                    u = units[n]
                    w = u["width"]
                    dve.wait_ge(f["scored"].sem, f["scored"].value(n + 1))
                    if n >= SL:
                        dve.wait_ge(f["turned"].sem, f["turned"].value(groups[n - SL][-1][0] + 1))
                    if u["bias_load"] is not None:
                        b = f[f"bias_loaded{u['bias_load'] % 2}"]
                        dve.wait_ge(b.sem, b.value(16 * (u["bias_load"] // 2 + 1)))
                    row = score[n % 2][:, 0:w]
                    if u["sink"] is not None:
                        dve.tensor_copy(probs[:, n % SL, w:w + 1], u["sink"])
                    if u["bias"] is not None:
                        core.v_chain(dve, dve.tensor_tensor(probs[:, n % SL, 0:w], row, u["bias"], ALU.add))
                        row = probs[:, n % SL, 0:w + (u["sink"] is not None)]
                    dve.tensor_reduce(stats[:, n % 4, 0:1], row, AX.X, ALU.max, negate=True)\
                        .then_inc(f["biased"].sem, 1)

                def weigh(n):
                    u = units[n]
                    w = u["width"]
                    dve.wait_ge(f["exped"].sem, f["exped"].value(n + 1))
                    core.v_chain(dve, dve.reciprocal(stats[:, n % 4, 2:3], stats[:, n % 4, 1:2]))
                    dve.tensor_scalar(probs[:, n % SL, 0:w], probs[:, n % SL, 0:w], stats[:, n % 4, 2:3], u["coef"],
                                      ALU.mult, ALU.mult).then_inc(f["weighted"].sem, 1)

                def empty(n):
                    dst, rows = units[n]["evac"]
                    dve.wait_ge(f["attended"].sem, f["attended"].value(n + 1))
                    a, b = rows
                    dve.tensor_copy(dst, core.psum[a:b, 6 + units[n]["bank"], 0:dst.shape[-1]])\
                        .then_inc(f["emptied"].sem, 1)

                for n in range(U + 4):
                    if n >= 4 and units[n - 4]["evac"]:
                        empty(n - 4)
                    if n < U:
                        soften(n)
                    if 1 <= n <= U:
                        weigh(n - 1)

            @block.scalar
            def _(act):
                for n in range(U + 2):
                    if n < U:
                        u = units[n]
                        act.wait_ge(f["biased"].sem, f["biased"].value(n + 1))
                        w = u["width"] + (u["sink"] is not None)
                        row = probs[:, n % SL, 0:w] if u["bias"] is not None else score[n % 2][:, 0:w]
                        act.activation(probs[:, n % SL, 0:w], row, ACT.Exp, bias=stats[:, n % 4, 0:1],
                                       accum_out=stats[:, n % 4, 1:2]).then_inc(f["exped"].sem, 1)
                    if n >= 2:
                        for g, t0, nt in groups[n - 2]:
                            act.wait_ge(f["turned"].sem, f["turned"].value(g + 1))
                            if g >= 3:
                                owner = next(i for i, x in enumerate(groups) if any(y[0] == g - 3 for y in x))
                                act.wait_ge(f["attended"].sem, f["attended"].value(owner + 1))
                            w = tile_keys(units[n - 2], t0) if nt == 1 else P
                            act.activation(turned[0:w, g % 3, 0:nt * P], core.bank(4 + g % 2, w, nt * P),
                                           ACT.Copy).then_inc(f["copied"].sem, 1)

    for k in ("scored", "biased", "exped", "weighted", "attended"):
        f[k].advance(U)
    f["turned"].advance(g_total(groups))
    f["copied"].advance(g_total(groups))
    f["emptied"].advance(len(evacs))
    for i in range(2):
        f[f"bias_loaded{i}"].advance(16 * len(bias_loads[i::2]))


def g_total(groups):
    return sum(len(x) for x in groups)


def unit(q, k, v, bank, col, first=True, last=True, bias=None, bias_load=None, sink=None, coef=1.0, evac=None):
    return dict(q=q, k=k, width=sum(x.shape[1] for x in k), bias=bias, bias_load=bias_load, sink=sink, coef=coef,
                v=v, bank=bank, col=col, first=first, last=last, evac=evac, clears=None)


def plan_outputs(units):
    done = 0
    fresh = True
    for u in units:
        if fresh and done >= 2:
            u["clears"] = done - 1
        fresh = False
        if u["evac"]:
            done += 1
            fresh = True
    return units


def plan_weights():
    plan = [(f"proj{i}", KD, 512) for i in range(7)] + [("proj7", KD, 24), ("cmp0", 16, 256), ("cmp1", 16, 256)]
    for n in range(3):
        plan += [(f"mg{n}_0", KD, 512), (f"mg{n}_1", KD, 512), (f"branch{n}", 4, 1024)]
    plan += [(f"out{i}", KD, 512) for i in range(2)]
    plan += [(f"up{i}", KD, 512) for i in range(8)] + [(f"down{i}", 32, P) for i in range(8)]
    plan += [(f"mod{l}_{i}", KD, 512) for l in range(2) for i in range(12)]
    plan += [("ev0", KD, 512), ("ev1", KD, 288), ("ev2", KD, 512), ("ev3", KD, 512), ("ev4", KD, 512)]
    plan += [(f"ev_out{i}", KD, 512) for i in range(2)]
    for l in range(2):
        for i in range(0, N_EXP, 2):
            plan += [(f"gu{l}_{i}", KD, 512), (f"gu{l}_{i + 1}", KD, 512)]
            plan += [(f"dn{l}_{i}", 2, 1024), (f"dn{l}_{i + 1}", 2, 1024)]
        if l == 0:
            plan += [("od0", KD, 512), ("od1", KD, 512), ("od2", KD, 256)]
            plan += [(f"od_out{i}", KD, 512) for i in range(2)]
    return plan


def load_inputs(core):
    nc, f, dram = core.nc, core.flags, core.dram
    x = dram["xT"].rearrange("(k p) t -> p k t", p=P)
    c = dram["ctxT"].rearrange("(k p) t -> p k t", p=P)
    with nc.Block("load") as block:
        @block.sync
        def _(sp):
            sp.dma_start(core.X[:, :, 0:S], x).then_inc(f["misc_loaded"].sem, 16)
            sp.dma_start(core.con[:, :], dram["con"]).then_inc(f["misc_loaded"].sem, 16)
            core.feed(sp, 0)

        @block.scalar
        def _(act):
            act.dma_start(core.par[:, :], dram["par"]).then_inc(f["misc_loaded"].sem, 16)
            act.dma_start(core.X[:, :, S:T], c).then_inc(f["misc_loaded"].sem, 16)
            act.dma_start(core.router[:, :, :, :], dram["router"]).then_inc(f["misc_loaded"].sem, 16)
            act.wait_ge(f["misc_loaded"].sem, 80)

        @block.vector
        def _(dve):
            dve.memset(core.eps[:, :], EPS)
    f["misc_loaded"].advance(80)


NEG_LAM, SUBLN, AQ_G, BQ_G, CQ_G, ATT_G, SWA_G, N_DERIVED = range(8)


def derive(core):
    nc, f, dram = core.nc, core.flags, core.dram
    scale = HD ** -0.5
    par = core.param
    der = core.derived
    with ExitStack() as stack:
        def sb(name, shape):
            return stack.enter_context(nc.sbuf_tensor(name, shape, F32))
        prod = sb("lam_products", [P, 2])
        exps = sb("lam_exps", [P, 2])
        sig = sb("c_sigmoid", [P, 16])
        onehot = sb("onehot", [32, TABLE])
        rel = sb("rel", [32, 20])
        table_ac, table_b = core.table_ac, core.table_b
        with nc.Block("derive") as block:
            @block.sync
            def _(sp):
                sp.dma_start(onehot[:, :], dram["onehot"]).then_inc(f["misc_loaded"].sem, 16)
                sp.dma_start(rel[:, :], dram["rel"]).then_inc(f["misc_loaded"].sem, 16)
                sp.wait_ge(f["made"].sem, f["made"].value(1))
                for lo, table in ((0, table_ac), (12, table_b)):
                    n = table.shape[0]
                    sp.dma_start(dram["bias"][lo:lo + n], table[:, :].rearrange("h (o t) -> h o t", o=1)
                                 .broadcast_to([n, P, TABLE])).then_inc(f["tables_stored"].sem, 16)

            @block.vector
            def _(dve):
                lam = par("lambda")
                dve.tensor_tensor(prod[:, 0:1], lam[:, 0:1], lam[:, 1:2], ALU.mult)
                dve.tensor_tensor(prod[:, 1:2], lam[:, 2:3], lam[:, 3:4], ALU.mult).then_inc(f["squared"].sem, 1)
                dve.tensor_scalar(der[:, SUBLN:SUBLN + 1], par("subln"), 1.0 - LAM_INIT, None, ALU.mult)
                for at, src in ((AQ_G, par("qk_gain", 0, 1)), (BQ_G, par("qk_gain", 2, 1)),
                                (CQ_G, par("qk_gain", 4, 1)), (ATT_G, par("att_q")), (SWA_G, par("swa_q"))):
                    dve.tensor_scalar(der[:, at:at + 1], src, scale, None, ALU.mult)
                dve.wait_ge(f["exped"].sem, f["exped"].value(1))
                dve.scalar_tensor_tensor(out=der[:, NEG_LAM:NEG_LAM + 1], in0=exps[:, 1:2], scalar=LAM_INIT,
                                         in1=exps[:, 0:1], op0=ALU.subtract, op1=ALU.subtract)
                dve.wait_ge(f["silued"].sem, f["silued"].value(1))
                dve.tensor_tensor(core.silu_c[:, :], par("c"), sig[:, :], ALU.mult)
                dve.wait_ge(f["products_done"].sem, f["products_done"].value(1))
                dve.tensor_copy(table_ac[:, :], core.psum[0:12, 0:2, :].rearrange("p a b -> p (a b)")[:, 0:TABLE])
                core.v_chain(dve, dve.tensor_copy(
                    table_b[:, :], core.psum[0:8, 2:4, :].rearrange("p a b -> p (a b)")[:, 0:TABLE]))
                dve.memset(table_ac[:, MASKED_FROM:TABLE], NEG)
                dve.memset(table_b[:, 0:S - WINDOW_B], NEG)
                dve.memset(table_b[:, MASKED_FROM:TABLE], NEG).then_inc(f["made"].sem, 1)

            @block.tensor
            def _(pe):
                pe.wait_ge(f["squared"].sem, f["squared"].value(1))
                pe.matmul(core.bank(4, P, 2), core.const("ones"), prod[:, :], start=True, stop=True)\
                    .then_inc(f["summed"].sem, 1)
                pe.wait_ge(f["misc_loaded"].sem, f["misc_loaded"].value(32))
                for b, (lo, hi) in enumerate(((0, 12), (12, 20))):
                    pe.matmul(core.bank(2 * b, hi - lo), rel[:, lo:hi], onehot[:, 0:512], start=True, stop=True)
                    last = pe.matmul(core.bank(2 * b + 1, hi - lo, TABLE - 512), rel[:, lo:hi],
                                     onehot[:, 512:TABLE], start=True, stop=True)
                last.then_inc(f["products_done"].sem, 1)

            @block.scalar
            def _(act):
                act.wait_ge(f["summed"].sem, f["summed"].value(1))
                act.activation(exps[:, :], core.bank(4, P, 2), ACT.Exp).then_inc(f["exped"].sem, 1)
                act.activation(sig[:, :], par("c"), ACT.Sigmoid).then_inc(f["silued"].sem, 1)
    f["misc_loaded"].advance(32)
    for k in ("squared", "exped", "silued", "products_done", "summed", "made"):
        f[k].advance(1)


def modulation(core):
    nc, f = core.nc, core.flags
    sc = core.silu_c[:, :].rearrange("p (k v) -> p k v", v=2)
    jobs = []
    for l in range(2):
        for i in range(12):
            c, w = core.chunk(f"mod{l}_{i}")
            for j in range(4):
                jobs.append((c, j == 3, P, 2, [(w[:, k, j * P:(j + 1) * P], sc[:, k, :]) for k in range(KD)]))

    def finish(eng, n, ps):
        b = core.param("mod_b", n, 1)
        dst = core.mods[:, n // 48, n % 48, :]
        if eng is nc.scalar:
            return eng.activation(dst, ps, ACT.Identity, bias=b)
        return eng.tensor_scalar(dst, ps, b, None, ALU.add)
    dense(core, "modulation", jobs, finish)

    with nc.Block("mod_gains") as block:
        @block.vector
        def _(dve):
            for l in range(2):
                for which, name in ((1, "norm_mix_2"), (4, "norm_ffn_2")):
                    for v in range(2):
                        dve.scalar_tensor_tensor(
                            out=core.mod_gain[:, l, which // 4, :, v], in0=core.mods[:, l, 8 * which:8 * which + 8, v],
                            scalar=1.0, in1=core.param(name, 8 * l, 8), op0=ALU.add, op1=ALU.mult)


def modulated_norm(core, name, l, ffn, parts):
    shift = 24 if ffn else 0
    normalise(core, name, parts, lambda k, p: core.mod_gain[:, l, ffn, k, p:p + 1],
              lambda k, p: core.mods[:, l, shift + k, p:p + 1])


def residual(core, name, chunks, src, parts, gate=None):
    jobs, where = [], []
    for i, cname in enumerate(chunks):
        c, w = core.chunk(cname)
        tiles = w.shape[2] // P
        for j in range(tiles):
            for p, (t0, tn) in enumerate(parts):
                jobs.append((c, j == tiles - 1 and p == len(parts) - 1, P, tn,
                             [(w[:, k, j * P:(j + 1) * P], src(k, t0, tn)) for k in range(w.shape[1])]))
                where.append((i * tiles + j, p, t0, tn))

    def finish(dve, n, ps):
        m, p, t0, tn = where[n]
        x = core.X[:, m, t0:t0 + tn]
        if gate is None:
            return dve.tensor_tensor(x, x, ps, ALU.add)
        return dve.scalar_tensor_tensor(out=x, in0=ps, scalar=gate(m, p), in1=x, op0=ALU.mult, op1=ALU.add)
    dense(core, name, jobs, finish, both=False)


def feature_jobs(core, cname, parts, tiles=None, release=True):
    c, w = core.chunk(cname)
    tiles = range(w.shape[2] // P) if tiles is None else tiles
    jobs = []
    for j in tiles:
        for p, (t0, tn) in enumerate(parts):
            jobs.append((c, release and j == tiles[-1] and p == len(parts) - 1, P, tn,
                         [(w[:, k, j * P:(j + 1) * P], core.H[:, k, t0:t0 + tn]) for k in range(KD)]))
    return jobs


def token_jobs(core, cname, tokens, lo, hi, release=True):
    c, w = core.chunk(cname)
    return [(c, release and t == tokens - 1, P, hi - lo,
             [(core.H[:, k, t * P:(t + 1) * P], w[:, k, lo:hi]) for k in range(KD)]) for t in range(tokens)]


def compress(core, CK, KC, VC, CG, CG0):
    nc, f, dram = core.nc, core.flags, core.dram
    N2 = 2 * NC_CMP
    with ExitStack() as stack:
        def sb(name, shape):
            return stack.enter_context(nc.sbuf_tensor(name, shape, F32))
        shifted = sb("cmp_shifted", [P, 2, 2, S])
        blocks = sb("cmp_blocks", [P, 2, 16, N2])
        x = sb("cmp_x", [P, 4 * N2])
        t = sb("cmp_t", [P, 4 * N2])
        w2 = sb("cmp_w2", [P, 2, 2, P])
        root = sb("cmp_root", [P, N2])
        sq = sb("cmp_sq", [P, N2])
        for kv in range(2):
            core.used_up[core.plan[f"cmp{kv}"][0]] = (f["products_done"], f["products_done"].value(kv + 1))
        with nc.Block("compress") as block:
            @block.sync
            def _(sp):
                w = dram["cmp_w2"].rearrange("v (k p) d -> p v k d", p=P)
                for half in range(2):
                    for v in range(2):
                        sp.dma_start(w2[:, v, :, 64 * half:64 * half + 64], w[:, v]).then_inc(f["misc_loaded"].sem, 16)
                for g in range(2):
                    sp.dma_start(shifted[0:64, :, g, :], CK[64 * g:64 * g + 64, :, :])\
                        .then_inc(f["misc_loaded"].sem, 16)
                    sp.dma_start(shifted[64:128, :, g, 0:S - 1], CK[64 * g:64 * g + 64, :, 1:S])\
                        .then_inc(f["misc_loaded"].sem, 16)
                core.feed(sp, core.consumed + 2)

            @block.vector
            def _(dve):
                dve.wait_ge(f["misc_loaded"].sem, f["misc_loaded"].value(128))
                for kv in range(2):
                    for m in range(16):
                        last = dve.tensor_scalar(
                            blocks[:, kv, m, :].rearrange("p (g c) -> p g c", g=2),
                            shifted[:, kv, :, 2 * m:2 * m + 16 * (NC_CMP - 1) + 1:16],
                            core.param("cmp_pos", 16 * kv + m, 1), None, ALU.add)
                    last.then_inc(f["made"].sem, 1)
                dve.wait_ge(f["products_done"].sem, f["products_done"].value(2))
                core.v_chain(dve, dve.tensor_copy(x[:, :], core.bank(0, P, 4 * N2)))
                core.v_chain(dve, dve.tensor_tensor(t[:, :], x[:, :], x[:, :], ALU.mult))
                core.v_chain(dve, dve.tensor_scalar(t[:, :], t[:, :], 0.044715, 1.0, ALU.mult, ALU.add))
                dve.tensor_tensor(t[:, :], t[:, :], x[:, :], ALU.mult).then_inc(f["squared"].sem, 1)
                dve.wait_ge(f["exped"].sem, f["exped"].value(1))
                core.v_chain(dve, dve.tensor_scalar(t[:, :], t[:, :], 1.0, 0.5, ALU.add, ALU.mult))
                dve.tensor_tensor(x[:, :], t[:, :], x[:, :], ALU.mult).then_inc(f["made"].sem, 1)
                dve.wait_ge(f["summed"].sem, f["summed"].value(1))
                dve.tensor_copy(VC[:, :], core.bank(2, NC_CMP, P))
                dve.wait_ge(f["rooted"].sem, f["rooted"].value(1))
                dve.scalar_tensor_tensor(out=KC[:, :], in0=core.bank(1, P, N2), scalar=core.param("qk_gain", 5, 1),
                                         in1=root[:, :], op0=ALU.mult, op1=ALU.mult)
                dve.wait_ge(f["silued"].sem, f["silued"].value(1))
                for h in range(8):
                    last = dve.tensor_tensor(CG0[:, h:h + 1], CG[:, 0, 3 * h:3 * h + 1], core.param("valid31"),
                                             ALU.mult)

            @block.tensor
            def _(pe):
                for kv in range(2):
                    c, w = core.chunk(f"cmp{kv}")
                    core.await_chunk(pe, c)
                    pe.wait_ge(f["made"].sem, f["made"].value(kv + 1))
                    for ht in range(2):
                        last = products(pe, core.bank(0, P, N2, (2 * kv + ht) * N2),
                                        [(w[:, m, ht * P:(ht + 1) * P], blocks[:, kv, m, :]) for m in range(16)])
                    last.then_inc(f["products_done"].sem, 1)
                pe.wait_ge(f["made"].sem, f["made"].value(3))
                products(pe, core.bank(1, P, N2), [(w2[:, 0, ht, :], x[:, ht * N2:(ht + 1) * N2]) for ht in range(2)])
                for g in range(2):
                    last = products(pe, core.bank(2, NC_CMP, HD, g * HD),
                                    [(x[:, (2 + ht) * N2 + g * NC_CMP:(2 + ht) * N2 + (g + 1) * NC_CMP],
                                      w2[:, 1, ht, 0:HD]) for ht in range(2)])
                last.then_inc(f["summed"].sem, 1)
                pe.wait_ge(f["normed"].sem, f["normed"].value(1))
                pe.matmul(core.bank(3, P, N2), core.const("blocks"), sq[:, :], start=True, stop=True)\
                    .then_inc(f["turned"].sem, 1)

            @block.scalar
            def _(act):
                act.activation(CG[:, :, :], CG[:, :, :], ACT.Sigmoid).then_inc(f["silued"].sem, 1)
                act.wait_ge(f["squared"].sem, f["squared"].value(1))
                act.activation(t[:, :], t[:, :], ACT.Tanh, scale=math.sqrt(2 / math.pi)).then_inc(f["exped"].sem, 1)
                act.wait_ge(f["summed"].sem, f["summed"].value(1))
                act.activation(sq[:, :], core.bank(1, P, N2), ACT.Square).then_inc(f["normed"].sem, 1)
                act.wait_ge(f["turned"].sem, f["turned"].value(1))
                core.s_chain(act, act.activation(root[:, :], core.bank(3, P, N2), ACT.Ln, bias=core.eps[:, 0:1],
                                                 scale=1.0 / HD))
                act.activation(root[:, :], root[:, :], ACT.Exp, scale=-0.5).then_inc(f["rooted"].sem, 1)
    core.consumed += 2
    f["misc_loaded"].advance(128)
    f["made"].advance(3)
    f["products_done"].advance(2)
    for k in ("squared", "exped", "summed", "rooted", "silued", "normed", "turned"):
        f[k].advance(1)


def bias_tile(core, row, u0, n):
    whole = core.dram["bias"]
    return bass.AP(whole.tensor, row * P * TABLE + P - 1 + u0, [[TABLE - 1, P], [1, n]])


def first_block(core):
    nc, f = core.nc, core.flags
    normalise(core, "norm1", [LAT], lambda k, p: core.param("norm_mix", k, 1))
    with ExitStack() as stack:
        def sb(name, shape):
            return stack.enter_context(nc.sbuf_tensor(name, shape, F32))
        Q = sb("Q", [P, 12, S])
        YS = sb("YS", [P, KD, S])
        V = sb("V", [P, 4, 512 + 384])
        CG = sb("CG", [P, 4, 24])
        CG0 = sb("CG0", [P, 8])
        KC = sb("KC", [P, 2 * NC_CMP])
        VC = sb("VC", [NC_CMP, P])
        AQ, BQ, CQ = Q[:, 0:4, :], Q[:, 4:8, :], Q[:, 8:12, :]
        AK, KK = YS[:, 0:4, :], YS[:, 4:7, :]
        with ExitStack() as inner:
            def tmp(name, shape):
                return inner.enter_context(nc.sbuf_tensor(name, shape, F32))
            CK = tmp("CK", [P, 2, S])
            jobs = [j for i in range(4) for j in feature_jobs(core, f"proj{i}", [LAT])]
            jobs += feature_jobs(core, "proj4", [LAT], tiles=range(3), release=False)
            dests = [AQ[:, i, :] for i in range(4)] + [AK[:, i, :] for i in range(4)] + \
                    [BQ[:, i, :] for i in range(4)] + [CQ[:, i, :] for i in range(4)] + \
                    [KK[:, i, :] for i in range(3)]
            der = core.derived
            gains = [der[:, AQ_G:AQ_G + 1]] * 4 + [core.param("qk_gain", 1, 1)] * 4 + [der[:, BQ_G:BQ_G + 1]] * 4 + \
                    [der[:, CQ_G:CQ_G + 1]] * 4 + [core.param("qk_gain", i, 1) for i in (3, 6, 7)]
            with nc.sbuf_tensor("squares", [P, 2, 512], F32) as sq, nc.sbuf_tensor("roots", [P, 2, 512], F32) as rt:
                head_normed(core, "project_qk", jobs, (sq, rt), lambda n: dests[n], lambda n: gains[n], HD,
                            core.const("blocks"))
            jobs = feature_jobs(core, "proj4", [LAT], tiles=range(3, 4))
            jobs += feature_jobs(core, "proj5", [LAT], tiles=range(0, 1), release=False)
            to = [CK[:, 0, :], CK[:, 1, :]]
            jobs += token_jobs(core, "proj5", 4, P, 512)
            to += [V[:, t, 512:896] for t in range(4)]
            jobs += token_jobs(core, "proj6", 4, 0, 512)
            to += [V[:, t, 0:512] for t in range(4)]
            jobs += token_jobs(core, "proj7", 4, 0, 24)
            to += [CG[:, t, :] for t in range(4)]
            dense(core, "project_v", jobs, copy_out(core, lambda n: to[n]))
            compress(core, CK, KC, VC, CG, CG0)

        with ExitStack() as inner:
            bias = inner.enter_context(nc.sbuf_tensor("bias_tiles", [P, 2, 512], F32))
            neg_lam = core.derived[:, NEG_LAM:NEG_LAM + 1]
            units, loads = [], []
            for h in range(4):
                loads.append((bias[:, h % 2, :], bias_tile(core, h, 0, 512), 8 * (h - 1) - 1 if h >= 2 else None))
                for i in range(4):
                    for c in range(2):
                        rows = slice(64 * c, 64 * c + 64)
                        units.append(unit(
                            AQ[rows, h, i * P:(i + 1) * P], [AK[rows, h, 0:(i + 1) * P]],
                            [V[:, t, h * P:(h + 1) * P] for t in range(i + 1)], h % 2, i * P, c == 0, c == 1,
                            bias=bias[:, h % 2, 384 - P * i:512], bias_load=h, coef=neg_lam if c else 1.0,
                            evac=(AQ[:, h, :], (0, P)) if (i, c) == (3, 1) else None))
            attention(core, "attn_a", plan_outputs(units), loads)

            units, loads = [], []
            for h in range(8):
                j, g = h % 4, h // 4
                rows = slice(64 * g, 64 * g + 64)
                loads.append((bias[:, h % 2, 0:256], bias_tile(core, 12 + h, 256, 256),
                              4 * (h - 1) - 1 if h >= 2 else None))
                for i in range(4):
                    lo = max(0, i - 1)
                    units.append(unit(
                        BQ[rows, j, i * P:(i + 1) * P], [KK[rows, 0, lo * P:(i + 1) * P]],
                        [V[:, t, 512:640] for t in range(lo, i + 1)], h % 2, i * P,
                        bias=bias[:, h % 2, 0 if i else P:256], bias_load=h, sink=core.param("sinks", h, 1),
                        evac=(BQ[rows, j, :], (64 * g, 64 * g + 64)) if i == 3 else None))
            attention(core, "attn_b", plan_outputs(units), loads)

            units, loads = [], []
            for h in range(8):
                j, g = h % 4, h // 4
                rows = slice(64 * g, 64 * g + 64)
                loads.append((bias[:, h % 2, :], bias_tile(core, 4 + h, 0, 512), 12 * (h - 1) - 1 if h >= 2 else None))
                for i in range(4):
                    q = CQ[rows, j, i * P:(i + 1) * P]
                    mask = core.const("cmask")[:, i * NC_CMP:(i + 1) * NC_CMP]
                    units.append(unit(q, [KC[rows, g * NC_CMP:(g + 1) * NC_CMP]], [VC[:, :]], h % 2, i * P, True, False,
                                      bias=mask, coef=CG[:, i, 3 * h:3 * h + 1] if i else CG0[:, h:h + 1]))
                    for b in range(2):
                        units.append(unit(
                            q, [KK[rows, 1 + b, 0:(i + 1) * P]],
                            [V[:, t, 640 + P * b:768 + P * b] for t in range(i + 1)], h % 2, i * P, False, b == 1,
                            bias=bias[:, h % 2, 384 - P * i:512], bias_load=h,
                            coef=CG[:, i, 3 * h + 1 + b:3 * h + 2 + b],
                            evac=(CQ[rows, j, :], (64 * g, 64 * g + 64)) if (i, b) == (3, 1) else None))
            attention(core, "attn_c", plan_outputs(units), loads)

        with ExitStack() as inner:
            def tmp(name, shape):
                return inner.enter_context(nc.sbuf_tensor(name, shape, F32))
            scratch = tmp("squares2", [P, 2, 512]), tmp("roots2", [P, 2, 512])
            head_normed(core, "norm_a", [(None, False, P, S, None)] * 4, scratch, lambda n: AQ[:, n, :],
                        lambda n: core.derived[:, SUBLN:SUBLN + 1], P, core.const("ones"),
                        sources=[AQ[:, n, :] for n in range(4)])
        branches(core, Q, YS)
        residual(core, "mix_out", ["out0", "out1"], lambda k, t0, tn: YS[:, k, t0:t0 + tn], [LAT])

    normalise(core, "norm_mlp", [LAT], lambda k, p: core.param("norm_mlp", k, 1))
    with nc.sbuf_tensor("hidden", [P, D_FF // P, S], F32) as U:
        jobs = [j for i in range(8) for j in feature_jobs(core, f"up{i}", [LAT])]

        def squared_relu(eng, n, ps):
            if eng is nc.scalar:
                core.s_chain(eng, eng.activation(U[:, n, :], ps, ACT.Relu))
                return eng.activation(U[:, n, :], U[:, n, :], ACT.Square)
            core.v_chain(eng, eng.tensor_scalar(U[:, n, :], ps, 0.0, None, ALU.max))
            return eng.tensor_tensor(U[:, n, :], U[:, n, :], U[:, n, :], ALU.mult)
        dense(core, "mlp_up", jobs, squared_relu)
        residual(core, "mlp_down", [f"down{i}" for i in range(8)], lambda k, t0, tn: U[:, k, t0:t0 + tn], [LAT])


def branches(core, Q, YS):
    nc, f = core.nc, core.flags
    with nc.sbuf_tensor("gates", [P, 2, S], F32) as SG, nc.sbuf_tensor("gated_y", [P, 2, S], F32) as GY:
        for n in range(3):
            for half in range(2):
                core.used_up[core.plan[f"mg{n}_{half}"][0]] = \
                    (f["products_done"], f["products_done"].value(8 * n + 4 * half + 4))
            core.used_up[core.plan[f"branch{n}"][0]] = (f["down_done"], f["down_done"].value(8 * n + 8))
        with nc.Block("branches") as block:
            @block.sync
            def _(sp):
                core.feed(sp, core.consumed + 9)

            @block.tensor
            def _(pe):
                for i in range(24):
                    n, m = i // 8, i % 8
                    if m % 4 == 0:
                        c, w = core.chunk(f"mg{n}_{m // 4}")
                        core.await_chunk(pe, c)
                    if i >= 2:
                        pe.wait_ge(f["silued"].sem, f["silued"].value(i - 1))
                    last = products(pe, core.bank(i % 2), [(w[:, k, (m % 4) * P:(m % 4 + 1) * P], core.H[:, k, 0:S])
                                                           for k in range(KD)])
                    last.then_inc(f["products_done"].sem, 1)
                    cb, wb = core.chunk(f"branch{n}")
                    if m == 0:
                        core.await_chunk(pe, cb)
                    if i >= 2:
                        pe.wait_ge(f["gated"].sem, f["gated"].value(i - 1))
                    last = products(pe, core.bank(2 + i % 2), [(wb[:, k, m * P:(m + 1) * P], Q[:, 4 * n + k, :])
                                                               for k in range(4)])
                    last.then_inc(f["down_done"].sem, 1)

            @block.scalar
            def _(act):
                for i in range(24):
                    act.wait_ge(f["products_done"].sem, f["products_done"].value(i + 1))
                    if i >= 2:
                        act.wait_ge(f["gated"].sem, f["gated"].value(i - 1))
                    act.activation(SG[:, i % 2, :], core.bank(i % 2), ACT.Sigmoid).then_inc(f["silued"].sem, 1)

            @block.vector
            def _(dve):
                for i in range(24):
                    m = i % 8
                    dve.wait_ge(f["silued"].sem, f["silued"].value(i + 1))
                    dve.wait_ge(f["down_done"].sem, f["down_done"].value(i + 1))
                    y = core.bank(2 + i % 2)
                    if i < 8:
                        dve.tensor_tensor(YS[:, m, :], SG[:, i % 2, :], y, ALU.mult).then_inc(f["gated"].sem, 1)
                    else:
                        core.v_chain(dve, dve.tensor_tensor(GY[:, i % 2, :], SG[:, i % 2, :], y, ALU.mult))
                        dve.tensor_tensor(YS[:, m, :], YS[:, m, :], GY[:, i % 2, :], ALU.add).then_inc(f["gated"].sem, 1)
    core.consumed += 9
    for k in ("products_done", "down_done", "silued", "gated"):
        f[k].advance(24)


def rotate(core, name, tiles, cos_sin):
    nc, f = core.nc, core.flags
    with nc.sbuf_tensor(name + "_turned", [P, 2, S], F32) as R, nc.Block(name) as block:
        @block.tensor
        def _(pe):
            for n, tile in enumerate(tiles):
                if n >= 2:
                    pe.wait_ge(f["normed"].sem, f["normed"].value(n - 1))
                pe.matmul(core.bank(n % 2), core.const("rot"), tile, start=True, stop=True)\
                    .then_inc(f["turned"].sem, 1)

        @block.vector
        def _(dve):
            for n, tile in enumerate(tiles):
                dve.wait_ge(f["turned"].sem, f["turned"].value(n + 1))
                dve.tensor_tensor(R[:, n % 2, :], core.bank(n % 2), cos_sin[:, 1, :], ALU.mult)
                core.v_chain(dve, dve.tensor_tensor(tile, tile, cos_sin[:, 0, :], ALU.mult))
                dve.tensor_tensor(tile, tile, R[:, n % 2, :], ALU.add).then_inc(f["normed"].sem, 1)
    f["turned"].advance(len(tiles))
    f["normed"].advance(len(tiles))


def over(ap, n):
    return ap.broadcast_to([ap.shape[0], ap.shape[1], n])


def gla_decays(core, z, GQ, GK, LR, gate_w, bufs, rates):
    nc, f = core.nc, core.flags
    CLIP = 40.0
    NCH = T // P
    B, G, EQ, EK0, EK1, QB, KE = (b[:, :] for b in bufs)
    GQf, GKf = (x[:, :, :].rearrange("p a t -> p (a t)") for x in (GQ, GK))
    parts = [LAT, CON]

    def by_chunk(x):
        return x.rearrange("p (c t) -> p c t", t=P)

    with nc.Block(f"decays{z}") as block:
        @block.tensor
        def _(pe):
            for a in range(2):
                for p, (t0, tn) in enumerate(parts):
                    pe.matmul(core.bank(2 * a + p, P, tn), gate_w[:, z, a * P:(a + 1) * P], LR[:, t0:t0 + tn],
                              start=True, stop=True).then_inc(f["products_done"].sem, 1)

        @block.vector
        def _(dve):
            def step(ins):
                core.v_chain(dve, ins)
            for a in range(2):
                for p, (t0, tn) in enumerate(parts):
                    dve.wait_ge(f["products_done"].sem, f["products_done"].value(2 * a + p + 1))
                    last = dve.tensor_scalar(G[:, a * T + t0:a * T + t0 + tn], core.bank(2 * a + p, P, tn),
                                             core.param("gla_b", 2 * z + a, 1), None, ALU.add)
            step(last)
            dve.scalar_tensor_tensor(out=B, in0=G, scalar=-1.0, in1=G, op0=ALU.mult, op1=ALU.max)\
                .then_inc(f["made"].sem, 1)
            dve.wait_ge(f["rooted"].sem, f["rooted"].value(1))
            step(dve.scalar_tensor_tensor(out=G, in0=G, scalar=0.0, in1=B, op0=ALU.min, op1=ALU.subtract))
            step(dve.tensor_scalar(G, G, 1.0 / 16.0, None, ALU.mult))
            step(dve.memset(KE, 1.0))
            for c in range(2 * NCH):
                last = dve.tensor_tensor_scan(out=by_chunk(B)[:, c, :], data0=by_chunk(KE)[:, c, :],
                                              data1=by_chunk(G)[:, c, :], initial=0.0, op0=ALU.mult, op1=ALU.add)
            step(last)
            if z == 1:
                step(dve.tensor_tensor(G, G, B, ALU.subtract))
                step(dve.tensor_copy(rates[:, 0:1, :].rearrange("p a c -> p c a"), by_chunk(B)[:, :, P - 1:P]))
                step(dve.tensor_tensor(by_chunk(B), by_chunk(G),
                                       over(rates[:, 0:1, :].rearrange("p a c -> p c a"), P), ALU.add))
            end = P - 1 if z == 0 else 0
            total = by_chunk(B)[:, :, end:end + 1]
            step(dve.tensor_copy(rates[:, 1:2, :].rearrange("p a c -> p c a"), total))
            total = rates[:, 1:2, :].rearrange("p a c -> p c a")
            for half in range(2):
                mid = by_chunk(B)[:, :, 64 * half + 32:64 * half + 33]
                EK = (EK0, EK1)[half]
                step(dve.tensor_copy(rates[:, 2 + half:3 + half, :].rearrange("p a c -> p c a"), mid))
                mid = rates[:, 2 + half:3 + half, :].rearrange("p a c -> p c a")
                dve.tensor_tensor(by_chunk(EK), over(mid, P), by_chunk(B), ALU.subtract)
                t = slice(64 * half, 64 * half + 64)
                step(dve.tensor_tensor(by_chunk(EQ)[:, :, t], by_chunk(B)[:, :, t], over(mid, 64), ALU.subtract))
                step(dve.tensor_scalar(EK, EK, CLIP, None, ALU.min))
            step(dve.tensor_scalar(EQ, EQ, CLIP, None, ALU.min))
            step(dve.tensor_tensor(by_chunk(KE), over(total, P), by_chunk(B), ALU.subtract))
            dve.tensor_copy(QB, B).then_inc(f["made"].sem, 1)
            for n, (e, x) in enumerate(((EQ, GQf), (QB, GQf), (EK0, GKf), (EK1, GKf), (KE, GKf))):
                dve.wait_ge(f["exped"].sem, f["exped"].value(n + 1))
                dve.tensor_tensor(e, e, x, ALU.mult)

        @block.scalar
        def _(act):
            act.wait_ge(f["made"].sem, f["made"].value(1))
            core.s_chain(act, act.activation(B, B, ACT.Exp, scale=-1.0))
            act.activation(B, B, ACT.Ln, bias=1.0).then_inc(f["rooted"].sem, 1)
            act.wait_ge(f["made"].sem, f["made"].value(2))
            for e in (EQ, QB, EK0, EK1, KE):
                act.activation(e, e, ACT.Exp).then_inc(f["exped"].sem, 1)
            act.activation(rates[:, 1, :], rates[:, 1, :], ACT.Exp)
    f["products_done"].advance(4)
    f["made"].advance(2)
    f["rooted"].advance(1)
    f["exped"].advance(5)


def gla_chunks(core, z, GV, GO, bufs, rates, state, keys, att):
    nc, f = core.nc, core.flags
    _, _, EQ, EK0, EK1, QB, KE = (b[:, :].rearrange("p (a t) -> p a t", a=2) for b in bufs)
    NCH = T // P
    order = [4, 5, 0, 1, 2, 3] if z == 0 else [5, 4, 3, 2, 1, 0]
    mask = core.const("causal_st") if z == 0 else core.const("anti_st")
    steps = [(n, c, h) for n, c in enumerate(order) for h in range(4)]

    with nc.Block(f"gla{z}") as block:
        @block.tensor
        def _(pe):
            def scores(i):
                n, c, h = steps[i]
                a, rows = h // 2, slice(64 * (h % 2), 64 * (h % 2) + 64)
                if i >= 2:
                    pe.wait_ge(f["weighted"].sem, f["weighted"].value(i - 1))
                for half, EK in enumerate((EK0, EK1)):
                    last = pe.matmul(core.bank(i % 2, P, 64, 64 * half), EK[rows, a, c * P:(c + 1) * P],
                                     EQ[rows, a, c * P + 64 * half:c * P + 64 * half + 64], start=True, stop=True)
                last.then_inc(f["scored"].sem, 1)
                if h % 2 == 0:
                    j = i // 2
                    if j >= 2:
                        pe.wait_ge(f["copied"].sem, f["copied"].value(j - 1))
                    pe.transpose(core.bank(2 + j % 2, P, P), KE[:, a, c * P:(c + 1) * P], core.const("ident"))\
                        .then_inc(f["turned"].sem, 1)

            def values(i):
                n, c, h = steps[i]
                a, rows = h // 2, slice(64 * (h % 2), 64 * (h % 2) + 64)
                v = GV[:, c, h * P:(h + 1) * P]
                pe.wait_ge(f["weighted"].sem, f["weighted"].value(i + 1))
                if i >= 2:
                    pe.wait_ge(f["emptied"].sem, f["emptied"].value(i - 1))
                last = pe.matmul(core.bank(4 + i % 2, P, P), v, att[:, i % 2, :], start=True, stop=n == 0)
                if n:
                    pe.wait_ge(f["added"].sem, f["added"].value(i - 3))
                    last = pe.matmul(core.bank(4 + i % 2, P, P), state[rows, h, :], QB[rows, a, c * P:(c + 1) * P],
                                     start=False, stop=True)
                last.then_inc(f["attended"].sem, 1)
                pe.wait_ge(f["copied"].sem, f["copied"].value(i // 2 + 1))
                if i >= 2:
                    pe.wait_ge(f["added"].sem, f["added"].value(i - 1))
                pe.matmul(core.bank(6 + i % 2, P, P), keys[:, (i // 2) % 2, :], v, start=True, stop=True)\
                    .then_inc(f["summed"].sem, 1)

            for i in range(len(steps) + 1):
                if i < len(steps):
                    scores(i)
                if i >= 1:
                    values(i - 1)

        @block.scalar
        def _(act):
            for j in range(len(steps) // 2):
                act.wait_ge(f["turned"].sem, f["turned"].value(j + 1))
                if j >= 2:
                    act.wait_ge(f["summed"].sem, f["summed"].value(2 * j - 2))
                act.activation(keys[:, j % 2, :], core.bank(2 + j % 2, P, P), ACT.Copy).then_inc(f["copied"].sem, 1)

        @block.vector
        def _(dve):
            def masked(i):
                dve.wait_ge(f["scored"].sem, f["scored"].value(i + 1))
                if i >= 2:
                    dve.wait_ge(f["attended"].sem, f["attended"].value(i - 1))
                dve.tensor_tensor(att[:, i % 2, :], mask, core.bank(i % 2, P, P), ALU.mult)\
                    .then_inc(f["weighted"].sem, 1)

            def out(i):
                n, c, h = steps[i]
                a, rows = h // 2, slice(64 * (h % 2), 64 * (h % 2) + 64)
                dve.wait_ge(f["attended"].sem, f["attended"].value(i + 1))
                dst, ps = GO[:, h, c * P:(c + 1) * P], core.bank(4 + i % 2, P, P)
                if z == 0:
                    last = dve.tensor_copy(dst, ps)
                else:
                    last = dve.tensor_tensor(dst, dst, ps, ALU.add)
                last.then_inc(f["emptied"].sem, 1)
                dve.wait_ge(f["summed"].sem, f["summed"].value(i + 1))
                u = core.psum[rows, 6 + i % 2, 0:P]
                if n == 0:
                    last = dve.tensor_copy(state[rows, h, :], u)
                else:
                    last = dve.scalar_tensor_tensor(out=state[rows, h, :], in0=state[rows, h, :],
                                                    scalar=rates[rows, 1, a * NCH + c:a * NCH + c + 1], in1=u,
                                                    op0=ALU.mult, op1=ALU.add)
                last.then_inc(f["added"].sem, 1)

            for i in range(len(steps) + 1):
                if i < len(steps):
                    masked(i)
                if i >= 1:
                    out(i - 1)
    N = len(steps)
    for k in ("scored", "weighted", "attended", "summed", "emptied", "added"):
        f[k].advance(N)
    f["turned"].advance(N // 2)
    f["copied"].advance(N // 2)


def even_layer(core):
    nc, f, dram = core.nc, core.flags, core.dram
    parts = [LAT, CON]
    modulated_norm(core, "norm_e", 0, 0, parts)
    with ExitStack() as stack:
        def sb(name, shape):
            return stack.enter_context(nc.sbuf_tensor(name, shape, F32))
        AQ = sb("eAQ", [P, 4, T])
        LR = sb("LR", [32, T])
        with ExitStack() as inner:
            def tmp(name, shape):
                return inner.enter_context(nc.sbuf_tensor(name, shape, F32))
            AK = tmp("eAK", [P, T])
            AV = tmp("eAV", [P, T // P, P])
            trig = tmp("trig", [P, 2, S])
            with nc.Block("load_trig") as block:
                @block.sync
                def _(sp):
                    sp.dma_start(trig[:, :, :], dram["trig"]).then_inc(f["misc_loaded"].sem, 16)
                    sp.wait_ge(f["misc_loaded"].sem, f["misc_loaded"].value(16))
            f["misc_loaded"].advance(16)
            scratch = tmp("squares_e", [P, 2, 512]), tmp("roots_e", [P, 2, 512])
            jobs = feature_jobs(core, "ev0", parts)
            jobs += feature_jobs(core, "ev1", parts, tiles=range(1), release=False)
            dests = [AQ[:, j, t0:t0 + tn] for j in range(4) for t0, tn in parts] + [AK[:, t0:t0 + tn] for t0, tn in parts]
            head_normed(core, "project_eqk", jobs, scratch, lambda n: dests[n],
                        lambda n: core.derived[:, ATT_G:ATT_G + 1] if n < 8 else core.param("att_k"), HD,
                        core.const("blocks"))
            c, w = core.chunk("ev1")
            jobs = [(c, False, 32, tn, [(w[:, k, 256:288], core.H[:, k, t0:t0 + tn]) for k in range(KD)])
                    for t0, tn in parts]
            jobs += token_jobs(core, "ev1", T // P, P, 2 * P)
            to = [LR[:, t0:t0 + tn] for t0, tn in parts] + [AV[:, t, :] for t in range(T // P)]
            dense(core, "project_ev", jobs, copy_out(core, lambda n: to[n]))
            rotate(core, "rope_e", [AQ[:, j, 0:S] for j in range(4)] + [AK[:, 0:S]], trig)
            units = []
            for h in range(8):
                j, g = h % 4, h // 4
                rows = slice(64 * g, 64 * g + 64)
                for t0, tn, keys in ((0, S, [(0, S), (S, CTX)]), (S, CTX, [(S, CTX)])):
                    tiles = [t for k0, kn in keys for t in range(k0 // P, (k0 + kn) // P)]
                    for i in range(tn // P):
                        last = i == tn // P - 1
                        units.append(unit(
                            AQ[rows, j, t0 + i * P:t0 + (i + 1) * P], [AK[rows, k0:k0 + kn] for k0, kn in keys],
                            [AV[:, t, :] for t in tiles], (0 if t0 == 0 else 1), i * P,
                            evac=(AQ[rows, j, t0:t0 + tn], (64 * g, 64 * g + 64)) if last else None))
            attention(core, "attn_e", plan_outputs(units))

        GQ, GK = sb("GQ", [P, 2, T]), sb("GK", [P, 2, T])
        GR = sb("GR", [P, 4, T])
        GV = sb("GV", [P, T // P, 512])
        jobs = feature_jobs(core, "ev2", parts)
        to = [x[:, a, t0:t0 + tn] for x in (GQ, GK) for a in range(2) for t0, tn in parts]

        def take_qk(eng, n, ps):
            scale = HD ** -0.5 if n < 4 else 1.0
            if eng is nc.scalar:
                return eng.activation(to[n], ps, ACT.Copy, scale=scale)
            return eng.tensor_scalar(to[n], ps, scale, None, ALU.mult)
        dense(core, "project_gqk", jobs, take_qk)
        to_r = [GR[:, a, t0:t0 + tn] for a in range(4) for t0, tn in parts]
        dense(core, "project_gr", feature_jobs(core, "ev3", parts), copy_out(core, lambda n: to_r[n]))
        dense(core, "project_gv", token_jobs(core, "ev4", T // P, 0, 512), copy_out(core, lambda n: GV[:, n, :]))

        GO = sb("GO", [P, 4, T])
        with ExitStack() as inner:
            def tmp(name, shape):
                return inner.enter_context(nc.sbuf_tensor(name, shape, F32))
            Hf = core.H[:, :, :].rearrange("p k t -> p (k t)")
            n = 2 * T
            bufs = [tmp("gB", [P, n]), tmp("gG", [P, n])] + [Hf[:, i * n:(i + 1) * n] for i in range(4)] + [tmp("gKE", [P, n])]
            rates = tmp("rates", [P, 4, 2 * T // P])
            state = tmp("state", [P, 4, P])
            keys = tmp("keys", [P, 2, P])
            att = tmp("att", [P, 2, P])
            gate_w = tmp("gate_w", [32, 2, 256])
            with nc.Block("load_gate_w") as block:
                @block.sync
                def _(sp):
                    sp.dma_start(gate_w[:, :, :], dram["gate_w"]).then_inc(f["misc_loaded"].sem, 16)
                    sp.wait_ge(f["misc_loaded"].sem, f["misc_loaded"].value(16))
            f["misc_loaded"].advance(16)
            for z in range(2):
                gla_decays(core, z, GQ, GK, LR, gate_w, bufs, rates)
                gla_chunks(core, z, GV, GO, bufs, rates, state, keys, att)
        with ExitStack() as inner:
            def tmp(name, shape):
                return inner.enter_context(nc.sbuf_tensor(name, shape, F32))
            scratch = core.H[:, 0:2, 0:512], core.H[:, 2:4, 0:512]
            tiles = [GO[:, h, t0:t0 + tn] for h in range(4) for t0, tn in parts]
            head_normed(core, "norm_g", [(None, False, P, t.shape[-1], None) for t in tiles], scratch,
                        lambda n: tiles[n], lambda n: core.param("gla_norm"), P, core.const("ones"), sources=tiles)
            with nc.Block("silu_r") as block:
                @block.scalar
                def _(act):
                    for h in range(4):
                        act.activation(core.H[:, h, :], GR[:, h, :], ACT.Sigmoid).then_inc(f["silued"].sem, 1)

                @block.vector
                def _(dve):
                    for h in range(4):
                        core.v_chain(dve, dve.tensor_tensor(GO[:, h, :], GO[:, h, :], GR[:, h, :], ALU.mult))
                        dve.wait_ge(f["silued"].sem, f["silued"].value(h + 1))
                        dve.tensor_tensor(GO[:, h, :], GO[:, h, :], core.H[:, h, :], ALU.mult)
            f["silued"].advance(4)
        residual(core, "even_out", ["ev_out0", "ev_out1"],
                 lambda k, t0, tn: (GO if k < 4 else AQ)[:, k % 4, t0:t0 + tn], parts,
                 gate=lambda m, p: core.mods[:, 0, 16 + m, p:p + 1])


def odd_layer(core):
    nc, f, dram = core.nc, core.flags, core.dram
    parts = [LAT, CON]
    modulated_norm(core, "norm_o", 1, 0, parts)
    with ExitStack() as stack:
        def sb(name, shape):
            return stack.enter_context(nc.sbuf_tensor(name, shape, F32))
        Q = sb("oQ", [P, 8, S])
        K = sb("oK", [P, T])
        V = sb("oV", [P, T // P, P])
        trig = sb("trig_o", [P, 2, S])
        masks = sb("masks_o", [P, 640 + 512])
        with nc.Block("load_trig_o") as block:
            @block.sync
            def _(sp):
                sp.dma_start(trig[:, :, :], dram["trig"]).then_inc(f["misc_loaded"].sem, 16)
                sp.dma_start(masks[:, :], dram["window"]).then_inc(f["misc_loaded"].sem, 16)
                sp.wait_ge(f["misc_loaded"].sem, f["misc_loaded"].value(32))
        f["misc_loaded"].advance(32)
        with ExitStack() as inner:
            scratch = [inner.enter_context(nc.sbuf_tensor(n, [P, 2, 512], F32)) for n in ("squares_o", "roots_o")]
            jobs = feature_jobs(core, "od0", [LAT]) + feature_jobs(core, "od1", [LAT])
            jobs += feature_jobs(core, "od2", parts, tiles=range(1), release=False)
            dests = [Q[:, j, :] for j in range(8)] + [K[:, t0:t0 + tn] for t0, tn in parts]
            head_normed(core, "project_oqk", jobs, scratch, lambda n: dests[n],
                        lambda n: core.derived[:, SWA_G:SWA_G + 1] if n < 8 else core.param("swa_k"), HD,
                        core.const("blocks"))
        dense(core, "project_ov", token_jobs(core, "od2", T // P, P, 2 * P), copy_out(core, lambda n: V[:, n, :]))
        rotate(core, "rope_o", [Q[:, j, :] for j in range(8)] + [K[:, 0:S]], trig)
        units = []
        for h in range(16):
            j, g = h % 8, h // 8
            rows = slice(64 * g, 64 * g + 64)
            for i in range(4):
                lo, hi = max(0, i - 1), min(3, i + 1)
                n = CTX + (hi - lo + 1) * P
                mask = masks[:, 0:n] if i else masks[:, 640:640 + n]
                units.append(unit(
                    Q[rows, j, i * P:(i + 1) * P], [K[rows, S:T], *split_keys(K, rows, lo, hi)],
                    [V[:, t, :] for t in (4, 5, *range(lo, hi + 1))], h % 2, i * P, bias=mask,
                    sink=core.param("swa_sink", h, 1),
                    evac=(Q[rows, j, :], (64 * g, 64 * g + 64)) if i == 3 else None))
        attention(core, "attn_o", plan_outputs(units))
        residual(core, "odd_out", ["od_out0", "od_out1"], lambda k, t0, tn: Q[:, k, t0:t0 + tn], [LAT],
                 gate=lambda m, p: core.mods[:, 1, 16 + m, p:p + 1])


def split_keys(K, rows, lo, hi):
    cut = min(lo + 2, hi + 1)
    return [K[rows, a * P:b * P] for a, b in ((lo, cut), (cut, hi + 1)) if b > a]


def route(core, l, tokens, comb_dram):
    nc, f = core.nc, core.flags
    NT = tokens // P
    with ExitStack() as stack:
        def sb(name, shape):
            return stack.enter_context(nc.sbuf_tensor(f"{name}{l}", shape, F32))
        L = sb("logits", [P, NT, 20])
        one = sb("rt_one", [P, NT, 8])
        hot = sb("rt_hot", [P, NT, 12])
        tmp4 = sb("rt_tmp4", [P, NT, 4])
        esel = sb("rt_esel", [P, NT, 4])
        eall = sb("rt_eall", [P, NT, 16])
        taken = sb("rt_taken", [P, NT])
        comb = sb("rt_comb", [P, NT, 16])
        combT = sb("rt_combT", [16, tokens])
        with nc.Block(f"route{l}") as block:
            @block.tensor
            def _(pe):
                for t in range(NT):
                    last = products(pe, core.bank(0, P, 20, 20 * t),
                                    [(core.H[:, k, t * P:(t + 1) * P], core.router[:, l, k, :]) for k in range(KD)])
                last.then_inc(f["products_done"].sem, 1)
                pe.wait_ge(f["made"].sem, f["made"].value(1))
                for t in range(NT):
                    last = pe.transpose(core.psum[0:16, 1 + t // 4, (t % 4) * P:(t % 4 + 1) * P], comb[:, t, :],
                                        core.const("ident"))
                last.then_inc(f["turned"].sem, 1)

            @block.vector
            def _(dve):
                def step(ins):
                    core.v_chain(dve, ins)

                def pick(best, scores, out):
                    step(dve.tensor_tensor(tmp4[:, :, :], scores, over(best, 4), ALU.is_equal))
                    step(dve.tensor_copy(out[:, :, 0], tmp4[:, :, 0]))
                    step(dve.tensor_copy(taken[:, :], tmp4[:, :, 0]))
                    for e in range(1, 4):
                        step(dve.tensor_tensor(out[:, :, e], tmp4[:, :, e], taken[:, :], ALU.is_gt))
                        if e < 3:
                            step(dve.tensor_tensor(taken[:, :], taken[:, :], tmp4[:, :, e], ALU.max))

                dve.wait_ge(f["products_done"].sem, f["products_done"].value(1))
                for t in range(NT):
                    last = dve.tensor_tensor(L[:, t, :], core.bank(0, P, 20, 20 * t),
                                             core.param("router_b", 20 * l, 20), ALU.add)
                step(last)
                G = L[:, :, 0:4]
                step(dve.tensor_reduce(one[:, :, 0:1], G, AX.X, ALU.max))
                pick(one[:, :, 0:1], G, hot[:, :, 0:4])
                step(dve.tensor_tensor(esel[:, :, :], G, over(one[:, :, 0:1], 4), ALU.subtract))
                dve.tensor_copy(tmp4[:, :, :], esel[:, :, :]).then_inc(f["weighted"].sem, 1)
                for g in range(4):
                    last = dve.tensor_tensor(eall[:, :, 4 * g:4 * g + 4], L[:, :, 4 + 4 * g:8 + 4 * g],
                                             over(hot[:, :, g:g + 1], 4), ALU.mult)
                step(last)
                for g in range(1, 4):
                    step(dve.tensor_tensor(eall[:, :, 0:4], eall[:, :, 0:4], eall[:, :, 4 * g:4 * g + 4], ALU.add))
                dve.wait_ge(f["exped"].sem, f["exped"].value(1))
                step(dve.tensor_reduce(one[:, :, 1:2], tmp4[:, :, :], AX.X, ALU.add))
                step(dve.reciprocal(one[:, :, 2:3], one[:, :, 1:2]))
                step(dve.tensor_copy(esel[:, :, :], eall[:, :, 0:4]))
                step(dve.tensor_reduce(one[:, :, 3:4], esel[:, :, :], AX.X, ALU.max))
                pick(one[:, :, 3:4], esel[:, :, :], hot[:, :, 4:8])
                step(dve.tensor_scalar(tmp4[:, :, :], hot[:, :, 4:8], NEG, None, ALU.mult))
                step(dve.tensor_tensor(esel[:, :, :], esel[:, :, :], tmp4[:, :, :], ALU.add))
                step(dve.tensor_reduce(one[:, :, 4:5], esel[:, :, :], AX.X, ALU.max))
                pick(one[:, :, 4:5], esel[:, :, :], hot[:, :, 8:12])
                dve.tensor_tensor(one[:, :, 6:7], one[:, :, 4:5], one[:, :, 3:4], ALU.subtract)\
                    .then_inc(f["weighted"].sem, 1)
                dve.wait_ge(f["exped"].sem, f["exped"].value(2))
                step(dve.tensor_scalar(one[:, :, 5:6], one[:, :, 6:7], 1.0, None, ALU.add))
                step(dve.reciprocal(one[:, :, 7:8], one[:, :, 5:6]))
                step(dve.tensor_tensor(one[:, :, 5:6], one[:, :, 7:8], one[:, :, 2:3], ALU.mult))
                step(dve.tensor_tensor(one[:, :, 6:7], one[:, :, 6:7], one[:, :, 5:6], ALU.mult))
                step(dve.tensor_tensor(tmp4[:, :, :], hot[:, :, 4:8], over(one[:, :, 5:6], 4), ALU.mult))
                step(dve.tensor_tensor(esel[:, :, :], hot[:, :, 8:12], over(one[:, :, 6:7], 4), ALU.mult))
                step(dve.tensor_tensor(esel[:, :, :], esel[:, :, :], tmp4[:, :, :], ALU.add))
                for g in range(4):
                    last = dve.tensor_tensor(comb[:, :, 4 * g:4 * g + 4], esel[:, :, :],
                                             over(hot[:, :, g:g + 1], 4), ALU.mult)
                last.then_inc(f["made"].sem, 1)
                dve.wait_ge(f["turned"].sem, f["turned"].value(1))
                dve.tensor_copy(combT[:, :], core.psum[0:16, 1:3, :].rearrange("p a b -> p (a b)")[:, 0:tokens])\
                    .then_inc(f["made"].sem, 1)

            @block.scalar
            def _(act):
                act.wait_ge(f["weighted"].sem, f["weighted"].value(1))
                act.activation(tmp4[:, :, :], tmp4[:, :, :], ACT.Exp).then_inc(f["exped"].sem, 1)
                act.wait_ge(f["weighted"].sem, f["weighted"].value(2))
                act.activation(one[:, :, 6:7], one[:, :, 6:7], ACT.Exp).then_inc(f["exped"].sem, 1)

            @block.sync
            def _(sp):
                sp.wait_ge(f["made"].sem, f["made"].value(2))
                sp.dma_start(comb_dram[:, 0:tokens], combT[:, :]).then_inc(f["stored"].sem, 16)
                sp.wait_ge(f["stored"].sem, f["stored"].value(16))
    for k, n in (("products_done", 1), ("made", 2), ("turned", 1), ("weighted", 2), ("exped", 2), ("stored", 16)):
        f[k].advance(n)


def experts(core, l, parts):
    nc, f, dram = core.nc, core.flags, core.dram
    tokens = sum(tn for _, tn in parts)
    comb_dram = dram["comb"]
    route(core, l, tokens, comb_dram)
    c0 = core.plan[f"gu{l}_0"][0]
    assert c0 == core.consumed
    per_expert = [(ft, p) for ft in range(2) for p in range(len(parts))]
    NU = len(per_expert)
    ND = KD * len(parts)
    ROUNDS = N_EXP // 2
    HELD, ADDS = 2, 4

    with ExitStack() as stack:
        def sb(name, shape):
            return stack.enter_context(nc.sbuf_tensor(f"{name}{l}", shape, F32))
        F = sb("ffn_sum", [P, KD, tokens])
        HID = sb("hid", [P, 2, 2, tokens])
        CB = sb("comb_rows", [P, 2, tokens])
        SL = sb("silu_a", [P, 2, 512])
        TM = sb("up_comb", [P, 2, 512])
        comb_flags = [f["comb_loaded"], f["comb_loaded1"]]

        def slot(k, kt, n):
            return core.ring[:, (c0 + k) % RING, 0:kt * n].rearrange("p (k n) -> p k n", k=kt)

        def used_in_round(k):
            if k < 2:
                return f["products_done"], 2 * NU, f["products_done"].value(NU * (k + 1))
            return f["down_done"], 2 * ND, f["down_done"].value(ND * (k - 1))

        for i in range(ROUNDS):
            for k in range(4):
                flag, per_round, value = used_in_round(k)
                core.used_up[c0 + 4 * i + k] = (flag, i * per_round + value)

        def comb_row(e):
            return comb_dram[bass.ds(e, 1), 0:tokens].broadcast_to([P, tokens])

        with nc.Block(f"experts{l}") as block:
            @block.sync
            def _(sp):
                for e in range(2):
                    sp.dma_start(CB[:, e, :], comb_dram[e:e + 1, 0:tokens].broadcast_to([P, tokens]))\
                        .then_inc(comb_flags[e].sem, 16)
                with sp.Fori(1, ROUNDS) as i:
                    for k, e in ((0, 0), (1, 1), (2, None), (3, None)):
                        width = 4096 if e is not None else 2048
                        flag, per_round, value = used_in_round(k)
                        sp.wait_ge(flag.sem, (i - 1) * per_round + value)
                        sp.dma_start(core.ring[:, (c0 + k) % RING, 0:width],
                                     dram["weights"][bass.ds(i * 4 + (c0 + k), 1), :, 0:width]
                                     .rearrange("c p n -> p (c n)")).then_inc(core.w_loaded[(c0 + k) % RING].sem, 16)
                        if e is not None:
                            sp.wait_ge(f["hid_ready"].sem, i * (2 * NU) + f["hid_ready"].value(HELD - 2 * NU + NU * (e + 1)))
                            sp.dma_start(CB[:, e, :], comb_row(i * 2 + e)).then_inc(comb_flags[e].sem, 16)
                core.issued = c0 + 4 * ROUNDS
                core.feed(sp, c0 + 4 * ROUNDS)

            @block.tensor
            def _(pe):
                with pe.Fori(0, ROUNDS) as i:
                    for e in range(2):
                        pe.wait_ge(core.w_loaded[(c0 + e) % RING].sem, i * 16 + 16 * ((c0 + e) // RING + 1))
                        w = slot(e, KD, 512)
                        for n, (ft, p) in enumerate(per_expert):
                            t0, tn = parts[p]
                            u = e * NU + n
                            pe.wait_ge(f["hid_ready"].sem, i * (2 * NU) + f["hid_ready"].value(HELD + u - 1))
                            for half in range(2):
                                last = products(pe, core.bank(2 * (u % 2) + half, P, tn),
                                                [(w[:, k, 256 * half + ft * P:256 * half + (ft + 1) * P],
                                                  core.H[:, k, t0:t0 + tn]) for k in range(KD)])
                            last.then_inc(f["products_done"].sem, 1)
                    for e in range(2):
                        pe.wait_ge(core.w_loaded[(c0 + 2 + e) % RING].sem, i * 16 + 16 * ((c0 + 2 + e) // RING + 1))
                        pe.wait_ge(f["hid_ready"].sem, i * (2 * NU) + f["hid_ready"].value(HELD + NU * (e + 1)))
                        w = slot(2 + e, 2, 1024)
                        for n in range(ND):
                            p, m = n // KD, n % KD
                            t0, tn = parts[p]
                            q = e * ND + n
                            pe.wait_ge(f["added"].sem, i * (2 * ND) + f["added"].value(ADDS + q - 3))
                            last = products(pe, core.bank(4 + q % 4, P, tn),
                                            [(w[:, ft, m * P:(m + 1) * P], HID[:, e, ft, t0:t0 + tn]) for ft in range(2)])
                            last.then_inc(f["down_done"].sem, 1)

            @block.scalar
            def _(act):
                with act.Fori(0, ROUNDS) as i:
                    for u in range(2 * NU):
                        tn = parts[per_expert[u % NU][1]][1]
                        act.wait_ge(f["products_done"].sem, i * (2 * NU) + f["products_done"].value(u + 1))
                        act.activation(SL[:, u % 2, 0:tn], core.bank(2 * (u % 2), P, tn), ACT.Silu)\
                            .then_inc(f["silued"].sem, 1)

            @block.vector
            def _(dve):
                for k in range(KD):
                    ins = dve.memset(F[:, k, :], 0.0)
                    if k < ADDS:
                        ins.then_inc(f["added"].sem, 1)
                    elif k < ADDS + HELD:
                        ins.then_inc(f["hid_ready"].sem, 1)
                with dve.Fori(0, ROUNDS) as i:
                    for e in range(2):
                        dve.wait_ge(comb_flags[e].sem, i * 16 + comb_flags[e].value(16))
                        for n, (ft, p) in enumerate(per_expert):
                            t0, tn = parts[p]
                            u = e * NU + n
                            dve.wait_ge(f["products_done"].sem, i * (2 * NU) + f["products_done"].value(u + 1))
                            dve.tensor_tensor(TM[:, u % 2, 0:tn], CB[:, e, t0:t0 + tn],
                                              core.bank(2 * (u % 2) + 1, P, tn), ALU.mult).then_inc(f["gated"].sem, 1)
                            dve.wait_ge(f["silued"].sem, i * (2 * NU) + f["silued"].value(u + 1))
                            dve.wait_ge(f["gated"].sem, i * (2 * NU) + f["gated"].value(u + 1))
                            dve.tensor_tensor(HID[:, e, ft, t0:t0 + tn], TM[:, u % 2, 0:tn], SL[:, u % 2, 0:tn],
                                              ALU.mult).then_inc(f["hid_ready"].sem, 1)
                    for q in range(2 * ND):
                        p, m = (q % ND) // KD, q % KD
                        t0, tn = parts[p]
                        dve.wait_ge(f["down_done"].sem, i * (2 * ND) + f["down_done"].value(q + 1))
                        dve.tensor_tensor(F[:, m, t0:t0 + tn], F[:, m, t0:t0 + tn], core.bank(4 + q % 4, P, tn),
                                          ALU.add).then_inc(f["added"].sem, 1)
                dve.wait_ge(f["added"].sem, f["added"].value(ADDS + 2 * ND * ROUNDS))
                for p, (t0, tn) in enumerate(parts):
                    for m in range(KD):
                        dve.scalar_tensor_tensor(out=core.X[:, m, t0:t0 + tn], in0=F[:, m, t0:t0 + tn],
                                                 scalar=core.mods[:, l, 40 + m, p:p + 1],
                                                 in1=core.X[:, m, t0:t0 + tn], op0=ALU.mult, op1=ALU.add)
    core.consumed = c0 + 4 * ROUNDS
    f["hid_ready"].advance(HELD + 2 * NU * ROUNDS)
    f["added"].advance(ADDS + 2 * ND * ROUNDS)
    f["down_done"].advance(2 * ND * ROUNDS)
    for k in ("products_done", "silued", "gated"):
        f[k].advance(2 * NU * ROUNDS)
    for c in comb_flags:
        c.advance(16 * ROUNDS)


def store(core):
    nc, f, dram = core.nc, core.flags, core.dram
    with nc.Block("store") as block:
        @block.sync
        def _(sp):
            sp.dma_start(dram["outT"].rearrange("(k p) t -> p k t", p=P), core.X[:, :, 0:S]).then_inc(f["out_stored"].sem, 16)
            sp.wait_ge(f["out_stored"].sem, 16)


def build_program(nc, dram, stages=99):
    with ExitStack() as ctx:
        core = Core(nc, ctx, dram)
        parts = [LAT, CON]

        def mix_ffn(l, tokens_of):
            modulated_norm(core, f"norm_f{l}", l, 1, tokens_of)
            experts(core, l, tokens_of)

        def first():
            with nc.sbuf_tensor("table_ac", [12, TABLE], F32) as core.table_ac, \
                 nc.sbuf_tensor("table_b", [8, TABLE], F32) as core.table_b:
                derive(core)
                first_block(core)
        program = [lambda: load_inputs(core), first,
                   lambda: modulation(core), lambda: even_layer(core), lambda: mix_ffn(0, parts),
                   lambda: odd_layer(core), lambda: mix_ffn(1, [LAT]), lambda: store(core)]
        for stage in program[0:stages]:
            stage()


def shape_constants():
    con = {}
    con["ident"] = np.eye(P)
    con["ones"] = np.ones((P, P))
    con["blocks"] = np.kron(np.eye(2), np.ones((HD, HD)))
    rot = np.zeros((P, P))
    for b in range(0, P, 32):
        for d in range(16):
            rot[b + 16 + d, b + d] = -1.0
            rot[b + d, b + 16 + d] = 1.0
    con["rot"] = rot
    s, t = np.arange(P)[:, None], np.arange(P)[None, :]
    con["causal_st"] = s <= t
    con["anti_st"] = s >= t
    pos = np.arange(S)
    ends = np.arange(NC_CMP) * 16 + 31
    con["cmask"] = np.where(ends[None, :] <= pos[:, None], 0.0, NEG).reshape(4, P, NC_CMP).transpose(1, 0, 2)\
        .reshape(P, -1)
    packed = np.concatenate([np.asarray(con[n], np.float32).reshape(P, -1) for n, _ in CONSTS], 1)
    n = np.maximum(511 - np.arange(TABLE), 0)
    large = 16 + (np.log(np.maximum(n, 1).astype(np.float32) / np.float32(16)) / np.float32(math.log(128 / 16))
                  * np.float32(16)).astype(np.int32)
    bucket = np.where(n < 16, n, np.minimum(large, 31))
    onehot = (bucket[None, :] == np.arange(32)[:, None]).astype(np.float32)
    row, col = np.arange(S) // 64, np.arange(S) % 64
    inv = np.float32(10000.0) ** (-np.arange(0, 32, 2, dtype=np.float32) / np.float32(32))
    ang = np.stack([row[:, None].astype(np.float32) * inv, col[:, None].astype(np.float32) * inv], 1)
    ang = np.tile(np.repeat(ang[:, :, None, :], 2, 2).reshape(S, HD).T, (2, 1))
    trig = np.stack([np.cos(ang), np.sin(ang)], 1).astype(np.float32)
    near_before = np.where(t >= s, 0.0, NEG)
    near_behind = np.where(t <= s, 0.0, NEG)
    zero = np.zeros((P, P))
    window = np.concatenate([zero, zero, near_before, zero, near_behind, zero, zero, zero, near_behind], 1)
    return packed, onehot, trig, window.astype(np.float32)


def pairs(w, heads, axis):
    order = np.arange(heads).reshape(2, heads // 2).T.reshape(-1)
    w = np.moveaxis(np.asarray(w), axis, -1)
    w = w.reshape(w.shape[:-1] + (heads, HD))[..., order, :].reshape(w.shape)
    return np.moveaxis(w, -1, axis)


def laid_out(a):
    D1 = {k: np.asarray(v) for k, v in a.items()}
    w = D1["w_in"][0]
    sizes = [512, 512, 512, 512, 128, 128, 512, 768, 24, 3072]
    at = np.concatenate([[0], np.cumsum(sizes)])
    aq, ak, av, bq, bk, bv, cq, ckv, cg, mg = (w[:, at[i]:at[i + 1]] for i in range(10))
    kv = [ckv[:, 128 * i:128 * i + 128] for i in range(6)]
    ev = D1["ev_w_in_2"][0]
    at = np.concatenate([[0], np.cumsum([256, 256, 512, 512, 32, 512, 128, 128])])
    gq, gk, gv, gr, lr, eq, ek, evv = (ev[:, at[i]:at[i + 1]] for i in range(8))
    od = D1["od_w_in_2"][0]
    ev_out = D1["ev_w_out_2"][0]
    ev_out = np.concatenate([ev_out[0:512], pairs(ev_out[512:1024], 8, 0)], 0)
    od_out = pairs(D1["od_w_out_2"][0], 16, 0)
    odq = pairs(od[:, 0:1024], 16, 1)
    wb = D1["w_branch"][0]
    wb = [wb[0], pairs(wb[1], 8, 0), pairs(wb[2], 8, 0)]
    src = {"proj0": aq, "proj1": ak, "proj2": pairs(bq, 8, 1), "proj3": pairs(cq, 8, 1),
           "proj4": np.concatenate([bk, kv[2], kv[4], kv[0]], 1), "proj5": np.concatenate([kv[1], bv, kv[3], kv[5]], 1),
           "proj6": av, "proj7": cg, "cmp0": D1["cmp_w1"][0, 0], "cmp1": D1["cmp_w1"][0, 1],
           "ev0": pairs(eq, 8, 1), "ev1": np.concatenate([ek, evv, lr], 1), "ev2": np.concatenate([gq, gk], 1),
           "ev3": gr, "ev4": gv, "od0": odq[:, 0:512], "od1": odq[:, 512:1024], "od2": od[:, 1024:1280]}
    for n in range(3):
        src[f"branch{n}"] = wb[n]
        for h in range(2):
            src[f"mg{n}_{h}"] = mg[:, 1024 * n + 512 * h:1024 * n + 512 * h + 512]
    for i in range(2):
        c = slice(512 * i, 512 * i + 512)
        src[f"out{i}"], src[f"ev_out{i}"], src[f"od_out{i}"] = D1["w_out"][0][:, c], ev_out[:, c], od_out[:, c]
    for i in range(8):
        src[f"up{i}"] = D1["w_up"][0][:, 512 * i:512 * i + 512]
        src[f"down{i}"] = D1["w_down"][0][:, P * i:P * i + P]
    for l in range(2):
        for i in range(12):
            src[f"mod{l}_{i}"] = D1["mod_w_2"][l][:, 512 * i:512 * i + 512]
        gate, up, down = (D1[n][l].reshape((N_EXP,) + D1[n].shape[3:]) for n in
                          ("exp_w_gate_2", "exp_w_up_2", "exp_w_down_2"))
        for e in range(N_EXP):
            src[f"gu{l}_{e}"] = np.concatenate([gate[e], up[e]], 1)
            src[f"dn{l}_{e}"] = down[e]
    plan = plan_weights()
    weights = np.zeros((len(plan), P, 4096), np.float32)
    for c, (name, kt, n) in enumerate(plan):
        weights[c, :, 0:kt * n] = src[name].reshape(kt, P, n).transpose(1, 0, 2).reshape(P, kt * n)

    def column(v):
        return v.reshape(-1, P).T

    def twice(v):
        return np.tile(v, 2)[:, None]

    def rows(v):
        return np.tile(v.reshape(1, -1), (P, 1))

    lam = np.zeros((P, 4), np.float32)
    lam[0:HD] = D1["diff_lambda"][0].T
    par = {
        "norm_mix": column(D1["norm_mix"][0]), "norm_mlp": column(D1["norm_mlp"][0]),
        "qk_gain": np.concatenate([twice(D1["qk_gain"][0, i]) for i in range(8)], 1),
        "subln": D1["diff_subln"][0][:, None], "mod_b": column(D1["mod_b_2"].reshape(-1)),
        "norm_mix_2": column(D1["norm_mix_2"].reshape(-1)), "norm_ffn_2": column(D1["norm_ffn_2"].reshape(-1)),
        "gla_b": column(D1["gla_gate_b_2"][0].reshape(-1)), "gla_norm": D1["gla_out_norm_2"][0][:, None],
        "att_q": twice(D1["att_q_norm_2"][0]), "att_k": twice(D1["att_k_norm_2"][0]),
        "swa_q": twice(D1["swa_q_norm_2"][0]), "swa_k": twice(D1["swa_k_norm_2"][0]),
        "c": np.stack([column(D1["c_2"][0]), column(D1["c_ctx_2"])], 2).reshape(P, 16),
        "sinks": rows(D1["sinks"][0]), "swa_sink": rows(D1["swa_sink_2"][0]),
        "router_b": rows(np.concatenate([D1["router_group_b_2"], D1["router_expert_b_2"]], 1)),
        "cmp_pos": D1["cmp_pos"][0].reshape(2, 16, P).transpose(2, 0, 1).reshape(P, 32),
        "lambda": lam, "valid31": (np.arange(P) >= 31)[:, None].astype(np.float32),
    }
    router = np.concatenate([D1["router_group_w_2"], D1["router_expert_w_2"]], 2)
    gate_w = np.zeros((32, 2, 256), np.float32)
    for z in range(2):
        gate_w[16 * z:16 * z + 16, z] = D1["gla_gate_w_2"][0, z]
    rel = D1["rel_bias"]
    packed, onehot, trig, window = shape_constants()
    return {
        "xT": D1["x"][0].T, "ctxT": D1["ctx_2"][0].T, "weights": weights,
        "par": np.concatenate([par[n].reshape(P, -1) for n, _ in PARAMS], 1), "con": packed,
        "router": router.reshape(2, KD, P, 20).transpose(2, 0, 1, 3), "gate_w": gate_w,
        "rel": np.concatenate([rel[:, 0:4], rel[:, 12:20], rel[:, 4:12]], 1), "onehot": onehot,
        "trig": trig, "window": window, "cmp_w2": D1["cmp_w2"][0],
    }


def kernel(**inputs):
    import concourse.bacc as _bacc
    from concourse.bass_utils import run_bass_kernel_spmd as _run

    nc = _bacc.Bacc("TRN2", target_bir_lowering=False, num_devices=1)
    arrays, dram = {}, {}
    for name, a in laid_out(inputs).items():
        a = np.ascontiguousarray(a)
        arrays[f"in_{name}"] = a
        dram[name] = nc.dram_tensor(f"in_{name}", a.shape, mybir.dt.from_np(a.dtype), kind="ExternalInput").ap()
    dram["bias"] = nc.dram_tensor("bias_tables", [20, P, TABLE], F32, kind="Internal").ap()
    dram["comb"] = nc.dram_tensor("combine", [N_EXP, T], F32, kind="Internal").ap()
    dram["outT"] = nc.dram_tensor("outT", [D, S], F32, kind="ExternalOutput").ap()
    build_program(nc, dram)
    r = _run(nc, [arrays], core_ids=[0])
    return np.ascontiguousarray(r.results[0]["outT"].T)[None]
```

```python
import math
from contextlib import ExitStack

import numpy as np
import concourse.bass as bass
from concourse import mybir

P = 128
D = 1024
KD = D // P
S = 512
CTX = 256
T = S + CTX
HD = 64
D_FF = 4096
EPS = 1e-6
NEG = -1e30
LAM_INIT = 0.8 - 0.6 * math.exp(-0.3 * 0)
NC_CMP = (S - 32) // 16 + 1
TABLE = 640
MASKED_FROM = 512
WINDOW_B = 128
N_EXP = 16
RING = 4
LAT = (0, S)
CON = (S, CTX)

F32 = mybir.dt.float32
U32 = mybir.dt.uint32
I32 = mybir.dt.int32
ALU = mybir.AluOpType
ACT = mybir.ActivationFunctionType
AX = mybir.AxisListType

PARAMS = [("norm_mix", 8), ("norm_mlp", 8), ("qk_gain", 8), ("subln", 1), ("mod_b", 2 * 48), ("norm_mix_2", 16),
          ("norm_ffn_2", 16), ("gla_b", 4), ("gla_norm", 1), ("att_q", 1), ("att_k", 1), ("swa_q", 1), ("swa_k", 1),
          ("c", 16), ("sinks", 8), ("swa_sink", 16), ("router_b", 2 * 20), ("cmp_pos", 32), ("lambda", 4),
          ("valid31", 1)]
CONSTS = [("ident", P), ("ones", P), ("blocks", P), ("rot", P), ("causal_st", P), ("anti_st", P), ("cmask", 4 * NC_CMP),
          ("token_no", T // P), ("tile_no", 32)]


def offsets(spec):
    at, out = 0, {}
    for name, width in spec:
        out[name] = (at, at + width)
        at += width
    return out, at


PARAM_AT, N_PARAM = offsets(PARAMS)
CONST_AT, N_CONST = offsets(CONSTS)


class Flag:

    def __init__(self, nc, name):
        self.sem = nc.alloc_semaphore(name)
        self.base = 0

    def value(self, n):
        return self.base + n

    def advance(self, n):
        self.base += n


class Chain:

    def __init__(self, flag):
        self.flag = flag

    def __call__(self, eng, ins):
        ins.then_inc(self.flag.sem, 1)
        self.flag.advance(1)
        eng.wait_ge(self.flag.sem, self.flag.base)


class Core:

    def __init__(self, nc, ctx, dram):
        self.nc = nc
        self.ctx = ctx
        self.dram = dram
        sb = self.sb
        self.X = sb("X", [P, KD, T])
        self.H = sb("H", [P, KD, T])
        self.ring = sb("ring", [P, RING, 4096])
        self.par = sb("par", [P, N_PARAM])
        self.con = sb("con", [P, N_CONST])
        self.eps = sb("eps", [P, 1])
        self.mods = sb("mods", [P, 2, 48, 2])
        self.mod_gain = sb("mod_gain", [P, 2, 2, KD, 2])
        self.silu_c = sb("silu_c", [P, 16])
        self.derived = sb("derived", [P, N_DERIVED])
        self.router = sb("router", [P, 2, KD, 20])
        self.psum = ctx.enter_context(nc.psum_tensor("banks", [P, 8, 512], F32))
        self.flags = {}
        for name in ("products_done", "evacuated_v", "evacuated_s", "squared", "summed", "rooted", "normed",
                     "scored", "biased", "exped", "weighted", "turned", "copied", "attended", "emptied",
                     "v_step", "s_step", "p_step", "misc_loaded", "bias_loaded0", "bias_loaded1", "hid_ready", "gated", "silued",
                     "down_done", "added", "out_stored", "stored", "made", "tables_stored",
                     "rows_turned", "rows_stored0", "rows_stored1", "scattered", "turned_v", "turned_s", "gate_up",
                     "hid_turned", "hidT_ready", "y_v", "y_s", "pair00", "pair01", "pair10", "pair11",
                     *(f"{name}{u}" for name in ("gu_loaded", "dn_loaded", "idx_loaded", "gathered", "y_stored")
                       for u in range(3))):
            self.flags[name] = Flag(nc, name)
        self.w_loaded = [Flag(nc, f"w_loaded{i}") for i in range(RING)]
        self.v_chain, self.s_chain, self.p_chain = (Chain(self.flags[n]) for n in ("v_step", "s_step", "p_step"))
        self.plan_list = plan_weights()
        self.plan = {name: (c, kt, n) for c, (name, kt, n) in enumerate(self.plan_list)}
        self.issued = 0
        self.used_up = {}
        self.consumed = 0

    def sb(self, name, shape):
        return self.ctx.enter_context(self.nc.sbuf_tensor(name, shape, F32))

    def bank(self, n, rows=P, cols=512, at=0):
        return self.psum[0:rows, n, at:at + cols]

    def param(self, name, a=0, n=None, rows=P):
        lo, hi = PARAM_AT[name]
        return self.par[0:rows, lo + a:hi if n is None else lo + a + n]

    def const(self, name, rows=P, at=0):
        lo, hi = CONST_AT[name]
        return self.con[at:at + rows, lo:hi]

    def chunk(self, name):
        c, kt, n = self.plan[name]
        return c, self.ring[:, c % RING, 0:kt * n].rearrange("p (k n) -> p k n", k=kt)

    def feed(self, sync, consumed):
        while self.issued < min(consumed + RING, len(self.plan_list)):
            c = self.issued
            _, kt, n = self.plan_list[c]
            if c >= RING:
                flag, value = self.used_up[c - RING]
                sync.wait_ge(flag.sem, value)
            sync.dma_start(self.ring[:, c % RING, 0:kt * n], self.dram["weights"][c, :, 0:kt * n])\
                .then_inc(self.w_loaded[c % RING].sem, 16)
            self.issued += 1

    def use_up(self, jobs):
        done = self.flags["products_done"]
        for n, job in enumerate(jobs):
            if job[1]:
                self.used_up[job[0]] = (done, done.value(n + 1))
        return self.consumed + sum(1 for j in jobs if j[1])

    def await_chunk(self, pe, c):
        pe.wait_ge(self.w_loaded[c % RING].sem, 16 * (c // RING + 1))


def products(pe, out, pairs):
    for n, (lhsT, rhs) in enumerate(pairs):
        last = pe.matmul(out, lhsT, rhs, start=n == 0, stop=n == len(pairs) - 1)
    return last


def dense(core, name, jobs, finish, both=True):
    nc, f = core.nc, core.flags
    lanes = 2 if both else 1
    used = core.use_up(jobs)

    with nc.Block(name) as block:
        @block.sync
        def _(sp):
            core.feed(sp, used)

        @block.tensor
        def _(pe):
            seen = None
            for n, (chunk, release, rows, cols, pairs) in enumerate(jobs):
                if chunk is not None and chunk != seen:
                    core.await_chunk(pe, chunk)
                    seen = chunk
                if n >= 8:
                    flag = f["evacuated_s"] if both and n % 2 else f["evacuated_v"]
                    pe.wait_ge(flag.sem, flag.value((n - 8) // lanes + 1))
                last = products(pe, core.bank(n % 8, rows, cols), pairs)
                last.then_inc(f["products_done"].sem, 1)

        @block.vector
        def _(dve):
            for n in range(0, len(jobs), lanes):
                dve.wait_ge(f["products_done"].sem, f["products_done"].value(n + 1))
                finish(dve, n, core.bank(n % 8, jobs[n][2], jobs[n][3])).then_inc(f["evacuated_v"].sem, 1)

        if both:
            @block.scalar
            def _(act):
                for n in range(1, len(jobs), 2):
                    act.wait_ge(f["products_done"].sem, f["products_done"].value(n + 1))
                    finish(act, n, core.bank(n % 8, jobs[n][2], jobs[n][3])).then_inc(f["evacuated_s"].sem, 1)

    f["products_done"].advance(len(jobs))
    f["evacuated_v"].advance((len(jobs) + lanes - 1) // lanes)
    f["evacuated_s"].advance(len(jobs) // 2 if both else 0)
    core.consumed = used


def copy_out(core, dst):
    def finish(eng, n, ps):
        if eng is core.nc.scalar:
            return eng.activation(dst(n), ps, ACT.Copy)
        return eng.tensor_copy(dst(n), ps)
    return finish


def head_normed(core, name, jobs, scratch, dest, gain, group, const, sources=None):
    nc, f = core.nc, core.flags
    squares, roots = scratch

    def tile(n):
        return sources[n] if sources else core.bank(n % 3, P, jobs[n][3])

    used = core.use_up(jobs)
    N = len(jobs)

    with nc.Block(name) as block:
        @block.sync
        def _(sp):
            core.feed(sp, used)

        @block.tensor
        def _(pe):
            seen = None
            for n in range(N + 1):
                if n < N and not sources:
                    chunk, release, rows, cols, pairs = jobs[n]
                    if chunk is not None and chunk != seen:
                        core.await_chunk(pe, chunk)
                        seen = chunk
                    if n >= 3:
                        pe.wait_ge(f["normed"].sem, f["normed"].value(n - 2))
                    last = products(pe, core.bank(n % 3, rows, cols), pairs)
                    last.then_inc(f["products_done"].sem, 1)
                if n >= 1:
                    m = n - 1
                    cols = jobs[m][3]
                    pe.wait_ge(f["squared"].sem, f["squared"].value(m + 1))
                    if m >= 2:
                        pe.wait_ge(f["rooted"].sem, f["rooted"].value(m - 1))
                    pe.matmul(core.bank(3 + m % 2, P, cols), const, squares[:, m % 2, 0:cols], start=True,
                              stop=True).then_inc(f["summed"].sem, 1)

        @block.scalar
        def _(act):
            for n in range(N + 1):
                if n < N:
                    cols = jobs[n][3]
                    if not sources:
                        act.wait_ge(f["products_done"].sem, f["products_done"].value(n + 1))
                    if n >= 2:
                        act.wait_ge(f["summed"].sem, f["summed"].value(n - 1))
                    act.activation(squares[:, n % 2, 0:cols], tile(n), ACT.Square)\
                        .then_inc(f["squared"].sem, 1)
                if n >= 1:
                    m = n - 1
                    cols = jobs[m][3]
                    act.wait_ge(f["summed"].sem, f["summed"].value(m + 1))
                    if m >= 2:
                        act.wait_ge(f["normed"].sem, f["normed"].value(m - 1))
                    r = roots[:, m % 2, 0:cols]
                    core.s_chain(act, act.activation(r, core.bank(3 + m % 2, P, cols), ACT.Ln,
                                                     bias=core.eps[:, 0:1], scale=1.0 / group))
                    act.activation(r, r, ACT.Exp, scale=-0.5).then_inc(f["rooted"].sem, 1)

        @block.vector
        def _(dve):
            for n in range(N):
                cols = jobs[n][3]
                dve.wait_ge(f["rooted"].sem, f["rooted"].value(n + 1))
                dve.scalar_tensor_tensor(out=dest(n), in0=tile(n), scalar=gain(n),
                                         in1=roots[:, n % 2, 0:cols], op0=ALU.mult, op1=ALU.mult)\
                    .then_inc(f["normed"].sem, 1)

    if not sources:
        f["products_done"].advance(N)
    for k in ("squared", "summed", "rooted", "normed"):
        f[k].advance(N)
    core.consumed = used


def normalise(core, name, parts, scale, shift=None):
    nc, f = core.nc, core.flags
    with ExitStack() as stack:
        squares = stack.enter_context(nc.sbuf_tensor(name + "_squares", [P, 2, 512], F32))
        roots = stack.enter_context(nc.sbuf_tensor(name + "_roots", [P, T], F32))
        N = KD * len(parts)
        with nc.Block(name) as block:
            @block.sync
            def _(sp):
                core.feed(sp, core.consumed)

            @block.scalar
            def _(act):
                for n in range(N):
                    (t0, tn), k = parts[n // KD], n % KD
                    if n >= 2:
                        act.wait_ge(f["summed"].sem, f["summed"].value(n - 1))
                    act.activation(squares[:, n % 2, 0:tn], core.X[:, k, t0:t0 + tn], ACT.Square)\
                        .then_inc(f["squared"].sem, 1)
                    if k == KD - 1:
                        act.wait_ge(f["summed"].sem, f["summed"].value(n + 1))
                        r = roots[:, t0:t0 + tn]
                        core.s_chain(act, act.activation(r, core.bank(n // KD, P, tn), ACT.Ln,
                                                         bias=core.eps[:, 0:1], scale=1.0 / D))
                        act.activation(r, r, ACT.Exp, scale=-0.5).then_inc(f["rooted"].sem, 1)

            @block.tensor
            def _(pe):
                for n in range(N):
                    (t0, tn), k = parts[n // KD], n % KD
                    pe.wait_ge(f["squared"].sem, f["squared"].value(n + 1))
                    pe.matmul(core.bank(n // KD, P, tn), core.const("ones"), squares[:, n % 2, 0:tn],
                              start=k == 0, stop=k == KD - 1).then_inc(f["summed"].sem, 1)

            @block.vector
            def _(dve):
                for p, (t0, tn) in enumerate(parts):
                    dve.wait_ge(f["rooted"].sem, f["rooted"].value(p + 1))
                    for k in range(KD):
                        last = dve.scalar_tensor_tensor(out=core.H[:, k, t0:t0 + tn], in0=core.X[:, k, t0:t0 + tn],
                                                        scalar=scale(k, p), in1=roots[:, t0:t0 + tn],
                                                        op0=ALU.mult, op1=ALU.mult)
                    if shift is not None:
                        core.v_chain(dve, last)
                        for k in range(KD):
                            dve.tensor_scalar(core.H[:, k, t0:t0 + tn], core.H[:, k, t0:t0 + tn], shift(k, p),
                                              None, ALU.add)
        for k, v in (("squared", N), ("summed", N), ("rooted", len(parts))):
            f[k].advance(v)


def attention(core, name, units, bias_loads=()):
    nc, f = core.nc, core.flags
    U = len(units)
    widest = max(u["width"] for u in units) + 1
    SL = 3
    groups = []
    g = 0
    for u in units:
        mine = []
        for t in range(0, len(u["v"]), 4):
            mine.append((g, t, min(4, len(u["v"]) - t)))
            g += 1
        groups.append(mine)
    evacs = [n for n, u in enumerate(units) if u["evac"]]
    score = [core.psum[:, 2 * i:2 * i + 2, :].rearrange("p a b -> p (a b)") for i in range(2)]
    ident = core.const("ident")

    with ExitStack() as stack:
        probs = stack.enter_context(nc.sbuf_tensor(name + "_probs", [P, SL, widest], F32))
        turned = stack.enter_context(nc.sbuf_tensor(name + "_turned", [P, 3, 512], F32))
        stats = stack.enter_context(nc.sbuf_tensor(name + "_stats", [P, 4, 3], F32))

        def tile_keys(u, t):
            return min(P, u["width"] - t * P)

        with nc.Block(name) as block:
            @block.sync
            def _(sp):
                if bias_loads:
                    sp.wait_ge(f["tables_stored"].sem, 32)
                for n, (dst, src, after) in enumerate(bias_loads):
                    if after is not None:
                        sp.wait_ge(f["biased"].sem, f["biased"].value(after + 1))
                    sp.dma_start(dst, src).then_inc(f[f"bias_loaded{n % 2}"].sem, 16)
                core.feed(sp, core.consumed)

            @block.tensor
            def _(pe):
                def scores(n):
                    u = units[n]
                    if n >= 2:
                        pe.wait_ge(f["exped"].sem, f["exped"].value(n - 1))
                    at = 0
                    for k in u["k"]:
                        last = pe.matmul(score[n % 2][:, at:at + k.shape[1]], u["q"], k, start=True, stop=True)
                        at += k.shape[1]
                    last.then_inc(f["scored"].sem, 1)

                def transposes(n):
                    u = units[n]
                    pe.wait_ge(f["weighted"].sem, f["weighted"].value(n + 1))
                    for g, t0, nt in groups[n]:
                        if g >= 2:
                            pe.wait_ge(f["copied"].sem, f["copied"].value(g - 1))
                        for t in range(t0, t0 + nt):
                            w = tile_keys(u, t)
                            last = pe.transpose(core.bank(4 + g % 2, w, P, (t - t0) * P),
                                                probs[:, n % SL, t * P:t * P + w], ident)
                        last.then_inc(f["turned"].sem, 1)

                def values(n):
                    u = units[n]
                    if u["first"] and u["clears"] is not None:
                        pe.wait_ge(f["emptied"].sem, f["emptied"].value(u["clears"]))
                    for g, t0, nt in groups[n]:
                        pe.wait_ge(f["copied"].sem, f["copied"].value(g + 1))
                        for t in range(t0, t0 + nt):
                            w = tile_keys(u, t)
                            last = pe.matmul(core.bank(6 + u["bank"], P, P, u["col"]), u["v"][t],
                                             turned[0:w, g % 3, (t - t0) * P:(t - t0) * P + P],
                                             start=u["first"] and t == 0,
                                             stop=u["last"] and t == len(u["v"]) - 1)
                    last.then_inc(f["attended"].sem, 1)

                for n in range(U + 3):
                    if n < U:
                        scores(n)
                    if 2 <= n < U + 2:
                        transposes(n - 2)
                    if n >= 3:
                        values(n - 3)

            @block.vector
            def _(dve):
                def soften(n):
                    u = units[n]
                    w = u["width"]
                    dve.wait_ge(f["scored"].sem, f["scored"].value(n + 1))
                    if n >= SL:
                        dve.wait_ge(f["turned"].sem, f["turned"].value(groups[n - SL][-1][0] + 1))
                    if u["bias_load"] is not None:
                        b = f[f"bias_loaded{u['bias_load'] % 2}"]
                        dve.wait_ge(b.sem, b.value(16 * (u["bias_load"] // 2 + 1)))
                    row = score[n % 2][:, 0:w]
                    if u["sink"] is not None:
                        dve.tensor_copy(probs[:, n % SL, w:w + 1], u["sink"])
                    if u["bias"] is not None:
                        core.v_chain(dve, dve.tensor_tensor(probs[:, n % SL, 0:w], row, u["bias"], ALU.add))
                        row = probs[:, n % SL, 0:w + (u["sink"] is not None)]
                    dve.tensor_reduce(stats[:, n % 4, 0:1], row, AX.X, ALU.max, negate=True)\
                        .then_inc(f["biased"].sem, 1)

                def weigh(n):
                    u = units[n]
                    w = u["width"]
                    dve.wait_ge(f["exped"].sem, f["exped"].value(n + 1))
                    core.v_chain(dve, dve.reciprocal(stats[:, n % 4, 2:3], stats[:, n % 4, 1:2]))
                    dve.tensor_scalar(probs[:, n % SL, 0:w], probs[:, n % SL, 0:w], stats[:, n % 4, 2:3], u["coef"],
                                      ALU.mult, ALU.mult).then_inc(f["weighted"].sem, 1)

                def empty(n):
                    dst, rows = units[n]["evac"]
                    dve.wait_ge(f["attended"].sem, f["attended"].value(n + 1))
                    a, b = rows
                    dve.tensor_copy(dst, core.psum[a:b, 6 + units[n]["bank"], 0:dst.shape[-1]])\
                        .then_inc(f["emptied"].sem, 1)

                for n in range(U + 4):
                    if n >= 4 and units[n - 4]["evac"]:
                        empty(n - 4)
                    if n < U:
                        soften(n)
                    if 1 <= n <= U:
                        weigh(n - 1)

            @block.scalar
            def _(act):
                for n in range(U + 2):
                    if n < U:
                        u = units[n]
                        act.wait_ge(f["biased"].sem, f["biased"].value(n + 1))
                        w = u["width"] + (u["sink"] is not None)
                        row = probs[:, n % SL, 0:w] if u["bias"] is not None else score[n % 2][:, 0:w]
                        act.activation(probs[:, n % SL, 0:w], row, ACT.Exp, bias=stats[:, n % 4, 0:1],
                                       accum_out=stats[:, n % 4, 1:2]).then_inc(f["exped"].sem, 1)
                    if n >= 2:
                        for g, t0, nt in groups[n - 2]:
                            act.wait_ge(f["turned"].sem, f["turned"].value(g + 1))
                            if g >= 3:
                                owner = next(i for i, x in enumerate(groups) if any(y[0] == g - 3 for y in x))
                                act.wait_ge(f["attended"].sem, f["attended"].value(owner + 1))
                            w = tile_keys(units[n - 2], t0) if nt == 1 else P
                            act.activation(turned[0:w, g % 3, 0:nt * P], core.bank(4 + g % 2, w, nt * P),
                                           ACT.Copy).then_inc(f["copied"].sem, 1)

    for k in ("scored", "biased", "exped", "weighted", "attended"):
        f[k].advance(U)
    f["turned"].advance(g_total(groups))
    f["copied"].advance(g_total(groups))
    f["emptied"].advance(len(evacs))
    for i in range(2):
        f[f"bias_loaded{i}"].advance(16 * len(bias_loads[i::2]))


def g_total(groups):
    return sum(len(x) for x in groups)


def unit(q, k, v, bank, col, first=True, last=True, bias=None, bias_load=None, sink=None, coef=1.0, evac=None):
    return dict(q=q, k=k, width=sum(x.shape[1] for x in k), bias=bias, bias_load=bias_load, sink=sink, coef=coef,
                v=v, bank=bank, col=col, first=first, last=last, evac=evac, clears=None)


def plan_outputs(units):
    done = 0
    fresh = True
    for u in units:
        if fresh and done >= 2:
            u["clears"] = done - 1
        fresh = False
        if u["evac"]:
            done += 1
            fresh = True
    return units


def plan_weights():
    plan = [(f"proj{i}", KD, 512) for i in range(7)] + [("proj7", KD, 24), ("cmp0", 16, 256), ("cmp1", 16, 256)]
    for n in range(3):
        plan += [(f"mg{n}_0", KD, 512), (f"mg{n}_1", KD, 512), (f"branch{n}", 4, 1024)]
    plan += [(f"out{i}", KD, 512) for i in range(2)]
    plan += [(f"up{i}", KD, 512) for i in range(8)] + [(f"down{i}", 32, P) for i in range(8)]
    plan += [(f"mod{l}_{i}", KD, 512) for l in range(2) for i in range(12)]
    plan += [("ev0", KD, 512), ("ev1", KD, 288), ("ev2", KD, 512), ("ev3", KD, 512), ("ev4", KD, 512)]
    plan += [(f"ev_out{i}", KD, 512) for i in range(2)]
    plan += [("od0", KD, 512), ("od1", KD, 512), ("od2", KD, 256)]
    plan += [(f"od_out{i}", KD, 512) for i in range(2)]
    return plan


def load_inputs(core):
    nc, f, dram = core.nc, core.flags, core.dram
    x = dram["xT"].rearrange("(k p) t -> p k t", p=P)
    c = dram["ctxT"].rearrange("(k p) t -> p k t", p=P)
    with nc.Block("load") as block:
        @block.sync
        def _(sp):
            sp.dma_start(core.X[:, :, 0:S], x).then_inc(f["misc_loaded"].sem, 16)
            sp.dma_start(core.con[:, :], dram["con"]).then_inc(f["misc_loaded"].sem, 16)
            core.feed(sp, 0)

        @block.scalar
        def _(act):
            act.dma_start(core.par[:, :], dram["par"]).then_inc(f["misc_loaded"].sem, 16)
            act.dma_start(core.X[:, :, S:T], c).then_inc(f["misc_loaded"].sem, 16)
            act.dma_start(core.router[:, :, :, :], dram["router"]).then_inc(f["misc_loaded"].sem, 16)
            act.wait_ge(f["misc_loaded"].sem, 80)

        @block.vector
        def _(dve):
            dve.memset(core.eps[:, :], EPS)
    f["misc_loaded"].advance(80)


NEG_LAM, SUBLN, AQ_G, BQ_G, CQ_G, ATT_G, SWA_G, N_DERIVED = range(8)


def derive(core):
    nc, f, dram = core.nc, core.flags, core.dram
    scale = HD ** -0.5
    par = core.param
    der = core.derived
    with ExitStack() as stack:
        def sb(name, shape):
            return stack.enter_context(nc.sbuf_tensor(name, shape, F32))
        prod = sb("lam_products", [P, 2])
        exps = sb("lam_exps", [P, 2])
        sig = sb("c_sigmoid", [P, 16])
        onehot = sb("onehot", [32, TABLE])
        rel = sb("rel", [32, 20])
        table_ac, table_b = core.table_ac, core.table_b
        with nc.Block("derive") as block:
            @block.sync
            def _(sp):
                sp.dma_start(onehot[:, :], dram["onehot"]).then_inc(f["misc_loaded"].sem, 16)
                sp.dma_start(rel[:, :], dram["rel"]).then_inc(f["misc_loaded"].sem, 16)
                sp.wait_ge(f["made"].sem, f["made"].value(1))
                for lo, table in ((0, table_ac), (12, table_b)):
                    n = table.shape[0]
                    sp.dma_start(dram["bias"][lo:lo + n], table[:, :].rearrange("h (o t) -> h o t", o=1)
                                 .broadcast_to([n, P, TABLE])).then_inc(f["tables_stored"].sem, 16)

            @block.vector
            def _(dve):
                lam = par("lambda")
                dve.tensor_tensor(prod[:, 0:1], lam[:, 0:1], lam[:, 1:2], ALU.mult)
                dve.tensor_tensor(prod[:, 1:2], lam[:, 2:3], lam[:, 3:4], ALU.mult).then_inc(f["squared"].sem, 1)
                dve.tensor_scalar(der[:, SUBLN:SUBLN + 1], par("subln"), 1.0 - LAM_INIT, None, ALU.mult)
                for at, src in ((AQ_G, par("qk_gain", 0, 1)), (BQ_G, par("qk_gain", 2, 1)),
                                (CQ_G, par("qk_gain", 4, 1)), (ATT_G, par("att_q")), (SWA_G, par("swa_q"))):
                    dve.tensor_scalar(der[:, at:at + 1], src, scale, None, ALU.mult)
                dve.wait_ge(f["exped"].sem, f["exped"].value(1))
                dve.scalar_tensor_tensor(out=der[:, NEG_LAM:NEG_LAM + 1], in0=exps[:, 1:2], scalar=LAM_INIT,
                                         in1=exps[:, 0:1], op0=ALU.subtract, op1=ALU.subtract)
                dve.wait_ge(f["silued"].sem, f["silued"].value(1))
                dve.tensor_tensor(core.silu_c[:, :], par("c"), sig[:, :], ALU.mult)
                dve.wait_ge(f["products_done"].sem, f["products_done"].value(1))
                dve.tensor_copy(table_ac[:, :], core.psum[0:12, 0:2, :].rearrange("p a b -> p (a b)")[:, 0:TABLE])
                core.v_chain(dve, dve.tensor_copy(
                    table_b[:, :], core.psum[0:8, 2:4, :].rearrange("p a b -> p (a b)")[:, 0:TABLE]))
                dve.memset(table_ac[:, MASKED_FROM:TABLE], NEG)
                dve.memset(table_b[:, 0:S - WINDOW_B], NEG)
                dve.memset(table_b[:, MASKED_FROM:TABLE], NEG).then_inc(f["made"].sem, 1)

            @block.tensor
            def _(pe):
                pe.wait_ge(f["squared"].sem, f["squared"].value(1))
                pe.matmul(core.bank(4, P, 2), core.const("ones"), prod[:, :], start=True, stop=True)\
                    .then_inc(f["summed"].sem, 1)
                pe.wait_ge(f["misc_loaded"].sem, f["misc_loaded"].value(32))
                for b, (lo, hi) in enumerate(((0, 12), (12, 20))):
                    pe.matmul(core.bank(2 * b, hi - lo), rel[:, lo:hi], onehot[:, 0:512], start=True, stop=True)
                    last = pe.matmul(core.bank(2 * b + 1, hi - lo, TABLE - 512), rel[:, lo:hi],
                                     onehot[:, 512:TABLE], start=True, stop=True)
                last.then_inc(f["products_done"].sem, 1)

            @block.scalar
            def _(act):
                act.wait_ge(f["summed"].sem, f["summed"].value(1))
                act.activation(exps[:, :], core.bank(4, P, 2), ACT.Exp).then_inc(f["exped"].sem, 1)
                act.activation(sig[:, :], par("c"), ACT.Sigmoid).then_inc(f["silued"].sem, 1)
    f["misc_loaded"].advance(32)
    for k in ("squared", "exped", "silued", "products_done", "summed", "made"):
        f[k].advance(1)


def modulation(core):
    nc, f = core.nc, core.flags
    sc = core.silu_c[:, :].rearrange("p (k v) -> p k v", v=2)
    jobs = []
    for l in range(2):
        for i in range(12):
            c, w = core.chunk(f"mod{l}_{i}")
            for j in range(4):
                jobs.append((c, j == 3, P, 2, [(w[:, k, j * P:(j + 1) * P], sc[:, k, :]) for k in range(KD)]))

    def finish(eng, n, ps):
        b = core.param("mod_b", n, 1)
        dst = core.mods[:, n // 48, n % 48, :]
        if eng is nc.scalar:
            return eng.activation(dst, ps, ACT.Identity, bias=b)
        return eng.tensor_scalar(dst, ps, b, None, ALU.add)
    dense(core, "modulation", jobs, finish)

    with nc.Block("mod_gains") as block:
        @block.vector
        def _(dve):
            for l in range(2):
                for which, name in ((1, "norm_mix_2"), (4, "norm_ffn_2")):
                    for v in range(2):
                        dve.scalar_tensor_tensor(
                            out=core.mod_gain[:, l, which // 4, :, v], in0=core.mods[:, l, 8 * which:8 * which + 8, v],
                            scalar=1.0, in1=core.param(name, 8 * l, 8), op0=ALU.add, op1=ALU.mult)


def modulated_norm(core, name, l, ffn, parts):
    shift = 24 if ffn else 0
    normalise(core, name, parts, lambda k, p: core.mod_gain[:, l, ffn, k, p:p + 1],
              lambda k, p: core.mods[:, l, shift + k, p:p + 1])


def residual(core, name, chunks, src, parts, gate=None):
    jobs, where = [], []
    for i, cname in enumerate(chunks):
        c, w = core.chunk(cname)
        tiles = w.shape[2] // P
        for j in range(tiles):
            for p, (t0, tn) in enumerate(parts):
                jobs.append((c, j == tiles - 1 and p == len(parts) - 1, P, tn,
                             [(w[:, k, j * P:(j + 1) * P], src(k, t0, tn)) for k in range(w.shape[1])]))
                where.append((i * tiles + j, p, t0, tn))

    def finish(dve, n, ps):
        m, p, t0, tn = where[n]
        x = core.X[:, m, t0:t0 + tn]
        if gate is None:
            return dve.tensor_tensor(x, x, ps, ALU.add)
        return dve.scalar_tensor_tensor(out=x, in0=ps, scalar=gate(m, p), in1=x, op0=ALU.mult, op1=ALU.add)
    dense(core, name, jobs, finish, both=False)


def feature_jobs(core, cname, parts, tiles=None, release=True):
    c, w = core.chunk(cname)
    tiles = range(w.shape[2] // P) if tiles is None else tiles
    jobs = []
    for j in tiles:
        for p, (t0, tn) in enumerate(parts):
            jobs.append((c, release and j == tiles[-1] and p == len(parts) - 1, P, tn,
                         [(w[:, k, j * P:(j + 1) * P], core.H[:, k, t0:t0 + tn]) for k in range(KD)]))
    return jobs


def token_jobs(core, cname, tokens, lo, hi, release=True):
    c, w = core.chunk(cname)
    return [(c, release and t == tokens - 1, P, hi - lo,
             [(core.H[:, k, t * P:(t + 1) * P], w[:, k, lo:hi]) for k in range(KD)]) for t in range(tokens)]


def compress(core, CK, KC, VC, CG, CG0):
    nc, f, dram = core.nc, core.flags, core.dram
    N2 = 2 * NC_CMP
    with ExitStack() as stack:
        def sb(name, shape):
            return stack.enter_context(nc.sbuf_tensor(name, shape, F32))
        shifted = sb("cmp_shifted", [P, 2, 2, S])
        blocks = sb("cmp_blocks", [P, 2, 16, N2])
        x = sb("cmp_x", [P, 4 * N2])
        t = sb("cmp_t", [P, 4 * N2])
        w2 = sb("cmp_w2", [P, 2, 2, P])
        root = sb("cmp_root", [P, N2])
        sq = sb("cmp_sq", [P, N2])
        for kv in range(2):
            core.used_up[core.plan[f"cmp{kv}"][0]] = (f["products_done"], f["products_done"].value(kv + 1))
        with nc.Block("compress") as block:
            @block.sync
            def _(sp):
                w = dram["cmp_w2"].rearrange("v (k p) d -> p v k d", p=P)
                for half in range(2):
                    for v in range(2):
                        sp.dma_start(w2[:, v, :, 64 * half:64 * half + 64], w[:, v]).then_inc(f["misc_loaded"].sem, 16)
                for g in range(2):
                    sp.dma_start(shifted[0:64, :, g, :], CK[64 * g:64 * g + 64, :, :])\
                        .then_inc(f["misc_loaded"].sem, 16)
                    sp.dma_start(shifted[64:128, :, g, 0:S - 1], CK[64 * g:64 * g + 64, :, 1:S])\
                        .then_inc(f["misc_loaded"].sem, 16)
                core.feed(sp, core.consumed + 2)

            @block.vector
            def _(dve):
                dve.wait_ge(f["misc_loaded"].sem, f["misc_loaded"].value(128))
                for kv in range(2):
                    for m in range(16):
                        last = dve.tensor_scalar(
                            blocks[:, kv, m, :].rearrange("p (g c) -> p g c", g=2),
                            shifted[:, kv, :, 2 * m:2 * m + 16 * (NC_CMP - 1) + 1:16],
                            core.param("cmp_pos", 16 * kv + m, 1), None, ALU.add)
                    last.then_inc(f["made"].sem, 1)
                dve.wait_ge(f["products_done"].sem, f["products_done"].value(2))
                core.v_chain(dve, dve.tensor_copy(x[:, :], core.bank(0, P, 4 * N2)))
                core.v_chain(dve, dve.tensor_tensor(t[:, :], x[:, :], x[:, :], ALU.mult))
                core.v_chain(dve, dve.tensor_scalar(t[:, :], t[:, :], 0.044715, 1.0, ALU.mult, ALU.add))
                dve.tensor_tensor(t[:, :], t[:, :], x[:, :], ALU.mult).then_inc(f["squared"].sem, 1)
                dve.wait_ge(f["exped"].sem, f["exped"].value(1))
                core.v_chain(dve, dve.tensor_scalar(t[:, :], t[:, :], 1.0, 0.5, ALU.add, ALU.mult))
                dve.tensor_tensor(x[:, :], t[:, :], x[:, :], ALU.mult).then_inc(f["made"].sem, 1)
                dve.wait_ge(f["summed"].sem, f["summed"].value(1))
                dve.tensor_copy(VC[:, :], core.bank(2, NC_CMP, P))
                dve.wait_ge(f["rooted"].sem, f["rooted"].value(1))
                dve.scalar_tensor_tensor(out=KC[:, :], in0=core.bank(1, P, N2), scalar=core.param("qk_gain", 5, 1),
                                         in1=root[:, :], op0=ALU.mult, op1=ALU.mult)
                dve.wait_ge(f["silued"].sem, f["silued"].value(1))
                for h in range(8):
                    last = dve.tensor_tensor(CG0[:, h:h + 1], CG[:, 0, 3 * h:3 * h + 1], core.param("valid31"),
                                             ALU.mult)

            @block.tensor
            def _(pe):
                for kv in range(2):
                    c, w = core.chunk(f"cmp{kv}")
                    core.await_chunk(pe, c)
                    pe.wait_ge(f["made"].sem, f["made"].value(kv + 1))
                    for ht in range(2):
                        last = products(pe, core.bank(0, P, N2, (2 * kv + ht) * N2),
                                        [(w[:, m, ht * P:(ht + 1) * P], blocks[:, kv, m, :]) for m in range(16)])
                    last.then_inc(f["products_done"].sem, 1)
                pe.wait_ge(f["made"].sem, f["made"].value(3))
                products(pe, core.bank(1, P, N2), [(w2[:, 0, ht, :], x[:, ht * N2:(ht + 1) * N2]) for ht in range(2)])
                for g in range(2):
                    last = products(pe, core.bank(2, NC_CMP, HD, g * HD),
                                    [(x[:, (2 + ht) * N2 + g * NC_CMP:(2 + ht) * N2 + (g + 1) * NC_CMP],
                                      w2[:, 1, ht, 0:HD]) for ht in range(2)])
                last.then_inc(f["summed"].sem, 1)
                pe.wait_ge(f["normed"].sem, f["normed"].value(1))
                pe.matmul(core.bank(3, P, N2), core.const("blocks"), sq[:, :], start=True, stop=True)\
                    .then_inc(f["turned"].sem, 1)

            @block.scalar
            def _(act):
                act.activation(CG[:, :, :], CG[:, :, :], ACT.Sigmoid).then_inc(f["silued"].sem, 1)
                act.wait_ge(f["squared"].sem, f["squared"].value(1))
                act.activation(t[:, :], t[:, :], ACT.Tanh, scale=math.sqrt(2 / math.pi)).then_inc(f["exped"].sem, 1)
                act.wait_ge(f["summed"].sem, f["summed"].value(1))
                act.activation(sq[:, :], core.bank(1, P, N2), ACT.Square).then_inc(f["normed"].sem, 1)
                act.wait_ge(f["turned"].sem, f["turned"].value(1))
                core.s_chain(act, act.activation(root[:, :], core.bank(3, P, N2), ACT.Ln, bias=core.eps[:, 0:1],
                                                 scale=1.0 / HD))
                act.activation(root[:, :], root[:, :], ACT.Exp, scale=-0.5).then_inc(f["rooted"].sem, 1)
    core.consumed += 2
    f["misc_loaded"].advance(128)
    f["made"].advance(3)
    f["products_done"].advance(2)
    for k in ("squared", "exped", "summed", "rooted", "silued", "normed", "turned"):
        f[k].advance(1)


def bias_tile(core, row, u0, n):
    whole = core.dram["bias"]
    return bass.AP(whole.tensor, row * P * TABLE + P - 1 + u0, [[TABLE - 1, P], [1, n]])


def first_block(core):
    nc, f = core.nc, core.flags
    normalise(core, "norm1", [LAT], lambda k, p: core.param("norm_mix", k, 1))
    with ExitStack() as stack:
        def sb(name, shape):
            return stack.enter_context(nc.sbuf_tensor(name, shape, F32))
        Q = sb("Q", [P, 12, S])
        YS = sb("YS", [P, KD, S])
        V = sb("V", [P, 4, 512 + 384])
        CG = sb("CG", [P, 4, 24])
        CG0 = sb("CG0", [P, 8])
        KC = sb("KC", [P, 2 * NC_CMP])
        VC = sb("VC", [NC_CMP, P])
        AQ, BQ, CQ = Q[:, 0:4, :], Q[:, 4:8, :], Q[:, 8:12, :]
        AK, KK = YS[:, 0:4, :], YS[:, 4:7, :]
        with ExitStack() as inner:
            def tmp(name, shape):
                return inner.enter_context(nc.sbuf_tensor(name, shape, F32))
            CK = tmp("CK", [P, 2, S])
            jobs = [j for i in range(4) for j in feature_jobs(core, f"proj{i}", [LAT])]
            jobs += feature_jobs(core, "proj4", [LAT], tiles=range(3), release=False)
            dests = [AQ[:, i, :] for i in range(4)] + [AK[:, i, :] for i in range(4)] + \
                    [BQ[:, i, :] for i in range(4)] + [CQ[:, i, :] for i in range(4)] + \
                    [KK[:, i, :] for i in range(3)]
            der = core.derived
            gains = [der[:, AQ_G:AQ_G + 1]] * 4 + [core.param("qk_gain", 1, 1)] * 4 + [der[:, BQ_G:BQ_G + 1]] * 4 + \
                    [der[:, CQ_G:CQ_G + 1]] * 4 + [core.param("qk_gain", i, 1) for i in (3, 6, 7)]
            with nc.sbuf_tensor("squares", [P, 2, 512], F32) as sq, nc.sbuf_tensor("roots", [P, 2, 512], F32) as rt:
                head_normed(core, "project_qk", jobs, (sq, rt), lambda n: dests[n], lambda n: gains[n], HD,
                            core.const("blocks"))
            jobs = feature_jobs(core, "proj4", [LAT], tiles=range(3, 4))
            jobs += feature_jobs(core, "proj5", [LAT], tiles=range(0, 1), release=False)
            to = [CK[:, 0, :], CK[:, 1, :]]
            jobs += token_jobs(core, "proj5", 4, P, 512)
            to += [V[:, t, 512:896] for t in range(4)]
            jobs += token_jobs(core, "proj6", 4, 0, 512)
            to += [V[:, t, 0:512] for t in range(4)]
            jobs += token_jobs(core, "proj7", 4, 0, 24)
            to += [CG[:, t, :] for t in range(4)]
            dense(core, "project_v", jobs, copy_out(core, lambda n: to[n]))
            compress(core, CK, KC, VC, CG, CG0)

        with ExitStack() as inner:
            bias = inner.enter_context(nc.sbuf_tensor("bias_tiles", [P, 2, 512], F32))
            neg_lam = core.derived[:, NEG_LAM:NEG_LAM + 1]
            units, loads = [], []
            for h in range(4):
                loads.append((bias[:, h % 2, :], bias_tile(core, h, 0, 512), 8 * (h - 1) - 1 if h >= 2 else None))
                for i in range(4):
                    for c in range(2):
                        rows = slice(64 * c, 64 * c + 64)
                        units.append(unit(
                            AQ[rows, h, i * P:(i + 1) * P], [AK[rows, h, 0:(i + 1) * P]],
                            [V[:, t, h * P:(h + 1) * P] for t in range(i + 1)], h % 2, i * P, c == 0, c == 1,
                            bias=bias[:, h % 2, 384 - P * i:512], bias_load=h, coef=neg_lam if c else 1.0,
                            evac=(AQ[:, h, :], (0, P)) if (i, c) == (3, 1) else None))
            attention(core, "attn_a", plan_outputs(units), loads)

            units, loads = [], []
            for h in range(8):
                j, g = h % 4, h // 4
                rows = slice(64 * g, 64 * g + 64)
                loads.append((bias[:, h % 2, 0:256], bias_tile(core, 12 + h, 256, 256),
                              4 * (h - 1) - 1 if h >= 2 else None))
                for i in range(4):
                    lo = max(0, i - 1)
                    units.append(unit(
                        BQ[rows, j, i * P:(i + 1) * P], [KK[rows, 0, lo * P:(i + 1) * P]],
                        [V[:, t, 512:640] for t in range(lo, i + 1)], h % 2, i * P,
                        bias=bias[:, h % 2, 0 if i else P:256], bias_load=h, sink=core.param("sinks", h, 1),
                        evac=(BQ[rows, j, :], (64 * g, 64 * g + 64)) if i == 3 else None))
            attention(core, "attn_b", plan_outputs(units), loads)

            units, loads = [], []
            for h in range(8):
                j, g = h % 4, h // 4
                rows = slice(64 * g, 64 * g + 64)
                loads.append((bias[:, h % 2, :], bias_tile(core, 4 + h, 0, 512), 12 * (h - 1) - 1 if h >= 2 else None))
                for i in range(4):
                    q = CQ[rows, j, i * P:(i + 1) * P]
                    mask = core.const("cmask")[:, i * NC_CMP:(i + 1) * NC_CMP]
                    units.append(unit(q, [KC[rows, g * NC_CMP:(g + 1) * NC_CMP]], [VC[:, :]], h % 2, i * P, True, False,
                                      bias=mask, coef=CG[:, i, 3 * h:3 * h + 1] if i else CG0[:, h:h + 1]))
                    for b in range(2):
                        units.append(unit(
                            q, [KK[rows, 1 + b, 0:(i + 1) * P]],
                            [V[:, t, 640 + P * b:768 + P * b] for t in range(i + 1)], h % 2, i * P, False, b == 1,
                            bias=bias[:, h % 2, 384 - P * i:512], bias_load=h,
                            coef=CG[:, i, 3 * h + 1 + b:3 * h + 2 + b],
                            evac=(CQ[rows, j, :], (64 * g, 64 * g + 64)) if (i, b) == (3, 1) else None))
            attention(core, "attn_c", plan_outputs(units), loads)

        with ExitStack() as inner:
            def tmp(name, shape):
                return inner.enter_context(nc.sbuf_tensor(name, shape, F32))
            scratch = tmp("squares2", [P, 2, 512]), tmp("roots2", [P, 2, 512])
            head_normed(core, "norm_a", [(None, False, P, S, None)] * 4, scratch, lambda n: AQ[:, n, :],
                        lambda n: core.derived[:, SUBLN:SUBLN + 1], P, core.const("ones"),
                        sources=[AQ[:, n, :] for n in range(4)])
        branches(core, Q, YS)
        residual(core, "mix_out", ["out0", "out1"], lambda k, t0, tn: YS[:, k, t0:t0 + tn], [LAT])

    normalise(core, "norm_mlp", [LAT], lambda k, p: core.param("norm_mlp", k, 1))
    with nc.sbuf_tensor("hidden", [P, D_FF // P, S], F32) as U:
        jobs = [j for i in range(8) for j in feature_jobs(core, f"up{i}", [LAT])]

        def squared_relu(eng, n, ps):
            if eng is nc.scalar:
                core.s_chain(eng, eng.activation(U[:, n, :], ps, ACT.Relu))
                return eng.activation(U[:, n, :], U[:, n, :], ACT.Square)
            core.v_chain(eng, eng.tensor_scalar(U[:, n, :], ps, 0.0, None, ALU.max))
            return eng.tensor_tensor(U[:, n, :], U[:, n, :], U[:, n, :], ALU.mult)
        dense(core, "mlp_up", jobs, squared_relu)
        residual(core, "mlp_down", [f"down{i}" for i in range(8)], lambda k, t0, tn: U[:, k, t0:t0 + tn], [LAT])


def branches(core, Q, YS):
    nc, f = core.nc, core.flags
    with nc.sbuf_tensor("gates", [P, 2, S], F32) as SG, nc.sbuf_tensor("gated_y", [P, 2, S], F32) as GY:
        for n in range(3):
            for half in range(2):
                core.used_up[core.plan[f"mg{n}_{half}"][0]] = \
                    (f["products_done"], f["products_done"].value(8 * n + 4 * half + 4))
            core.used_up[core.plan[f"branch{n}"][0]] = (f["down_done"], f["down_done"].value(8 * n + 8))
        with nc.Block("branches") as block:
            @block.sync
            def _(sp):
                core.feed(sp, core.consumed + 9)

            @block.tensor
            def _(pe):
                for i in range(24):
                    n, m = i // 8, i % 8
                    if m % 4 == 0:
                        c, w = core.chunk(f"mg{n}_{m // 4}")
                        core.await_chunk(pe, c)
                    if i >= 2:
                        pe.wait_ge(f["silued"].sem, f["silued"].value(i - 1))
                    last = products(pe, core.bank(i % 2), [(w[:, k, (m % 4) * P:(m % 4 + 1) * P], core.H[:, k, 0:S])
                                                           for k in range(KD)])
                    last.then_inc(f["products_done"].sem, 1)
                    cb, wb = core.chunk(f"branch{n}")
                    if m == 0:
                        core.await_chunk(pe, cb)
                    if i >= 2:
                        pe.wait_ge(f["gated"].sem, f["gated"].value(i - 1))
                    last = products(pe, core.bank(2 + i % 2), [(wb[:, k, m * P:(m + 1) * P], Q[:, 4 * n + k, :])
                                                               for k in range(4)])
                    last.then_inc(f["down_done"].sem, 1)

            @block.scalar
            def _(act):
                for i in range(24):
                    act.wait_ge(f["products_done"].sem, f["products_done"].value(i + 1))
                    if i >= 2:
                        act.wait_ge(f["gated"].sem, f["gated"].value(i - 1))
                    act.activation(SG[:, i % 2, :], core.bank(i % 2), ACT.Sigmoid).then_inc(f["silued"].sem, 1)

            @block.vector
            def _(dve):
                for i in range(24):
                    m = i % 8
                    dve.wait_ge(f["silued"].sem, f["silued"].value(i + 1))
                    dve.wait_ge(f["down_done"].sem, f["down_done"].value(i + 1))
                    y = core.bank(2 + i % 2)
                    if i < 8:
                        dve.tensor_tensor(YS[:, m, :], SG[:, i % 2, :], y, ALU.mult).then_inc(f["gated"].sem, 1)
                    else:
                        core.v_chain(dve, dve.tensor_tensor(GY[:, i % 2, :], SG[:, i % 2, :], y, ALU.mult))
                        dve.tensor_tensor(YS[:, m, :], YS[:, m, :], GY[:, i % 2, :], ALU.add).then_inc(f["gated"].sem, 1)
    core.consumed += 9
    for k in ("products_done", "down_done", "silued", "gated"):
        f[k].advance(24)


def rotate(core, name, tiles, cos_sin):
    nc, f = core.nc, core.flags
    with nc.sbuf_tensor(name + "_turned", [P, 2, S], F32) as R, nc.Block(name) as block:
        @block.tensor
        def _(pe):
            for n, tile in enumerate(tiles):
                if n >= 2:
                    pe.wait_ge(f["normed"].sem, f["normed"].value(n - 1))
                pe.matmul(core.bank(n % 2), core.const("rot"), tile, start=True, stop=True)\
                    .then_inc(f["turned"].sem, 1)

        @block.vector
        def _(dve):
            for n, tile in enumerate(tiles):
                dve.wait_ge(f["turned"].sem, f["turned"].value(n + 1))
                dve.tensor_tensor(R[:, n % 2, :], core.bank(n % 2), cos_sin[:, 1, :], ALU.mult)
                core.v_chain(dve, dve.tensor_tensor(tile, tile, cos_sin[:, 0, :], ALU.mult))
                dve.tensor_tensor(tile, tile, R[:, n % 2, :], ALU.add).then_inc(f["normed"].sem, 1)
    f["turned"].advance(len(tiles))
    f["normed"].advance(len(tiles))


def over(ap, n):
    return ap.broadcast_to([ap.shape[0], ap.shape[1], n])


def gla_decays(core, z, GQ, GK, LR, gate_w, bufs, rates):
    nc, f = core.nc, core.flags
    CLIP = 40.0
    NCH = T // P
    B, G, EQ, EK0, EK1, QB, KE = (b[:, :] for b in bufs)
    GQf, GKf = (x[:, :, :].rearrange("p a t -> p (a t)") for x in (GQ, GK))
    parts = [LAT, CON]

    def by_chunk(x):
        return x.rearrange("p (c t) -> p c t", t=P)

    with nc.Block(f"decays{z}") as block:
        @block.tensor
        def _(pe):
            for a in range(2):
                for p, (t0, tn) in enumerate(parts):
                    pe.matmul(core.bank(2 * a + p, P, tn), gate_w[:, z, a * P:(a + 1) * P], LR[:, t0:t0 + tn],
                              start=True, stop=True).then_inc(f["products_done"].sem, 1)

        @block.vector
        def _(dve):
            def step(ins):
                core.v_chain(dve, ins)
            for a in range(2):
                for p, (t0, tn) in enumerate(parts):
                    dve.wait_ge(f["products_done"].sem, f["products_done"].value(2 * a + p + 1))
                    last = dve.tensor_scalar(G[:, a * T + t0:a * T + t0 + tn], core.bank(2 * a + p, P, tn),
                                             core.param("gla_b", 2 * z + a, 1), None, ALU.add)
            step(last)
            dve.scalar_tensor_tensor(out=B, in0=G, scalar=-1.0, in1=G, op0=ALU.mult, op1=ALU.max)\
                .then_inc(f["made"].sem, 1)
            dve.wait_ge(f["rooted"].sem, f["rooted"].value(1))
            step(dve.scalar_tensor_tensor(out=G, in0=G, scalar=0.0, in1=B, op0=ALU.min, op1=ALU.subtract))
            step(dve.tensor_scalar(G, G, 1.0 / 16.0, None, ALU.mult))
            step(dve.memset(KE, 1.0))
            for c in range(2 * NCH):
                last = dve.tensor_tensor_scan(out=by_chunk(B)[:, c, :], data0=by_chunk(KE)[:, c, :],
                                              data1=by_chunk(G)[:, c, :], initial=0.0, op0=ALU.mult, op1=ALU.add)
            step(last)
            if z == 1:
                step(dve.tensor_tensor(G, G, B, ALU.subtract))
                step(dve.tensor_copy(rates[:, 0:1, :].rearrange("p a c -> p c a"), by_chunk(B)[:, :, P - 1:P]))
                step(dve.tensor_tensor(by_chunk(B), by_chunk(G),
                                       over(rates[:, 0:1, :].rearrange("p a c -> p c a"), P), ALU.add))
            end = P - 1 if z == 0 else 0
            total = by_chunk(B)[:, :, end:end + 1]
            step(dve.tensor_copy(rates[:, 1:2, :].rearrange("p a c -> p c a"), total))
            total = rates[:, 1:2, :].rearrange("p a c -> p c a")
            for half in range(2):
                mid = by_chunk(B)[:, :, 64 * half + 32:64 * half + 33]
                EK = (EK0, EK1)[half]
                step(dve.tensor_copy(rates[:, 2 + half:3 + half, :].rearrange("p a c -> p c a"), mid))
                mid = rates[:, 2 + half:3 + half, :].rearrange("p a c -> p c a")
                dve.tensor_tensor(by_chunk(EK), over(mid, P), by_chunk(B), ALU.subtract)
                t = slice(64 * half, 64 * half + 64)
                step(dve.tensor_tensor(by_chunk(EQ)[:, :, t], by_chunk(B)[:, :, t], over(mid, 64), ALU.subtract))
                step(dve.tensor_scalar(EK, EK, CLIP, None, ALU.min))
            step(dve.tensor_scalar(EQ, EQ, CLIP, None, ALU.min))
            step(dve.tensor_tensor(by_chunk(KE), over(total, P), by_chunk(B), ALU.subtract))
            dve.tensor_copy(QB, B).then_inc(f["made"].sem, 1)
            for n, (e, x) in enumerate(((EQ, GQf), (QB, GQf), (EK0, GKf), (EK1, GKf), (KE, GKf))):
                dve.wait_ge(f["exped"].sem, f["exped"].value(n + 1))
                dve.tensor_tensor(e, e, x, ALU.mult)

        @block.scalar
        def _(act):
            act.wait_ge(f["made"].sem, f["made"].value(1))
            core.s_chain(act, act.activation(B, B, ACT.Exp, scale=-1.0))
            act.activation(B, B, ACT.Ln, bias=1.0).then_inc(f["rooted"].sem, 1)
            act.wait_ge(f["made"].sem, f["made"].value(2))
            for e in (EQ, QB, EK0, EK1, KE):
                act.activation(e, e, ACT.Exp).then_inc(f["exped"].sem, 1)
            act.activation(rates[:, 1, :], rates[:, 1, :], ACT.Exp)
    f["products_done"].advance(4)
    f["made"].advance(2)
    f["rooted"].advance(1)
    f["exped"].advance(5)


def gla_chunks(core, z, GV, GO, bufs, rates, state, keys, att):
    nc, f = core.nc, core.flags
    _, _, EQ, EK0, EK1, QB, KE = (b[:, :].rearrange("p (a t) -> p a t", a=2) for b in bufs)
    NCH = T // P
    order = [4, 5, 0, 1, 2, 3] if z == 0 else [5, 4, 3, 2, 1, 0]
    mask = core.const("causal_st") if z == 0 else core.const("anti_st")
    steps = [(n, c, h) for n, c in enumerate(order) for h in range(4)]

    with nc.Block(f"gla{z}") as block:
        @block.tensor
        def _(pe):
            def scores(i):
                n, c, h = steps[i]
                a, rows = h // 2, slice(64 * (h % 2), 64 * (h % 2) + 64)
                if i >= 2:
                    pe.wait_ge(f["weighted"].sem, f["weighted"].value(i - 1))
                for half, EK in enumerate((EK0, EK1)):
                    last = pe.matmul(core.bank(i % 2, P, 64, 64 * half), EK[rows, a, c * P:(c + 1) * P],
                                     EQ[rows, a, c * P + 64 * half:c * P + 64 * half + 64], start=True, stop=True)
                last.then_inc(f["scored"].sem, 1)
                if h % 2 == 0:
                    j = i // 2
                    if j >= 2:
                        pe.wait_ge(f["copied"].sem, f["copied"].value(j - 1))
                    pe.transpose(core.bank(2 + j % 2, P, P), KE[:, a, c * P:(c + 1) * P], core.const("ident"))\
                        .then_inc(f["turned"].sem, 1)

            def values(i):
                n, c, h = steps[i]
                a, rows = h // 2, slice(64 * (h % 2), 64 * (h % 2) + 64)
                v = GV[:, c, h * P:(h + 1) * P]
                pe.wait_ge(f["weighted"].sem, f["weighted"].value(i + 1))
                if i >= 2:
                    pe.wait_ge(f["emptied"].sem, f["emptied"].value(i - 1))
                last = pe.matmul(core.bank(4 + i % 2, P, P), v, att[:, i % 2, :], start=True, stop=n == 0)
                if n:
                    pe.wait_ge(f["added"].sem, f["added"].value(i - 3))
                    last = pe.matmul(core.bank(4 + i % 2, P, P), state[rows, h, :], QB[rows, a, c * P:(c + 1) * P],
                                     start=False, stop=True)
                last.then_inc(f["attended"].sem, 1)
                pe.wait_ge(f["copied"].sem, f["copied"].value(i // 2 + 1))
                if i >= 2:
                    pe.wait_ge(f["added"].sem, f["added"].value(i - 1))
                pe.matmul(core.bank(6 + i % 2, P, P), keys[:, (i // 2) % 2, :], v, start=True, stop=True)\
                    .then_inc(f["summed"].sem, 1)

            for i in range(len(steps) + 1):
                if i < len(steps):
                    scores(i)
                if i >= 1:
                    values(i - 1)

        @block.scalar
        def _(act):
            for j in range(len(steps) // 2):
                act.wait_ge(f["turned"].sem, f["turned"].value(j + 1))
                if j >= 2:
                    act.wait_ge(f["summed"].sem, f["summed"].value(2 * j - 2))
                act.activation(keys[:, j % 2, :], core.bank(2 + j % 2, P, P), ACT.Copy).then_inc(f["copied"].sem, 1)

        @block.vector
        def _(dve):
            def masked(i):
                dve.wait_ge(f["scored"].sem, f["scored"].value(i + 1))
                if i >= 2:
                    dve.wait_ge(f["attended"].sem, f["attended"].value(i - 1))
                dve.tensor_tensor(att[:, i % 2, :], mask, core.bank(i % 2, P, P), ALU.mult)\
                    .then_inc(f["weighted"].sem, 1)

            def out(i):
                n, c, h = steps[i]
                a, rows = h // 2, slice(64 * (h % 2), 64 * (h % 2) + 64)
                dve.wait_ge(f["attended"].sem, f["attended"].value(i + 1))
                dst, ps = GO[:, h, c * P:(c + 1) * P], core.bank(4 + i % 2, P, P)
                if z == 0:
                    last = dve.tensor_copy(dst, ps)
                else:
                    last = dve.tensor_tensor(dst, dst, ps, ALU.add)
                last.then_inc(f["emptied"].sem, 1)
                dve.wait_ge(f["summed"].sem, f["summed"].value(i + 1))
                u = core.psum[rows, 6 + i % 2, 0:P]
                if n == 0:
                    last = dve.tensor_copy(state[rows, h, :], u)
                else:
                    last = dve.scalar_tensor_tensor(out=state[rows, h, :], in0=state[rows, h, :],
                                                    scalar=rates[rows, 1, a * NCH + c:a * NCH + c + 1], in1=u,
                                                    op0=ALU.mult, op1=ALU.add)
                last.then_inc(f["added"].sem, 1)

            for i in range(len(steps) + 1):
                if i < len(steps):
                    masked(i)
                if i >= 1:
                    out(i - 1)
    N = len(steps)
    for k in ("scored", "weighted", "attended", "summed", "emptied", "added"):
        f[k].advance(N)
    f["turned"].advance(N // 2)
    f["copied"].advance(N // 2)


def even_layer(core):
    nc, f, dram = core.nc, core.flags, core.dram
    parts = [LAT, CON]
    modulated_norm(core, "norm_e", 0, 0, parts)
    with ExitStack() as stack:
        def sb(name, shape):
            return stack.enter_context(nc.sbuf_tensor(name, shape, F32))
        AQ = sb("eAQ", [P, 4, T])
        LR = sb("LR", [32, T])
        with ExitStack() as inner:
            def tmp(name, shape):
                return inner.enter_context(nc.sbuf_tensor(name, shape, F32))
            AK = tmp("eAK", [P, T])
            AV = tmp("eAV", [P, T // P, P])
            trig = tmp("trig", [P, 2, S])
            with nc.Block("load_trig") as block:
                @block.sync
                def _(sp):
                    sp.dma_start(trig[:, :, :], dram["trig"]).then_inc(f["misc_loaded"].sem, 16)
                    sp.wait_ge(f["misc_loaded"].sem, f["misc_loaded"].value(16))
            f["misc_loaded"].advance(16)
            scratch = tmp("squares_e", [P, 2, 512]), tmp("roots_e", [P, 2, 512])
            jobs = feature_jobs(core, "ev0", parts)
            jobs += feature_jobs(core, "ev1", parts, tiles=range(1), release=False)
            dests = [AQ[:, j, t0:t0 + tn] for j in range(4) for t0, tn in parts] + [AK[:, t0:t0 + tn] for t0, tn in parts]
            head_normed(core, "project_eqk", jobs, scratch, lambda n: dests[n],
                        lambda n: core.derived[:, ATT_G:ATT_G + 1] if n < 8 else core.param("att_k"), HD,
                        core.const("blocks"))
            c, w = core.chunk("ev1")
            jobs = [(c, False, 32, tn, [(w[:, k, 256:288], core.H[:, k, t0:t0 + tn]) for k in range(KD)])
                    for t0, tn in parts]
            jobs += token_jobs(core, "ev1", T // P, P, 2 * P)
            to = [LR[:, t0:t0 + tn] for t0, tn in parts] + [AV[:, t, :] for t in range(T // P)]
            dense(core, "project_ev", jobs, copy_out(core, lambda n: to[n]))
            rotate(core, "rope_e", [AQ[:, j, 0:S] for j in range(4)] + [AK[:, 0:S]], trig)
            units = []
            for h in range(8):
                j, g = h % 4, h // 4
                rows = slice(64 * g, 64 * g + 64)
                for t0, tn, keys in ((0, S, [(0, S), (S, CTX)]), (S, CTX, [(S, CTX)])):
                    tiles = [t for k0, kn in keys for t in range(k0 // P, (k0 + kn) // P)]
                    for i in range(tn // P):
                        last = i == tn // P - 1
                        units.append(unit(
                            AQ[rows, j, t0 + i * P:t0 + (i + 1) * P], [AK[rows, k0:k0 + kn] for k0, kn in keys],
                            [AV[:, t, :] for t in tiles], (0 if t0 == 0 else 1), i * P,
                            evac=(AQ[rows, j, t0:t0 + tn], (64 * g, 64 * g + 64)) if last else None))
            attention(core, "attn_e", plan_outputs(units))

        GQ, GK = sb("GQ", [P, 2, T]), sb("GK", [P, 2, T])
        GR = sb("GR", [P, 4, T])
        GV = sb("GV", [P, T // P, 512])
        jobs = feature_jobs(core, "ev2", parts)
        to = [x[:, a, t0:t0 + tn] for x in (GQ, GK) for a in range(2) for t0, tn in parts]

        def take_qk(eng, n, ps):
            scale = HD ** -0.5 if n < 4 else 1.0
            if eng is nc.scalar:
                return eng.activation(to[n], ps, ACT.Copy, scale=scale)
            return eng.tensor_scalar(to[n], ps, scale, None, ALU.mult)
        dense(core, "project_gqk", jobs, take_qk)
        to_r = [GR[:, a, t0:t0 + tn] for a in range(4) for t0, tn in parts]
        dense(core, "project_gr", feature_jobs(core, "ev3", parts), copy_out(core, lambda n: to_r[n]))
        dense(core, "project_gv", token_jobs(core, "ev4", T // P, 0, 512), copy_out(core, lambda n: GV[:, n, :]))

        GO = sb("GO", [P, 4, T])
        with ExitStack() as inner:
            def tmp(name, shape):
                return inner.enter_context(nc.sbuf_tensor(name, shape, F32))
            Hf = core.H[:, :, :].rearrange("p k t -> p (k t)")
            n = 2 * T
            bufs = [tmp("gB", [P, n]), tmp("gG", [P, n])] + [Hf[:, i * n:(i + 1) * n] for i in range(4)] + [tmp("gKE", [P, n])]
            rates = tmp("rates", [P, 4, 2 * T // P])
            state = tmp("state", [P, 4, P])
            keys = tmp("keys", [P, 2, P])
            att = tmp("att", [P, 2, P])
            gate_w = tmp("gate_w", [32, 2, 256])
            with nc.Block("load_gate_w") as block:
                @block.sync
                def _(sp):
                    sp.dma_start(gate_w[:, :, :], dram["gate_w"]).then_inc(f["misc_loaded"].sem, 16)
                    sp.wait_ge(f["misc_loaded"].sem, f["misc_loaded"].value(16))
            f["misc_loaded"].advance(16)
            for z in range(2):
                gla_decays(core, z, GQ, GK, LR, gate_w, bufs, rates)
                gla_chunks(core, z, GV, GO, bufs, rates, state, keys, att)
        with ExitStack() as inner:
            def tmp(name, shape):
                return inner.enter_context(nc.sbuf_tensor(name, shape, F32))
            scratch = core.H[:, 0:2, 0:512], core.H[:, 2:4, 0:512]
            tiles = [GO[:, h, t0:t0 + tn] for h in range(4) for t0, tn in parts]
            head_normed(core, "norm_g", [(None, False, P, t.shape[-1], None) for t in tiles], scratch,
                        lambda n: tiles[n], lambda n: core.param("gla_norm"), P, core.const("ones"), sources=tiles)
            with nc.Block("silu_r") as block:
                @block.scalar
                def _(act):
                    for h in range(4):
                        act.activation(core.H[:, h, :], GR[:, h, :], ACT.Sigmoid).then_inc(f["silued"].sem, 1)

                @block.vector
                def _(dve):
                    for h in range(4):
                        core.v_chain(dve, dve.tensor_tensor(GO[:, h, :], GO[:, h, :], GR[:, h, :], ALU.mult))
                        dve.wait_ge(f["silued"].sem, f["silued"].value(h + 1))
                        dve.tensor_tensor(GO[:, h, :], GO[:, h, :], core.H[:, h, :], ALU.mult)
            f["silued"].advance(4)
        residual(core, "even_out", ["ev_out0", "ev_out1"],
                 lambda k, t0, tn: (GO if k < 4 else AQ)[:, k % 4, t0:t0 + tn], parts,
                 gate=lambda m, p: core.mods[:, 0, 16 + m, p:p + 1])


def odd_layer(core):
    nc, f, dram = core.nc, core.flags, core.dram
    parts = [LAT, CON]
    modulated_norm(core, "norm_o", 1, 0, parts)
    with ExitStack() as stack:
        def sb(name, shape):
            return stack.enter_context(nc.sbuf_tensor(name, shape, F32))
        Q = sb("oQ", [P, 8, S])
        K = sb("oK", [P, T])
        V = sb("oV", [P, T // P, P])
        trig = sb("trig_o", [P, 2, S])
        masks = sb("masks_o", [P, 640 + 512])
        with nc.Block("load_trig_o") as block:
            @block.sync
            def _(sp):
                sp.dma_start(trig[:, :, :], dram["trig"]).then_inc(f["misc_loaded"].sem, 16)
                sp.dma_start(masks[:, :], dram["window"]).then_inc(f["misc_loaded"].sem, 16)
                sp.wait_ge(f["misc_loaded"].sem, f["misc_loaded"].value(32))
        f["misc_loaded"].advance(32)
        with ExitStack() as inner:
            scratch = [inner.enter_context(nc.sbuf_tensor(n, [P, 2, 512], F32)) for n in ("squares_o", "roots_o")]
            jobs = feature_jobs(core, "od0", [LAT]) + feature_jobs(core, "od1", [LAT])
            jobs += feature_jobs(core, "od2", parts, tiles=range(1), release=False)
            dests = [Q[:, j, :] for j in range(8)] + [K[:, t0:t0 + tn] for t0, tn in parts]
            head_normed(core, "project_oqk", jobs, scratch, lambda n: dests[n],
                        lambda n: core.derived[:, SWA_G:SWA_G + 1] if n < 8 else core.param("swa_k"), HD,
                        core.const("blocks"))
        dense(core, "project_ov", token_jobs(core, "od2", T // P, P, 2 * P), copy_out(core, lambda n: V[:, n, :]))
        rotate(core, "rope_o", [Q[:, j, :] for j in range(8)] + [K[:, 0:S]], trig)
        units = []
        for h in range(16):
            j, g = h % 8, h // 8
            rows = slice(64 * g, 64 * g + 64)
            for i in range(4):
                lo, hi = max(0, i - 1), min(3, i + 1)
                n = CTX + (hi - lo + 1) * P
                mask = masks[:, 0:n] if i else masks[:, 640:640 + n]
                units.append(unit(
                    Q[rows, j, i * P:(i + 1) * P], [K[rows, S:T], *split_keys(K, rows, lo, hi)],
                    [V[:, t, :] for t in (4, 5, *range(lo, hi + 1))], h % 2, i * P, bias=mask,
                    sink=core.param("swa_sink", h, 1),
                    evac=(Q[rows, j, :], (64 * g, 64 * g + 64)) if i == 3 else None))
        attention(core, "attn_o", plan_outputs(units))
        residual(core, "odd_out", ["od_out0", "od_out1"], lambda k, t0, tn: Q[:, k, t0:t0 + tn], [LAT],
                 gate=lambda m, p: core.mods[:, 1, 16 + m, p:p + 1])


def split_keys(K, rows, lo, hi):
    cut = min(lo + 2, hi + 1)
    return [K[rows, a * P:b * P] for a, b in ((lo, cut), (cut, hi + 1)) if b > a]


def expert_tiles(tokens):
    return (2 * tokens + N_EXP * (P - 1)) // P


def route(core, l, tokens, weight, posu, tile_expert):
    nc, f, dram = core.nc, core.flags, core.dram
    NT = tokens // P
    TILES = expert_tiles(tokens)
    with ExitStack() as stack:
        def sb(name, shape, dtype=F32):
            return stack.enter_context(nc.sbuf_tensor(f"{name}{l}", shape, dtype))
        L = sb("logits", [P, NT, 20])
        one = sb("rt_one", [P, NT, 8])
        hot = sb("rt_hot", [P, NT, 12])
        tmp4 = sb("rt_tmp4", [P, NT, 4])
        esel = sb("rt_esel", [P, NT, 4])
        eall = sb("rt_eall", [P, NT, 16])
        taken = sb("rt_taken", [P, NT])
        first = sb("rt_first", [P, NT, 16])
        second = sb("rt_second", [P, NT, 16])
        both = sb("rt_both", [P, NT, 16])
        rank = sb("rt_rank", [P, NT, 16])
        before = sb("rt_before", [P, NT + 1, 16])
        count = sb("rt_count", [P, NT, 16])
        tiles = sb("rt_tiles", [P, 16])
        ends = sb("rt_ends", [P, 2, 16])
        start = sb("rt_start", [P, 1, 16])
        pos = sb("rt_pos", [P, 2, NT])
        passed = sb("rt_passed", [1, TILES, 16])
        index = sb("rt_index", [1, TILES, 1])
        no_token = sb("rt_no_token", [TILES, P], U32)
        token = sb("rt_token", [P, NT], U32)
        rows = sb("rt_rows", [P, 2, D])
        with nc.Block(f"route{l}") as block:
            @block.tensor
            def _(pe):
                for t in range(NT):
                    last = products(pe, core.bank(0, P, 20, 20 * t),
                                    [(core.H[:, k, t * P:(t + 1) * P], core.router[:, l, k, :]) for k in range(KD)])
                last.then_inc(f["products_done"].sem, 1)
                for t in range(NT):
                    if t >= 2:
                        pe.wait_ge(f["copied"].sem, f["copied"].value(t - 1))
                    for k in range(KD):
                        last = pe.transpose(core.bank(4 + 2 * (t % 2) + k // 4, P, P, P * (k % 4)),
                                            core.H[:, k, t * P:(t + 1) * P], core.const("ident"))
                    last.then_inc(f["rows_turned"].sem, 1)
                pe.wait_ge(f["made"].sem, f["made"].value(2))
                pe.matmul(core.bank(1, P, 16 * NT), core.const("causal_st"),
                          both[:, :, :].rearrange("p t e -> p (t e)"), start=True, stop=True)
                pe.matmul(core.bank(2, P, 16 * NT), core.const("ones"),
                          both[:, :, :].rearrange("p t e -> p (t e)"), start=True, stop=True)\
                    .then_inc(f["turned"].sem, 1)

            @block.vector
            def _(dve):
                def step(ins):
                    core.v_chain(dve, ins)

                def pick(best, scores, out):
                    step(dve.tensor_tensor(tmp4[:, :, :], scores, over(best, 4), ALU.is_equal))
                    step(dve.tensor_copy(out[:, :, 0], tmp4[:, :, 0]))
                    step(dve.tensor_copy(taken[:, :], tmp4[:, :, 0]))
                    for e in range(1, 4):
                        step(dve.tensor_tensor(out[:, :, e], tmp4[:, :, e], taken[:, :], ALU.is_gt))
                        if e < 3:
                            step(dve.tensor_tensor(taken[:, :], taken[:, :], tmp4[:, :, e], ALU.max))

                dve.memset(no_token[:, :], 0).then_inc(f["made"].sem, 1)
                dve.memset(before[:, 0, :], 0.0)
                step(dve.tensor_copy(token[:, :], core.const("token_no")[:, 0:NT]))
                dve.wait_ge(f["products_done"].sem, f["products_done"].value(1))
                for t in range(NT):
                    last = dve.tensor_tensor(L[:, t, :], core.bank(0, P, 20, 20 * t),
                                             core.param("router_b", 20 * l, 20), ALU.add)
                step(last)
                G = L[:, :, 0:4]
                step(dve.tensor_reduce(one[:, :, 0:1], G, AX.X, ALU.max))
                pick(one[:, :, 0:1], G, hot[:, :, 0:4])
                step(dve.tensor_tensor(esel[:, :, :], G, over(one[:, :, 0:1], 4), ALU.subtract))
                dve.tensor_copy(tmp4[:, :, :], esel[:, :, :]).then_inc(f["weighted"].sem, 1)
                for g in range(4):
                    last = dve.tensor_tensor(eall[:, :, 4 * g:4 * g + 4], L[:, :, 4 + 4 * g:8 + 4 * g],
                                             over(hot[:, :, g:g + 1], 4), ALU.mult)
                step(last)
                for g in range(1, 4):
                    step(dve.tensor_tensor(eall[:, :, 0:4], eall[:, :, 0:4], eall[:, :, 4 * g:4 * g + 4], ALU.add))
                dve.wait_ge(f["exped"].sem, f["exped"].value(1))
                step(dve.tensor_reduce(one[:, :, 1:2], tmp4[:, :, :], AX.X, ALU.add))
                step(dve.reciprocal(one[:, :, 2:3], one[:, :, 1:2]))
                step(dve.tensor_copy(esel[:, :, :], eall[:, :, 0:4]))
                step(dve.tensor_reduce(one[:, :, 3:4], esel[:, :, :], AX.X, ALU.max))
                pick(one[:, :, 3:4], esel[:, :, :], hot[:, :, 4:8])
                step(dve.tensor_scalar(tmp4[:, :, :], hot[:, :, 4:8], NEG, None, ALU.mult))
                step(dve.tensor_tensor(esel[:, :, :], esel[:, :, :], tmp4[:, :, :], ALU.add))
                step(dve.tensor_reduce(one[:, :, 4:5], esel[:, :, :], AX.X, ALU.max))
                pick(one[:, :, 4:5], esel[:, :, :], hot[:, :, 8:12])
                for g in range(4):
                    dve.tensor_tensor(first[:, :, 4 * g:4 * g + 4], hot[:, :, 4:8], over(hot[:, :, g:g + 1], 4), ALU.mult)
                    last = dve.tensor_tensor(second[:, :, 4 * g:4 * g + 4], hot[:, :, 8:12],
                                             over(hot[:, :, g:g + 1], 4), ALU.mult)
                step(last)
                dve.tensor_tensor(both[:, :, :], first[:, :, :], second[:, :, :], ALU.add).then_inc(f["made"].sem, 1)
                dve.tensor_tensor(one[:, :, 6:7], one[:, :, 4:5], one[:, :, 3:4], ALU.subtract)\
                    .then_inc(f["weighted"].sem, 1)
                dve.wait_ge(f["turned"].sem, f["turned"].value(1))
                dve.tensor_copy(rank[:, :, :], core.bank(1, P, 16 * NT).rearrange("p (t e) -> p t e", e=16))
                step(dve.tensor_copy(count[:, :, :], core.bank(2, P, 16 * NT).rearrange("p (t e) -> p t e", e=16)))
                for t in range(NT):
                    step(dve.tensor_tensor(before[:, t + 1, :], before[:, t, :], count[:, t, :], ALU.add))
                step(dve.tensor_tensor(rank[:, :, :], rank[:, :, :], before[:, 0:NT, :], ALU.add))
                step(dve.tensor_scalar(tiles[:, :], before[:, NT, :], 0.0, None, ALU.is_gt))
                for m in range(1, NT):
                    step(dve.scalar_tensor_tensor(out=tiles[:, :], in0=before[:, NT, :], scalar=float(P * m),
                                                  in1=tiles[:, :], op0=ALU.is_gt, op1=ALU.add))
                step(dve.tensor_copy(ends[:, 0, :], tiles[:, :]))
                for n in range(4):
                    a, b, d = n % 2, (n + 1) % 2, 1 << n
                    dve.tensor_copy(ends[:, b, 0:d], ends[:, a, 0:d])
                    step(dve.tensor_tensor(ends[:, b, d:16], ends[:, a, d:16], ends[:, a, 0:16 - d], ALU.add))
                step(dve.tensor_tensor(start[:, 0, :], ends[:, 0, :], tiles[:, :], ALU.subtract))
                step(dve.tensor_scalar(start[:, 0, :], start[:, 0, :], float(P), -1.0, ALU.mult, ALU.add))
                step(dve.tensor_tensor(rank[:, :, :], rank[:, :, :], start[:, :, :].broadcast_to([P, NT, 16]), ALU.add))
                dve.tensor_tensor(first[:, :, :], first[:, :, :], rank[:, :, :], ALU.mult)
                step(dve.tensor_tensor(second[:, :, :], second[:, :, :], rank[:, :, :], ALU.mult))
                dve.tensor_reduce(pos[:, 0, :], first[:, :, :], AX.X, ALU.add)
                step(dve.tensor_reduce(pos[:, 1, :], second[:, :, :], AX.X, ALU.add))
                dve.tensor_copy(posu[:, :, :], pos[:, :, :]).then_inc(f["made"].sem, 1)
                step(dve.tensor_tensor(passed[:, :, :], ends[0:1, 0:1, :].broadcast_to([1, TILES, 16]),
                                       over(core.const("tile_no", 1)[:, 0:TILES].rearrange("p (t o) -> p t o", o=1), 16),
                                       ALU.is_le))
                step(dve.tensor_reduce(index[:, :, :], passed[:, :, :], AX.X, ALU.add))
                step(dve.tensor_scalar(index[:, :, :], index[:, :, :], 15.0, float(N_EXP * l), ALU.min, ALU.add))
                dve.tensor_copy(tile_expert[:, 0:TILES], index[:, :, :].rearrange("p t o -> p (t o)"))\
                    .then_inc(f["made"].sem, 1)
                dve.wait_ge(f["exped"].sem, f["exped"].value(2))
                step(dve.tensor_scalar(one[:, :, 5:6], one[:, :, 6:7], 1.0, None, ALU.add))
                step(dve.reciprocal(one[:, :, 7:8], one[:, :, 5:6]))
                step(dve.tensor_tensor(weight[:, 0, 0:NT], one[:, :, 7], one[:, :, 2], ALU.mult))
                dve.tensor_tensor(weight[:, 1, 0:NT], one[:, :, 6], weight[:, 0, 0:NT], ALU.mult)

            @block.scalar
            def _(act):
                for t in range(NT):
                    if t == 2:
                        act.wait_ge(f["weighted"].sem, f["weighted"].value(1))
                        act.activation(tmp4[:, :, :], tmp4[:, :, :], ACT.Exp).then_inc(f["exped"].sem, 1)
                    act.wait_ge(f["rows_turned"].sem, f["rows_turned"].value(t + 1))
                    if t >= 2:
                        act.wait_ge(f[f"rows_stored{t % 2}"].sem, f[f"rows_stored{t % 2}"].value(16 * (t // 2)))
                    act.activation(rows[:, t % 2, :], core.psum[:, 4 + 2 * (t % 2):6 + 2 * (t % 2), :]
                                   .rearrange("p a b -> p (a b)"), ACT.Copy).then_inc(f["copied"].sem, 1)
                act.wait_ge(f["weighted"].sem, f["weighted"].value(2))
                act.activation(one[:, :, 6:7], one[:, :, 6:7], ACT.Exp).then_inc(f["exped"].sem, 1)

            @block.sync
            def _(sp):
                sp.wait_ge(f["made"].sem, f["made"].value(1))
                sp.dma_start(dram["slot_token"][0:TILES * P, :].rearrange("(j p) o -> j (p o)", p=P), no_token[:, :])\
                    .then_inc(f["stored"].sem, 16)
                for t in range(NT):
                    sp.wait_ge(f["copied"].sem, f["copied"].value(t + 1))
                    sp.dma_start(dram["h_rows"][t * P:(t + 1) * P, :], rows[:, t % 2, :])\
                        .then_inc(f[f"rows_stored{t % 2}"].sem, 16)
                for z in range(2):
                    sp.wait_ge(f[f"rows_stored{z}"].sem, f[f"rows_stored{z}"].value(16 * (NT // 2)))

            @block.gpsimd
            def _(pool):
                pool.wait_ge(f["stored"].sem, f["stored"].value(16))
                pool.wait_ge(f["made"].sem, f["made"].value(3))
                for z in range(2):
                    for t in range(NT):
                        pool.indirect_dma_start(dram["slot_token"][0:TILES * P, :],
                                                bass.IndirectOffsetOnAxis(ap=posu[:, z, t:t + 1], axis=0),
                                                token[:, t:t + 1], None).then_inc(f["scattered"].sem, 16)
                pool.wait_ge(f["scattered"].sem, f["scattered"].value(32 * NT))
    for k, n in (("products_done", 1), ("made", 4), ("turned", 1), ("weighted", 2), ("exped", 2), ("stored", 16),
                 ("rows_turned", NT), ("copied", NT), ("rows_stored0", 16 * (NT // 2)), ("rows_stored1", 16 * (NT // 2)),
                 ("scattered", 32 * NT)):
        f[k].advance(n)


def experts(core, l, parts):
    nc, f, dram = core.nc, core.flags, core.dram
    tokens = sum(tn for _, tn in parts)
    NT = tokens // P
    TILES = expert_tiles(tokens)
    U = 3
    ROUNDS = (TILES + U - 1) // U

    def round_of(i, last=False):
        return [(i, u) for u in range(TILES - U * (ROUNDS - 1) if last else U)]

    def at(name, i, u, n=0):
        return i * U + f[name].value(u + n)

    def loaded(name, i, u, n=0):
        return i * 16 + f[f"{name}{(u + n) % U}"].value(16 * (1 + (u + n) // U))

    with ExitStack() as stack:
        def sb(name, shape, dtype=F32):
            return stack.enter_context(nc.sbuf_tensor(f"{name}{l}", shape, dtype))
        weight = sb("pair_weight", [P, 2, NT])
        posu = sb("pair_slot", [P, 2, NT], U32)
        tile_expert = sb("tile_expert", [1, TILES], I32)
        route(core, l, tokens, weight, posu, tile_expert)

        with ExitStack() as inner:
            def tile_sb(name, shape, dtype=F32):
                return inner.enter_context(nc.sbuf_tensor(f"{name}{l}", shape, dtype))
            GU = tile_sb("gate_up_w", [P, U, 4096])
            DN = tile_sb("down_w", [P, U, 2048])
            IDX = tile_sb("slot_tokens", [P, U], U32)
            HR = tile_sb("h_gathered", [P, U, D])
            SL = tile_sb("silu_a", [P, 256])
            HID = tile_sb("hid", [P, 256])
            HIDT = tile_sb("hid_t", [P, 256])
            h_flat = core.H[:, :, :].rearrange("p k t -> p (k t)")
            HT = [h_flat[:, n * D:(n + 1) * D] for n in range(U)]
            Y = [h_flat[:, (U + n) * D:(U + n + 1) * D] for n in range(U)]

            with nc.Block(f"experts{l}") as block:
                @block.sync
                def _(sp):
                    def load(i, u, free):
                        e = sp.value_load(tile_expert[0:1, bass.ds(i * U + u, 1)], min_val=0, max_val=2 * N_EXP - 1)
                        if free:
                            sp.wait_ge(f["gate_up"].sem, at("gate_up", i, u, 1 - U))
                        sp.dma_start(GU[:, u, :], dram["experts"][bass.ds(e, 1), :, 0:4096]
                                     .rearrange("e p n -> p (e n)")).then_inc(f[f"gu_loaded{u}"].sem, 16)
                        if free:
                            sp.wait_ge(f["down_done"].sem, at("down_done", i, u, 1 - U))
                        sp.dma_start(DN[:, u, :], dram["experts"][bass.ds(e, 1), :, 4096:6144]
                                     .rearrange("e p n -> p (e n)")).then_inc(f[f"dn_loaded{u}"].sem, 16)

                    def store_y(i, u, n):
                        k = (u + n) % U
                        for half in ("y_v", "y_s"):
                            sp.wait_ge(f[half].sem, at(half, i, u, n + 1))
                        sp.dma_start(dram["y_rows"][bass.ds(i * (U * P) + (u + n) * P, P), :], Y[k])\
                            .then_inc(f[f"y_stored{k}"].sem, 16)

                    for i, u in round_of(0):
                        load(i, u, False)
                    with sp.Fori(1, ROUNDS - 1) as r:
                        for i, u in round_of(r):
                            load(i, u, True)
                            store_y(i, u, -U)
                    for i, u in round_of(ROUNDS - 1, True):
                        load(i, u, True)
                        store_y(i, u, -U)
                    for n in range(1 - U, 1):
                        store_y(i, u, n)
                    for n in range(1 - U, 1):
                        sp.wait_ge(f[f"y_stored{(u + n) % U}"].sem, loaded("y_stored", i, u, n))

                @block.gpsimd
                def _(pool):
                    def load_index(i, u, n=0):
                        k = (u + n) % U
                        pool.dma_start(IDX[:, k:k + 1], dram["slot_token"][bass.ds(i * (U * P) + (u + n) * P, P), :])\
                            .then_inc(f[f"idx_loaded{k}"].sem, 16)

                    def gather(i, u, first=False, last=False):
                        pool.wait_ge(f[f"idx_loaded{u}"].sem, loaded("idx_loaded", i, u))
                        if not first:
                            pool.wait_ge(f["rows_turned"].sem, at("rows_turned", i, u, 1 - U))
                        if not (first and u + 1 < U):
                            pool.wait_ge(f[f"gathered{(u + 1) % U}"].sem, loaded("gathered", i, u, 1 - U))
                        if not last:
                            load_index(i, u, 1)
                        pool.indirect_dma_start(HR[:, u, :], None, dram["h_rows"][0:tokens, :],
                                                bass.IndirectOffsetOnAxis(ap=IDX[:, u:u + 1], axis=0))\
                            .then_inc(f[f"gathered{u}"].sem, 16)

                    load_index(0, 0)
                    for i, u in round_of(0):
                        gather(i, u, first=True)
                    with pool.Fori(1, ROUNDS - 1) as r:
                        for i, u in round_of(r):
                            gather(i, u)
                    tail = round_of(ROUNDS - 1, True)
                    for i, u in tail:
                        gather(i, u, last=(i, u) == tail[-1])

                @block.tensor
                def _(pe):
                    def turn_rows(i, u, n, first=False):
                        k = (u + n) % U
                        pe.wait_ge(f[f"gathered{k}"].sem, loaded("gathered", i, u, n))
                        if not first:
                            for half in ("turned_v", "turned_s"):
                                pe.wait_ge(f[half].sem, at(half, i, u, n))
                        for m in range(KD):
                            last = pe.transpose(core.bank(m // 4, P, P, P * (m % 4)), HR[:, k, m * P:(m + 1) * P],
                                                core.const("ident"))
                        last.then_inc(f["rows_turned"].sem, 1)

                    def turn_hidden(i, u, n, second=False):
                        pe.wait_ge(f["hid_ready"].sem, at("hid_ready", i, u, n + 1))
                        if not second:
                            pe.wait_ge(f["hidT_ready"].sem, at("hidT_ready", i, u, n))
                        for m in range(2):
                            last = pe.transpose(core.bank(3, P, P, P * m), HID[:, m * P:(m + 1) * P], core.const("ident"))
                        last.then_inc(f["hid_turned"].sem, 1)

                    def gate_up(i, u):
                        pe.wait_ge(f[f"gu_loaded{u}"].sem, loaded("gu_loaded", i, u))
                        for half in ("turned_v", "turned_s"):
                            pe.wait_ge(f[half].sem, at(half, i, u, 1))
                        products(pe, core.bank(2), [(HT[u][:, m * P:(m + 1) * P], GU[:, u, m * 512:(m + 1) * 512])
                                                    for m in range(KD)]).then_inc(f["gate_up"].sem, 1)

                    def down(i, u, n, second=False):
                        k = (u + n) % U
                        pe.wait_ge(f[f"dn_loaded{k}"].sem, loaded("dn_loaded", i, u, n))
                        pe.wait_ge(f["hidT_ready"].sem, at("hidT_ready", i, u, n + 1))
                        if not second:
                            for half in ("y_v", "y_s"):
                                pe.wait_ge(f[half].sem, at(half, i, u, n))
                        for half in range(2):
                            last = products(pe, core.bank(4 + half),
                                            [(HIDT[:, m * P:(m + 1) * P],
                                              DN[:, k, 1024 * m + 512 * half:1024 * m + 512 * half + 512])
                                             for m in range(2)])
                        last.then_inc(f["down_done"].sem, 1)

                    def tile(i, u, number=None, last=False):
                        if not last:
                            turn_rows(i, u, 1)
                        if number != 0:
                            turn_hidden(i, u, -1, second=number == 1)
                        gate_up(i, u)
                        if number != 0:
                            down(i, u, -1, second=number == 1)

                    turn_rows(0, 0, 0, first=True)
                    for i, u in round_of(0):
                        tile(i, u, number=u)
                    with pe.Fori(1, ROUNDS - 1) as r:
                        for i, u in round_of(r):
                            tile(i, u)
                    tail = round_of(ROUNDS - 1, True)
                    for i, u in tail:
                        tile(i, u, last=(i, u) == tail[-1])
                    turn_hidden(i, u, 0)
                    down(i, u, 0)

                @block.vector
                def _(dve):
                    def turned(i, u, n, first=False):
                        k = (u + n) % U
                        dve.wait_ge(f["rows_turned"].sem, at("rows_turned", i, u, n + 1))
                        if not first:
                            dve.wait_ge(f["gate_up"].sem, at("gate_up", i, u, n + 1 - U))
                        dve.tensor_copy(HT[k][:, 0:512], core.bank(0)).then_inc(f["turned_v"].sem, 1)

                    def hidden(i, u, first=False):
                        dve.wait_ge(f["gate_up"].sem, at("gate_up", i, u, 1))
                        dve.wait_ge(f["silued"].sem, at("silued", i, u, 1))
                        if not first:
                            dve.wait_ge(f["hid_turned"].sem, at("hid_turned", i, u))
                        dve.tensor_tensor(HID[:, :], SL[:, :], core.bank(2, P, 256, 256), ALU.mult)\
                            .then_inc(f["hid_ready"].sem, 1)

                    def hidden_turned(i, u, n, second=False):
                        dve.wait_ge(f["hid_turned"].sem, at("hid_turned", i, u, n + 1))
                        if not second:
                            dve.wait_ge(f["down_done"].sem, at("down_done", i, u, n))
                        dve.tensor_copy(HIDT[:, :], core.bank(3, P, 256)).then_inc(f["hidT_ready"].sem, 1)

                    def y_half(i, u, n, first=False):
                        k = (u + n) % U
                        dve.wait_ge(f["down_done"].sem, at("down_done", i, u, n + 1))
                        if not first:
                            dve.wait_ge(f[f"y_stored{k}"].sem, loaded("y_stored", i, u, n - U))
                        dve.tensor_copy(Y[k][:, 0:512], core.bank(4)).then_inc(f["y_v"].sem, 1)

                    def tile(i, u, number=None, last=False):
                        if not last:
                            turned(i, u, 1, first=number in (0, 1))
                        if number != 0:
                            hidden_turned(i, u, -1, second=number == 1)
                        hidden(i, u, first=number == 0)
                        if number != 0:
                            y_half(i, u, -1, first=number in (1, 2, 3))

                    turned(0, 0, 0, first=True)
                    for i, u in round_of(0) + round_of(1):
                        tile(i, u, number=U * i + u)
                    with dve.Fori(2, ROUNDS - 1) as r:
                        for i, u in round_of(r):
                            tile(i, u)
                    tail = round_of(ROUNDS - 1, True)
                    for i, u in tail:
                        tile(i, u, last=(i, u) == tail[-1])
                    hidden_turned(i, u, 0)
                    y_half(i, u, 0)

                @block.scalar
                def _(act):
                    def turned(i, u, n, first=False):
                        k = (u + n) % U
                        act.wait_ge(f["rows_turned"].sem, at("rows_turned", i, u, n + 1))
                        if not first:
                            act.wait_ge(f["gate_up"].sem, at("gate_up", i, u, n + 1 - U))
                        act.activation(HT[k][:, 512:1024], core.bank(1), ACT.Copy).then_inc(f["turned_s"].sem, 1)

                    def y_half(i, u, n, first=False):
                        k = (u + n) % U
                        act.wait_ge(f["down_done"].sem, at("down_done", i, u, n + 1))
                        if not first:
                            act.wait_ge(f[f"y_stored{k}"].sem, loaded("y_stored", i, u, n - U))
                        act.activation(Y[k][:, 512:1024], core.bank(5), ACT.Copy).then_inc(f["y_s"].sem, 1)

                    def tile(i, u, number=None, last=False):
                        if not last:
                            turned(i, u, 1, first=number in (0, 1))
                        act.wait_ge(f["gate_up"].sem, at("gate_up", i, u, 1))
                        if number != 0:
                            act.wait_ge(f["hid_ready"].sem, at("hid_ready", i, u))
                        act.activation(SL[:, :], core.bank(2, P, 256), ACT.Silu).then_inc(f["silued"].sem, 1)
                        if number != 0:
                            y_half(i, u, -1, first=number in (1, 2, 3))

                    turned(0, 0, 0, first=True)
                    for i, u in round_of(0) + round_of(1):
                        tile(i, u, number=U * i + u)
                    with act.Fori(2, ROUNDS - 1) as r:
                        for i, u in round_of(r):
                            tile(i, u)
                    tail = round_of(ROUNDS - 1, True)
                    for i, u in tail:
                        tile(i, u, last=(i, u) == tail[-1])
                    y_half(i, u, 0)
        for name in ("rows_turned", "turned_v", "turned_s", "gate_up", "silued", "hid_ready", "hid_turned",
                     "hidT_ready", "down_done", "y_v", "y_s"):
            f[name].advance(TILES)
        for name in ("gu_loaded", "dn_loaded", "idx_loaded", "gathered", "y_stored"):
            for u in range(U):
                f[f"{name}{u}"].advance(16 * ((TILES - u + U - 1) // U))
        combine_pairs(core, l, parts, weight, posu)


def combine_pairs(core, l, parts, weight, posu):
    nc, f, dram = core.nc, core.flags, core.dram
    tokens = sum(tn for _, tn in parts)
    NT = tokens // P
    TILES = expert_tiles(tokens)
    with nc.sbuf_tensor(f"y_pair{l}", [P, 2, 2, D], F32) as YP, nc.sbuf_tensor(f"y_sum{l}", [P, 2, D], F32) as YS, \
         nc.Block(f"combine{l}") as block:
        @block.gpsimd
        def _(pool):
            for t in range(NT):
                if t >= 2:
                    pool.wait_ge(f["made"].sem, f["made"].value(t - 1))
                for z in range(2):
                    pool.indirect_dma_start(YP[:, t % 2, z, :], None, dram["y_rows"][0:TILES * P, :],
                                            bass.IndirectOffsetOnAxis(ap=posu[:, z, t:t + 1], axis=0))\
                        .then_inc(f[f"pair{t % 2}{z}"].sem, 16)

        @block.tensor
        def _(pe):
            for t in range(NT):
                pe.wait_ge(f["made"].sem, f["made"].value(t + 1))
                if t >= 2:
                    pe.wait_ge(f["added"].sem, f["added"].value(t - 1))
                for k in range(KD):
                    last = pe.transpose(core.bank(2 * (t % 2) + k // 4, P, P, P * (k % 4)), YS[:, t % 2, k * P:(k + 1) * P],
                                        core.const("ident"))
                last.then_inc(f["turned"].sem, 1)

        @block.vector
        def _(dve):
            def weighted_sum(t):
                dve.wait_ge(f[f"pair{t % 2}0"].sem, f[f"pair{t % 2}0"].value(16 * (t // 2 + 1)))
                dve.wait_ge(f[f"pair{t % 2}1"].sem, f[f"pair{t % 2}1"].value(16 * (t // 2 + 1)))
                if t >= 2:
                    dve.wait_ge(f["turned"].sem, f["turned"].value(t - 1))
                core.v_chain(dve, dve.tensor_scalar(YS[:, t % 2, :], YP[:, t % 2, 0, :], weight[:, 0, t:t + 1], None,
                                                    ALU.mult))
                dve.scalar_tensor_tensor(out=YS[:, t % 2, :], in0=YP[:, t % 2, 1, :], scalar=weight[:, 1, t:t + 1],
                                         in1=YS[:, t % 2, :], op0=ALU.mult, op1=ALU.add).then_inc(f["made"].sem, 1)

            weighted_sum(0)
            for t in range(NT):
                if t + 1 < NT:
                    weighted_sum(t + 1)
                dve.wait_ge(f["turned"].sem, f["turned"].value(t + 1))
                p = 0 if t * P < S else 1
                for m in range(KD):
                    last = dve.scalar_tensor_tensor(
                        out=core.X[:, m, t * P:(t + 1) * P], in0=core.bank(2 * (t % 2) + m // 4, P, P, P * (m % 4)),
                        scalar=core.mods[:, l, 40 + m, p:p + 1], in1=core.X[:, m, t * P:(t + 1) * P],
                        op0=ALU.mult, op1=ALU.add)
                last.then_inc(f["added"].sem, 1)
    for name in ("made", "turned", "added"):
        f[name].advance(NT)
    for u in range(2):
        for z in range(2):
            f[f"pair{u}{z}"].advance(16 * (NT // 2))


def store(core):
    nc, f, dram = core.nc, core.flags, core.dram
    with nc.Block("store") as block:
        @block.sync
        def _(sp):
            sp.dma_start(dram["outT"].rearrange("(k p) t -> p k t", p=P), core.X[:, :, 0:S]).then_inc(f["out_stored"].sem, 16)
            sp.wait_ge(f["out_stored"].sem, 16)


def build_program(nc, dram, stages=99):
    with ExitStack() as ctx:
        core = Core(nc, ctx, dram)
        parts = [LAT, CON]

        def mix_ffn(l, tokens_of):
            modulated_norm(core, f"norm_f{l}", l, 1, tokens_of)
            experts(core, l, tokens_of)

        def first():
            with nc.sbuf_tensor("table_ac", [12, TABLE], F32) as core.table_ac, \
                 nc.sbuf_tensor("table_b", [8, TABLE], F32) as core.table_b:
                derive(core)
                first_block(core)
        program = [lambda: load_inputs(core), first,
                   lambda: modulation(core), lambda: even_layer(core), lambda: mix_ffn(0, parts),
                   lambda: odd_layer(core), lambda: mix_ffn(1, [LAT]), lambda: store(core)]
        for stage in program[0:stages]:
            stage()


def shape_constants():
    con = {}
    con["ident"] = np.eye(P)
    con["ones"] = np.ones((P, P))
    con["blocks"] = np.kron(np.eye(2), np.ones((HD, HD)))
    rot = np.zeros((P, P))
    for b in range(0, P, 32):
        for d in range(16):
            rot[b + 16 + d, b + d] = -1.0
            rot[b + d, b + 16 + d] = 1.0
    con["rot"] = rot
    s, t = np.arange(P)[:, None], np.arange(P)[None, :]
    con["causal_st"] = s <= t
    con["anti_st"] = s >= t
    pos = np.arange(S)
    ends = np.arange(NC_CMP) * 16 + 31
    con["cmask"] = np.where(ends[None, :] <= pos[:, None], 0.0, NEG).reshape(4, P, NC_CMP).transpose(1, 0, 2)\
        .reshape(P, -1)
    con["token_no"] = s + P * np.arange(T // P)[None, :]
    con["tile_no"] = np.tile(np.arange(32)[None, :], (P, 1))
    packed = np.concatenate([np.asarray(con[n], np.float32).reshape(P, -1) for n, _ in CONSTS], 1)
    n = np.maximum(511 - np.arange(TABLE), 0)
    large = 16 + (np.log(np.maximum(n, 1).astype(np.float32) / np.float32(16)) / np.float32(math.log(128 / 16))
                  * np.float32(16)).astype(np.int32)
    bucket = np.where(n < 16, n, np.minimum(large, 31))
    onehot = (bucket[None, :] == np.arange(32)[:, None]).astype(np.float32)
    row, col = np.arange(S) // 64, np.arange(S) % 64
    inv = np.float32(10000.0) ** (-np.arange(0, 32, 2, dtype=np.float32) / np.float32(32))
    ang = np.stack([row[:, None].astype(np.float32) * inv, col[:, None].astype(np.float32) * inv], 1)
    ang = np.tile(np.repeat(ang[:, :, None, :], 2, 2).reshape(S, HD).T, (2, 1))
    trig = np.stack([np.cos(ang), np.sin(ang)], 1).astype(np.float32)
    near_before = np.where(t >= s, 0.0, NEG)
    near_behind = np.where(t <= s, 0.0, NEG)
    zero = np.zeros((P, P))
    window = np.concatenate([zero, zero, near_before, zero, near_behind, zero, zero, zero, near_behind], 1)
    return packed, onehot, trig, window.astype(np.float32)


def pairs(w, heads, axis):
    order = np.arange(heads).reshape(2, heads // 2).T.reshape(-1)
    w = np.moveaxis(np.asarray(w), axis, -1)
    w = w.reshape(w.shape[:-1] + (heads, HD))[..., order, :].reshape(w.shape)
    return np.moveaxis(w, -1, axis)


def laid_out(a):
    D1 = {k: np.asarray(v) for k, v in a.items()}
    w = D1["w_in"][0]
    sizes = [512, 512, 512, 512, 128, 128, 512, 768, 24, 3072]
    at = np.concatenate([[0], np.cumsum(sizes)])
    aq, ak, av, bq, bk, bv, cq, ckv, cg, mg = (w[:, at[i]:at[i + 1]] for i in range(10))
    kv = [ckv[:, 128 * i:128 * i + 128] for i in range(6)]
    ev = D1["ev_w_in_2"][0]
    at = np.concatenate([[0], np.cumsum([256, 256, 512, 512, 32, 512, 128, 128])])
    gq, gk, gv, gr, lr, eq, ek, evv = (ev[:, at[i]:at[i + 1]] for i in range(8))
    od = D1["od_w_in_2"][0]
    ev_out = D1["ev_w_out_2"][0]
    ev_out = np.concatenate([ev_out[0:512], pairs(ev_out[512:1024], 8, 0)], 0)
    od_out = pairs(D1["od_w_out_2"][0], 16, 0)
    odq = pairs(od[:, 0:1024], 16, 1)
    wb = D1["w_branch"][0]
    wb = [wb[0], pairs(wb[1], 8, 0), pairs(wb[2], 8, 0)]
    src = {"proj0": aq, "proj1": ak, "proj2": pairs(bq, 8, 1), "proj3": pairs(cq, 8, 1),
           "proj4": np.concatenate([bk, kv[2], kv[4], kv[0]], 1), "proj5": np.concatenate([kv[1], bv, kv[3], kv[5]], 1),
           "proj6": av, "proj7": cg, "cmp0": D1["cmp_w1"][0, 0], "cmp1": D1["cmp_w1"][0, 1],
           "ev0": pairs(eq, 8, 1), "ev1": np.concatenate([ek, evv, lr], 1), "ev2": np.concatenate([gq, gk], 1),
           "ev3": gr, "ev4": gv, "od0": odq[:, 0:512], "od1": odq[:, 512:1024], "od2": od[:, 1024:1280]}
    for n in range(3):
        src[f"branch{n}"] = wb[n]
        for h in range(2):
            src[f"mg{n}_{h}"] = mg[:, 1024 * n + 512 * h:1024 * n + 512 * h + 512]
    for i in range(2):
        c = slice(512 * i, 512 * i + 512)
        src[f"out{i}"], src[f"ev_out{i}"], src[f"od_out{i}"] = D1["w_out"][0][:, c], ev_out[:, c], od_out[:, c]
    for i in range(8):
        src[f"up{i}"] = D1["w_up"][0][:, 512 * i:512 * i + 512]
        src[f"down{i}"] = D1["w_down"][0][:, P * i:P * i + P]
    experts = np.zeros((2 * N_EXP, P, 6144), np.float32)
    for l in range(2):
        for i in range(12):
            src[f"mod{l}_{i}"] = D1["mod_w_2"][l][:, 512 * i:512 * i + 512]
        gate, up, down = (D1[n][l].reshape((N_EXP,) + D1[n].shape[3:]) for n in
                          ("exp_w_gate_2", "exp_w_up_2", "exp_w_down_2"))
        for e in range(N_EXP):
            gate_up = np.concatenate([gate[e], up[e]], 1)
            experts[N_EXP * l + e] = np.concatenate(
                [gate_up.reshape(KD, P, 512).transpose(1, 0, 2).reshape(P, 4096),
                 down[e].reshape(2, P, D).transpose(1, 0, 2).reshape(P, 2048)], 1)
    plan = plan_weights()
    weights = np.zeros((len(plan), P, 4096), np.float32)
    for c, (name, kt, n) in enumerate(plan):
        weights[c, :, 0:kt * n] = src[name].reshape(kt, P, n).transpose(1, 0, 2).reshape(P, kt * n)

    def column(v):
        return v.reshape(-1, P).T

    def twice(v):
        return np.tile(v, 2)[:, None]

    def rows(v):
        return np.tile(v.reshape(1, -1), (P, 1))

    lam = np.zeros((P, 4), np.float32)
    lam[0:HD] = D1["diff_lambda"][0].T
    par = {
        "norm_mix": column(D1["norm_mix"][0]), "norm_mlp": column(D1["norm_mlp"][0]),
        "qk_gain": np.concatenate([twice(D1["qk_gain"][0, i]) for i in range(8)], 1),
        "subln": D1["diff_subln"][0][:, None], "mod_b": column(D1["mod_b_2"].reshape(-1)),
        "norm_mix_2": column(D1["norm_mix_2"].reshape(-1)), "norm_ffn_2": column(D1["norm_ffn_2"].reshape(-1)),
        "gla_b": column(D1["gla_gate_b_2"][0].reshape(-1)), "gla_norm": D1["gla_out_norm_2"][0][:, None],
        "att_q": twice(D1["att_q_norm_2"][0]), "att_k": twice(D1["att_k_norm_2"][0]),
        "swa_q": twice(D1["swa_q_norm_2"][0]), "swa_k": twice(D1["swa_k_norm_2"][0]),
        "c": np.stack([column(D1["c_2"][0]), column(D1["c_ctx_2"])], 2).reshape(P, 16),
        "sinks": rows(D1["sinks"][0]), "swa_sink": rows(D1["swa_sink_2"][0]),
        "router_b": rows(np.concatenate([D1["router_group_b_2"], D1["router_expert_b_2"]], 1)),
        "cmp_pos": D1["cmp_pos"][0].reshape(2, 16, P).transpose(2, 0, 1).reshape(P, 32),
        "lambda": lam, "valid31": (np.arange(P) >= 31)[:, None].astype(np.float32),
    }
    router = np.concatenate([D1["router_group_w_2"], D1["router_expert_w_2"]], 2)
    gate_w = np.zeros((32, 2, 256), np.float32)
    for z in range(2):
        gate_w[16 * z:16 * z + 16, z] = D1["gla_gate_w_2"][0, z]
    rel = D1["rel_bias"]
    packed, onehot, trig, window = shape_constants()
    return {
        "xT": D1["x"][0].T, "ctxT": D1["ctx_2"][0].T, "weights": weights, "experts": experts,
        "par": np.concatenate([par[n].reshape(P, -1) for n, _ in PARAMS], 1), "con": packed,
        "router": router.reshape(2, KD, P, 20).transpose(2, 0, 1, 3), "gate_w": gate_w,
        "rel": np.concatenate([rel[:, 0:4], rel[:, 12:20], rel[:, 4:12]], 1), "onehot": onehot,
        "trig": trig, "window": window, "cmp_w2": D1["cmp_w2"][0],
    }


def kernel(**inputs):
    import concourse.bacc as _bacc
    from concourse.bass_utils import run_bass_kernel_spmd as _run

    nc = _bacc.Bacc("TRN2", target_bir_lowering=False, num_devices=1)
    arrays, dram = {}, {}
    for name, a in laid_out(inputs).items():
        a = np.ascontiguousarray(a)
        arrays[f"in_{name}"] = a
        dram[name] = nc.dram_tensor(f"in_{name}", a.shape, mybir.dt.from_np(a.dtype), kind="ExternalInput").ap()
    dram["bias"] = nc.dram_tensor("bias_tables", [20, P, TABLE], F32, kind="Internal").ap()
    dram["h_rows"] = nc.dram_tensor("h_rows", [T, D], F32, kind="Internal").ap()
    dram["slot_token"] = nc.dram_tensor("slot_token", [P * expert_tiles(T), 1], U32, kind="Internal").ap()
    dram["y_rows"] = nc.dram_tensor("y_rows", [P * expert_tiles(T), D], F32, kind="Internal").ap()
    dram["outT"] = nc.dram_tensor("outT", [D, S], F32, kind="ExternalOutput").ap()
    build_program(nc, dram)
    r = _run(nc, [arrays], core_ids=[0])
    return np.ascontiguousarray(r.results[0]["outT"].T)[None]
```

```python
import math
from contextlib import ExitStack

import numpy as np
import concourse.bass as bass
from concourse import mybir

P = 128
D = 1024
KD = D // P
S = 512
CTX = 256
T = S + CTX
HD = 64
D_FF = 4096
EPS = 1e-6
NEG = -1e30
LAM_INIT = 0.8 - 0.6 * math.exp(-0.3 * 0)
NC_CMP = (S - 32) // 16 + 1
TABLE = 640
MASKED_FROM = 512
WINDOW_B = 128
N_EXP = 16
U = 3
RING = 4
MODS_BESIDE_UP = [[0], [1], [2, 3], [4], [5, 6], [7], [8, 9], [10]]
MODS_BESIDE_DOWN = [[11, 12], [13, 14], [15, 16], [17], [18, 19], [20], [21, 22], [23]]
LAT = (0, S)
CON = (S, CTX)

F32 = mybir.dt.float32
U32 = mybir.dt.uint32
I32 = mybir.dt.int32
ALU = mybir.AluOpType
ACT = mybir.ActivationFunctionType
AX = mybir.AxisListType

PARAMS = [("norm_mix", 8), ("norm_mlp", 8), ("qk_gain", 8), ("subln", 1), ("mod_b", 2 * 48), ("norm_mix_2", 16),
          ("norm_ffn_2", 16), ("gla_b", 4), ("gla_norm", 1), ("att_q", 1), ("att_k", 1), ("swa_q", 1), ("swa_k", 1),
          ("c", 16), ("sinks", 8), ("swa_sink", 16), ("router_b", 2 * 20), ("cmp_pos", 32), ("lambda", 4),
          ("valid31", 1)]
CONSTS = [("ident", P), ("ones", P), ("blocks", P), ("rot", P), ("causal_st", P), ("anti_st", P), ("cmask", 4 * NC_CMP),
          ("token_no", T // P), ("tile_no", 32), ("pick_row", 4)]


def offsets(spec):
    at, out = 0, {}
    for name, width in spec:
        out[name] = (at, at + width)
        at += width
    return out, at


PARAM_AT, N_PARAM = offsets(PARAMS)
CONST_AT, N_CONST = offsets(CONSTS)


class Flag:

    def __init__(self, nc, name):
        self.sem = nc.alloc_semaphore(name)
        self.base = 0

    def value(self, n):
        return self.base + n

    def advance(self, n):
        self.base += n


class Chain:

    def __init__(self, flag):
        self.flag = flag

    def __call__(self, eng, ins):
        ins.then_inc(self.flag.sem, 1)
        self.flag.advance(1)
        eng.wait_ge(self.flag.sem, self.flag.base)


class Core:

    def __init__(self, nc, ctx, dram):
        self.nc = nc
        self.ctx = ctx
        self.dram = dram
        sb = self.sb
        self.X = sb("X", [P, KD, T])
        self.H = sb("H", [P, KD, T])
        self.ring = sb("ring", [P, RING, 4096])
        self.par = sb("par", [P, N_PARAM])
        self.con = sb("con", [P, N_CONST])
        self.eps = sb("eps", [P, 1])
        self.mods = sb("mods", [P, 2, 48, 2])
        self.mod_gain = sb("mod_gain", [P, 2, 2, KD, 2])
        self.silu_c = sb("silu_c", [P, 16])
        self.derived = sb("derived", [P, N_DERIVED])
        self.router = sb("router", [P, 2, KD, 20])
        self.psum = ctx.enter_context(nc.psum_tensor("banks", [P, 8, 512], F32))
        self.flags = {}
        for name in ("products_done", "evacuated_v", "evacuated_s", "squared", "summed", "rooted", "normed",
                     "scored", "biased", "exped", "weighted", "turned", "copied", "attended", "emptied",
                     "v_step", "s_step", "p_step", "misc_loaded", "bias_loaded0", "bias_loaded1", "hid_ready", "gated", "silued",
                     "down_done", "added", "out_stored", "stored", "made", "tables_stored",
                     "rows_turned", "rows_stored0", "rows_stored1", "scattered", "turned_v", "turned_s", "gate_up",
                     "hid_turned", "hidT_ready", "y_v", "y_s", "experts_ready", "late_loaded", "mod_scaled", "mod_summed", "mod_copied",
                     "mod_stored0", "mod_stored1", "pair00", "pair01", "pair10", "pair11",
                     *(f"{name}{u}" for name in ("gu_loaded", "dn_loaded", "idx_loaded", "gathered", "y_stored")
                       for u in range(U))):
            self.flags[name] = Flag(nc, name)
        self.w_loaded = [Flag(nc, f"w_loaded{i}") for i in range(RING)]
        self.v_chain, self.s_chain, self.p_chain = (Chain(self.flags[n]) for n in ("v_step", "s_step", "p_step"))
        self.plan_list = plan_weights()
        self.plan = {name: (c, kt, n) for c, (name, kt, n) in enumerate(self.plan_list)}
        self.issued = 0
        self.used_up = {}
        self.consumed = 0
        self.mods_done = 0
        self.lent = 0

    def sb(self, name, shape):
        return self.ctx.enter_context(self.nc.sbuf_tensor(name, shape, F32))

    def bank(self, n, rows=P, cols=512, at=0):
        return self.psum[0:rows, n, at:at + cols]

    def param(self, name, a=0, n=None, rows=P):
        lo, hi = PARAM_AT[name]
        return self.par[0:rows, lo + a:hi if n is None else lo + a + n]

    def const(self, name, rows=P, at=0):
        lo, hi = CONST_AT[name]
        return self.con[at:at + rows, lo:hi]

    def chunk(self, name):
        c, kt, n = self.plan[name]
        return c, self.ring[:, c % RING, 0:kt * n].rearrange("p (k n) -> p k n", k=kt)

    def feed(self, sync, consumed):
        while self.issued < min(consumed + RING - self.lent, len(self.plan_list)):
            c = self.issued
            _, kt, n = self.plan_list[c]
            if c >= RING:
                flag, value = self.used_up[c - RING]
                sync.wait_ge(flag.sem, value)
            sync.dma_start(self.ring[:, c % RING, 0:kt * n], self.dram["weights"][c, :, 0:kt * n])\
                .then_inc(self.w_loaded[c % RING].sem, 16)
            self.issued += 1

    def use_up(self, jobs):
        done = self.flags["products_done"]
        for n, job in enumerate(jobs):
            if job[1]:
                self.used_up[job[0]] = (done, done.value(n + 1))
        return self.consumed + sum(1 for j in jobs if j[1])

    def await_chunk(self, pe, c):
        pe.wait_ge(self.w_loaded[c % RING].sem, 16 * (c // RING + 1))


def products(pe, out, pairs):
    for n, (lhsT, rhs) in enumerate(pairs):
        last = pe.matmul(out, lhsT, rhs, start=n == 0, stop=n == len(pairs) - 1)
    return last


def dense(core, name, jobs, finish, both=True, beside=None, loads=None):
    nc, f = core.nc, core.flags
    lanes = 2 if both else 1
    banks = 8 if beside is None else 7
    used = core.use_up(jobs)
    ends = [n for n, job in enumerate(jobs) if job[1]]
    before, after = {}, {}
    if beside is not None:
        done = core.mods_done
        for c, mods in enumerate(beside):
            start = ends[c - 1] + 1 if c else 0
            for z, m in enumerate(mods):
                assert m == done
                before.setdefault(min(start + z * lanes, ends[c] - ends[c] % lanes), []).append(m)
                after.setdefault(ends[c], []).append(m)
                core.used_up[core.plan[f"mod{m}"][0]] = (f["mod_scaled"], f["mod_scaled"].value(m + 1))
                done += 1
        used += done - core.mods_done
        core.mods_done = done

    with ExitStack() as stack:
        if beside is not None:
            scaled = stack.enter_context(nc.sbuf_tensor(name + "_scaled", [P, 2, 2, 512], F32))
            rows = stack.enter_context(nc.sbuf_tensor(name + "_mod_rows", [2, 2, 512], F32))
        block = stack.enter_context(nc.Block(name))

        @block.sync
        def _(sp):
            if loads is not None:
                loads(sp)
            core.feed(sp, used)

        @block.tensor
        def _(pe):
            seen = None
            for n, (chunk, release, rows_n, cols, pairs) in enumerate(jobs):
                if chunk is not None and chunk != seen:
                    core.await_chunk(pe, chunk)
                    seen = chunk
                if n >= banks:
                    old = n - banks
                    flag = f["evacuated_s"] if both and old % 2 else f["evacuated_v"]
                    pe.wait_ge(flag.sem, flag.value(old // lanes + 1))
                last = products(pe, core.bank(n % banks, rows_n, cols), pairs)
                last.then_inc(f["products_done"].sem, 1)
                for m in after.get(n, ()):
                    pe.wait_ge(f["mod_scaled"].sem, f["mod_scaled"].value(m + 1))
                    if m:
                        pe.wait_ge(f["mod_copied"].sem, f["mod_copied"].value(m))
                    products(pe, core.bank(7, 2), [(core.const("pick_row")[:, 2 * v:2 * v + 2], scaled[:, m % 2, v, :])
                                                   for v in range(2)]).then_inc(f["mod_summed"].sem, 1)

        @block.vector
        def _(dve):
            def scale(m):
                c, w = core.chunk(f"mod{m}")
                dve.wait_ge(core.w_loaded[c % RING].sem, 16 * (c // RING + 1))
                if m >= 2:
                    dve.wait_ge(f["mod_summed"].sem, f["mod_summed"].value(m - 1))
                for k in range(KD):
                    for v in range(2):
                        sc, acc = core.silu_c[:, 2 * k + v:2 * k + v + 1], scaled[:, m % 2, v, :]
                        if k == 0:
                            last = dve.tensor_scalar(acc, w[:, k, :], sc, None, ALU.mult)
                        else:
                            last = dve.scalar_tensor_tensor(out=acc, in0=w[:, k, :], scalar=sc, in1=acc,
                                                            op0=ALU.mult, op1=ALU.add)
                    if k < KD - 1:
                        core.v_chain(dve, last)
                last.then_inc(f["mod_scaled"].sem, 1)

            for n in range(0, len(jobs), lanes):
                for m in before.get(n, ()):
                    scale(m)
                dve.wait_ge(f["products_done"].sem, f["products_done"].value(n + 1))
                finish(dve, n, core.bank(n % banks, jobs[n][2], jobs[n][3])).then_inc(f["evacuated_v"].sem, 1)

        if both or beside is not None:
            @block.scalar
            def _(act):
                for n in range(len(jobs)):
                    if both and n % 2:
                        act.wait_ge(f["products_done"].sem, f["products_done"].value(n + 1))
                        finish(act, n, core.bank(n % banks, jobs[n][2], jobs[n][3])).then_inc(f["evacuated_s"].sem, 1)
                    for m in after.get(n, ()):
                        act.wait_ge(f["mod_summed"].sem, f["mod_summed"].value(m + 1))
                        if m >= 2:
                            stored = f[f"mod_stored{m % 2}"]
                            act.wait_ge(stored.sem, stored.value(16 * (m // 2)))
                        act.activation(rows[:, m % 2, :], core.bank(7, 2), ACT.Copy).then_inc(f["mod_copied"].sem, 1)

        if beside is not None:
            @block.gpsimd
            def _(pool):
                for mods in beside:
                    for m in mods:
                        pool.wait_ge(f["mod_copied"].sem, f["mod_copied"].value(m + 1))
                        pool.dma_start(core.dram["mod_rows"][m // 12, :, 512 * (m % 12):512 * (m % 12) + 512],
                                       rows[:, m % 2, :]).then_inc(f[f"mod_stored{m % 2}"].sem, 16)
                for z in range(2):
                    pool.wait_ge(f[f"mod_stored{z}"].sem, f[f"mod_stored{z}"].value(16 * (core.mods_done // 2)))

    f["products_done"].advance(len(jobs))
    f["evacuated_v"].advance((len(jobs) + lanes - 1) // lanes)
    f["evacuated_s"].advance(len(jobs) // 2 if both else 0)
    core.consumed = used


def copy_out(core, dst):
    def finish(eng, n, ps):
        if eng is core.nc.scalar:
            return eng.activation(dst(n), ps, ACT.Copy)
        return eng.tensor_copy(dst(n), ps)
    return finish


def head_normed(core, name, jobs, scratch, dest, gain, group, const, sources=None):
    nc, f = core.nc, core.flags
    squares, roots = scratch

    def tile(n):
        return sources[n] if sources else core.bank(n % 3, P, jobs[n][3])

    used = core.use_up(jobs)
    N = len(jobs)

    with nc.Block(name) as block:
        @block.sync
        def _(sp):
            core.feed(sp, used)

        @block.tensor
        def _(pe):
            seen = None
            for n in range(N + 1):
                if n < N and not sources:
                    chunk, release, rows, cols, pairs = jobs[n]
                    if chunk is not None and chunk != seen:
                        core.await_chunk(pe, chunk)
                        seen = chunk
                    if n >= 3:
                        pe.wait_ge(f["normed"].sem, f["normed"].value(n - 2))
                    last = products(pe, core.bank(n % 3, rows, cols), pairs)
                    last.then_inc(f["products_done"].sem, 1)
                if n >= 1:
                    m = n - 1
                    cols = jobs[m][3]
                    pe.wait_ge(f["squared"].sem, f["squared"].value(m + 1))
                    if m >= 2:
                        pe.wait_ge(f["rooted"].sem, f["rooted"].value(m - 1))
                    pe.matmul(core.bank(3 + m % 2, P, cols), const, squares[:, m % 2, 0:cols], start=True,
                              stop=True).then_inc(f["summed"].sem, 1)

        @block.scalar
        def _(act):
            for n in range(N + 1):
                if n < N:
                    cols = jobs[n][3]
                    if not sources:
                        act.wait_ge(f["products_done"].sem, f["products_done"].value(n + 1))
                    if n >= 2:
                        act.wait_ge(f["summed"].sem, f["summed"].value(n - 1))
                    act.activation(squares[:, n % 2, 0:cols], tile(n), ACT.Square)\
                        .then_inc(f["squared"].sem, 1)
                if n >= 1:
                    m = n - 1
                    cols = jobs[m][3]
                    act.wait_ge(f["summed"].sem, f["summed"].value(m + 1))
                    if m >= 2:
                        act.wait_ge(f["normed"].sem, f["normed"].value(m - 1))
                    r = roots[:, m % 2, 0:cols]
                    core.s_chain(act, act.activation(r, core.bank(3 + m % 2, P, cols), ACT.Ln,
                                                     bias=core.eps[:, 0:1], scale=1.0 / group))
                    act.activation(r, r, ACT.Exp, scale=-0.5).then_inc(f["rooted"].sem, 1)

        @block.vector
        def _(dve):
            for n in range(N):
                cols = jobs[n][3]
                dve.wait_ge(f["rooted"].sem, f["rooted"].value(n + 1))
                dve.scalar_tensor_tensor(out=dest(n), in0=tile(n), scalar=gain(n),
                                         in1=roots[:, n % 2, 0:cols], op0=ALU.mult, op1=ALU.mult)\
                    .then_inc(f["normed"].sem, 1)

    if not sources:
        f["products_done"].advance(N)
    for k in ("squared", "summed", "rooted", "normed"):
        f[k].advance(N)
    core.consumed = used


def normalise(core, name, parts, scale, shift=None):
    nc, f = core.nc, core.flags
    with ExitStack() as stack:
        squares = stack.enter_context(nc.sbuf_tensor(name + "_squares", [P, 2, 512], F32))
        roots = stack.enter_context(nc.sbuf_tensor(name + "_roots", [P, T], F32))
        N = KD * len(parts)
        with nc.Block(name) as block:
            @block.sync
            def _(sp):
                core.feed(sp, core.consumed)

            @block.scalar
            def _(act):
                for n in range(N):
                    (t0, tn), k = parts[n // KD], n % KD
                    if n >= 2:
                        act.wait_ge(f["summed"].sem, f["summed"].value(n - 1))
                    act.activation(squares[:, n % 2, 0:tn], core.X[:, k, t0:t0 + tn], ACT.Square)\
                        .then_inc(f["squared"].sem, 1)
                    if k == KD - 1:
                        act.wait_ge(f["summed"].sem, f["summed"].value(n + 1))
                        r = roots[:, t0:t0 + tn]
                        core.s_chain(act, act.activation(r, core.bank(n // KD, P, tn), ACT.Ln,
                                                         bias=core.eps[:, 0:1], scale=1.0 / D))
                        act.activation(r, r, ACT.Exp, scale=-0.5).then_inc(f["rooted"].sem, 1)

            @block.tensor
            def _(pe):
                for n in range(N):
                    (t0, tn), k = parts[n // KD], n % KD
                    pe.wait_ge(f["squared"].sem, f["squared"].value(n + 1))
                    pe.matmul(core.bank(n // KD, P, tn), core.const("ones"), squares[:, n % 2, 0:tn],
                              start=k == 0, stop=k == KD - 1).then_inc(f["summed"].sem, 1)

            @block.vector
            def _(dve):
                for p, (t0, tn) in enumerate(parts):
                    dve.wait_ge(f["rooted"].sem, f["rooted"].value(p + 1))
                    for k in range(KD):
                        last = dve.scalar_tensor_tensor(out=core.H[:, k, t0:t0 + tn], in0=core.X[:, k, t0:t0 + tn],
                                                        scalar=scale(k, p), in1=roots[:, t0:t0 + tn],
                                                        op0=ALU.mult, op1=ALU.mult)
                    if shift is not None:
                        core.v_chain(dve, last)
                        for k in range(KD):
                            dve.tensor_scalar(core.H[:, k, t0:t0 + tn], core.H[:, k, t0:t0 + tn], shift(k, p),
                                              None, ALU.add)
        for k, v in (("squared", N), ("summed", N), ("rooted", len(parts))):
            f[k].advance(v)


def attention(core, name, units, bias_loads=()):
    nc, f = core.nc, core.flags
    U = len(units)
    widest = max(u["width"] for u in units) + 1
    LAG = 2
    SL = LAG + 1
    NS = 4 if widest <= 513 else 2
    groups = []
    g = 0
    for u in units:
        mine = []
        for t in range(0, len(u["v"]), 4):
            mine.append((g, t, min(4, len(u["v"]) - t)))
            g += 1
        groups.append(mine)
    evacs = [n for n, u in enumerate(units) if u["evac"]]
    score = [core.psum[:, 4 // NS * i:4 // NS * (i + 1), :].rearrange("p a b -> p (a b)") for i in range(NS)]
    ident = core.const("ident")

    with ExitStack() as stack:
        probs = stack.enter_context(nc.sbuf_tensor(name + "_probs", [P, SL, widest], F32))
        turned = stack.enter_context(nc.sbuf_tensor(name + "_turned", [P, 3, 512], F32))
        stats = stack.enter_context(nc.sbuf_tensor(name + "_stats", [P, 4, 3], F32))

        def tile_keys(u, t):
            return min(P, u["width"] - t * P)

        with nc.Block(name) as block:
            @block.sync
            def _(sp):
                if bias_loads:
                    sp.wait_ge(f["tables_stored"].sem, 32)
                for n, (dst, src, after) in enumerate(bias_loads):
                    if after is not None:
                        sp.wait_ge(f["biased"].sem, f["biased"].value(after + 1))
                    sp.dma_start(dst, src).then_inc(f[f"bias_loaded{n % 2}"].sem, 16)
                core.feed(sp, core.consumed)

            @block.tensor
            def _(pe):
                def scores(n):
                    u = units[n]
                    if n >= NS:
                        pe.wait_ge(f["exped"].sem, f["exped"].value(n - NS + 1))
                    at = 0
                    for k in u["k"]:
                        last = pe.matmul(score[n % NS][:, at:at + k.shape[1]], u["q"], k, start=True, stop=True)
                        at += k.shape[1]
                    last.then_inc(f["scored"].sem, 1)

                def transposes(n):
                    u = units[n]
                    pe.wait_ge(f["weighted"].sem, f["weighted"].value(n + 1))
                    for g, t0, nt in groups[n]:
                        if g >= 2:
                            pe.wait_ge(f["copied"].sem, f["copied"].value(g - 1))
                        for t in range(t0, t0 + nt):
                            w = tile_keys(u, t)
                            last = pe.transpose(core.bank(4 + g % 2, w, P, (t - t0) * P),
                                                probs[:, n % SL, t * P:t * P + w], ident)
                        last.then_inc(f["turned"].sem, 1)

                def values(n):
                    u = units[n]
                    if u["first"] and u["clears"] is not None:
                        pe.wait_ge(f["emptied"].sem, f["emptied"].value(u["clears"]))
                    for g, t0, nt in groups[n]:
                        pe.wait_ge(f["copied"].sem, f["copied"].value(g + 1))
                        for t in range(t0, t0 + nt):
                            w = tile_keys(u, t)
                            last = pe.matmul(core.bank(6 + u["bank"], P, P, u["col"]), u["v"][t],
                                             turned[0:w, g % 3, (t - t0) * P:(t - t0) * P + P],
                                             start=u["first"] and t == 0,
                                             stop=u["last"] and t == len(u["v"]) - 1)
                    last.then_inc(f["attended"].sem, 1)

                for n in range(U + LAG + 1):
                    if n < U:
                        scores(n)
                    if LAG <= n < U + LAG:
                        transposes(n - LAG)
                    if n > LAG:
                        values(n - LAG - 1)

            @block.vector
            def _(dve):
                def soften(n):
                    u = units[n]
                    w = u["width"]
                    dve.wait_ge(f["scored"].sem, f["scored"].value(n + 1))
                    if n >= SL:
                        dve.wait_ge(f["turned"].sem, f["turned"].value(groups[n - SL][-1][0] + 1))
                    if u["bias_load"] is not None:
                        b = f[f"bias_loaded{u['bias_load'] % 2}"]
                        dve.wait_ge(b.sem, b.value(16 * (u["bias_load"] // 2 + 1)))
                    row = score[n % NS][:, 0:w]
                    if u["bias"] is None:
                        dve.tensor_reduce(stats[:, n % 4, 0:1], row, AX.X, ALU.max, negate=True)\
                            .then_inc(f["biased"].sem, 1)
                        return
                    least = -NEG * 1e8
                    if u["sink"] is not None:
                        least = probs[:, n % SL, w:w + 1]
                        core.v_chain(dve, dve.tensor_scalar(least, u["sink"], -1.0, None, ALU.mult))
                    dve.tensor_tensor_reduce(out=probs[:, n % SL, 0:w], in0=row, in1=u["bias"], scale=-1.0, scalar=least,
                                             op0=ALU.add, op1=ALU.min, accum_out=stats[:, n % 4, 0:1])\
                        .then_inc(f["biased"].sem, 1)

                def weigh(n):
                    u = units[n]
                    w = u["width"]
                    dve.wait_ge(f["exped"].sem, f["exped"].value(n + 1))
                    core.v_chain(dve, dve.reciprocal(stats[:, n % 4, 2:3], stats[:, n % 4, 1:2]))
                    dve.tensor_scalar(probs[:, n % SL, 0:w], probs[:, n % SL, 0:w], stats[:, n % 4, 2:3], u["coef"],
                                      ALU.mult, ALU.mult).then_inc(f["weighted"].sem, 1)

                def empty(n):
                    dst, rows = units[n]["evac"]
                    dve.wait_ge(f["attended"].sem, f["attended"].value(n + 1))
                    a, b = rows
                    dve.tensor_copy(dst, core.psum[a:b, 6 + units[n]["bank"], 0:dst.shape[-1]])\
                        .then_inc(f["emptied"].sem, 1)

                for n in range(U + LAG + 2):
                    if n >= LAG + 2 and units[n - LAG - 2]["evac"]:
                        empty(n - LAG - 2)
                    if n < U:
                        soften(n)
                    if 1 <= n <= U:
                        weigh(n - 1)

            @block.scalar
            def _(act):
                for n in range(U + LAG):
                    if n < U:
                        u = units[n]
                        act.wait_ge(f["biased"].sem, f["biased"].value(n + 1))
                        w = u["width"] + (u["sink"] is not None)
                        row = probs[:, n % SL, 0:w] if u["bias"] is not None else score[n % NS][:, 0:w]
                        act.activation(probs[:, n % SL, 0:w], row, ACT.Exp, bias=stats[:, n % 4, 0:1],
                                       scale=1.0 if u["bias"] is None else -1.0,
                                       accum_out=stats[:, n % 4, 1:2]).then_inc(f["exped"].sem, 1)
                    if n >= LAG:
                        for g, t0, nt in groups[n - LAG]:
                            act.wait_ge(f["turned"].sem, f["turned"].value(g + 1))
                            if g >= 3:
                                owner = next(i for i, x in enumerate(groups) if any(y[0] == g - 3 for y in x))
                                act.wait_ge(f["attended"].sem, f["attended"].value(owner + 1))
                            w = tile_keys(units[n - LAG], t0) if nt == 1 else P
                            act.activation(turned[0:w, g % 3, 0:nt * P], core.bank(4 + g % 2, w, nt * P),
                                           ACT.Copy).then_inc(f["copied"].sem, 1)

    for k in ("scored", "biased", "exped", "weighted", "attended"):
        f[k].advance(U)
    f["turned"].advance(g_total(groups))
    f["copied"].advance(g_total(groups))
    f["emptied"].advance(len(evacs))
    for i in range(2):
        f[f"bias_loaded{i}"].advance(16 * len(bias_loads[i::2]))


def g_total(groups):
    return sum(len(x) for x in groups)


def unit(q, k, v, bank, col, first=True, last=True, bias=None, bias_load=None, sink=None, coef=1.0, evac=None):
    return dict(q=q, k=k, width=sum(x.shape[1] for x in k), bias=bias, bias_load=bias_load, sink=sink, coef=coef,
                v=v, bank=bank, col=col, first=first, last=last, evac=evac, clears=None)


def plan_outputs(units):
    done = 0
    fresh = True
    for u in units:
        if fresh and done >= 2:
            u["clears"] = done - 1
        fresh = False
        if u["evac"]:
            done += 1
            fresh = True
    return units


def plan_weights():
    plan = [(f"proj{i}", KD, 512) for i in range(7)] + [("proj7", KD, 24), ("cmp0", 16, 256), ("cmp1", 16, 256)]
    for n in range(3):
        plan += [(f"mg{n}_0", KD, 512), (f"mg{n}_1", KD, 512), (f"branch{n}", 4, 1024)]
    plan += [(f"out{i}", KD, 512) for i in range(2)]
    for name, kt, n, beside in (("up", KD, 512, MODS_BESIDE_UP), ("down", 32, P, MODS_BESIDE_DOWN)):
        for i in range(8):
            plan += [(f"{name}{i}", kt, n)] + [(f"mod{m}", KD, 512) for m in beside[i]]
    plan += [("ev0", KD, 512), ("ev1", KD, 288), ("ev2", KD, 512), ("ev3", KD, 512), ("ev4", KD, 512)]
    plan += [(f"ev_out{i}", KD, 512) for i in range(2)]
    plan += [("od0", KD, 512), ("od1", KD, 512), ("od2", KD, 256)]
    plan += [(f"od_out{i}", KD, 512) for i in range(2)]
    return plan


def load_inputs(core, onehot, rel):
    nc, f, dram = core.nc, core.flags, core.dram
    x = dram["xT"].rearrange("(k p) t -> p k t", p=P)
    c = dram["ctxT"].rearrange("(k p) t -> p k t", p=P)
    with nc.Block("load") as block:
        @block.sync
        def _(sp):
            sp.dma_start(onehot[:, :], dram["onehot"]).then_inc(f["misc_loaded"].sem, 16)
            sp.dma_start(rel[:, :], dram["rel"]).then_inc(f["misc_loaded"].sem, 16)
            sp.dma_start(core.X[:, :, 0:S], x).then_inc(f["misc_loaded"].sem, 16)
            sp.dma_start(core.con[:, :], dram["con"]).then_inc(f["misc_loaded"].sem, 16)
            core.feed(sp, 0)

        @block.scalar
        def _(act):
            act.dma_start(core.par[:, :], dram["par"]).then_inc(f["misc_loaded"].sem, 16)
            act.wait_ge(f["misc_loaded"].sem, 80)
            act.dma_start(core.X[:, :, S:T], c).then_inc(f["late_loaded"].sem, 16)
            act.dma_start(core.router[:, :, :, :], dram["router"]).then_inc(f["late_loaded"].sem, 16)

        @block.vector
        def _(dve):
            dve.memset(core.eps[:, :], EPS)
    f["misc_loaded"].advance(80)
    f["late_loaded"].advance(32)


NEG_LAM, SUBLN, AQ_G, BQ_G, CQ_G, ATT_G, SWA_G, N_DERIVED = range(8)


def derive(core, onehot, rel):
    nc, f, dram = core.nc, core.flags, core.dram
    scale = HD ** -0.5
    par = core.param
    der = core.derived
    with ExitStack() as stack:
        def sb(name, shape):
            return stack.enter_context(nc.sbuf_tensor(name, shape, F32))
        prod = sb("lam_products", [P, 2])
        exps = sb("lam_exps", [P, 2])
        sig = sb("c_sigmoid", [P, 16])
        table_ac, table_b = core.table_ac, core.table_b
        with nc.Block("derive") as block:
            @block.sync
            def _(sp):
                sp.wait_ge(f["made"].sem, f["made"].value(1))
                for lo, table in ((0, table_ac), (12, table_b)):
                    n = table.shape[0]
                    sp.dma_start(dram["bias"][lo:lo + n], table[:, :].rearrange("h (o t) -> h o t", o=1)
                                 .broadcast_to([n, P, TABLE])).then_inc(f["tables_stored"].sem, 16)

            @block.vector
            def _(dve):
                lam = par("lambda")
                dve.tensor_tensor(prod[:, 0:1], lam[:, 0:1], lam[:, 1:2], ALU.mult)
                dve.tensor_tensor(prod[:, 1:2], lam[:, 2:3], lam[:, 3:4], ALU.mult).then_inc(f["squared"].sem, 1)
                dve.tensor_scalar(der[:, SUBLN:SUBLN + 1], par("subln"), 1.0 - LAM_INIT, None, ALU.mult)
                for at, src in ((AQ_G, par("qk_gain", 0, 1)), (BQ_G, par("qk_gain", 2, 1)),
                                (CQ_G, par("qk_gain", 4, 1)), (ATT_G, par("att_q")), (SWA_G, par("swa_q"))):
                    dve.tensor_scalar(der[:, at:at + 1], src, scale, None, ALU.mult)
                dve.wait_ge(f["exped"].sem, f["exped"].value(1))
                dve.scalar_tensor_tensor(out=der[:, NEG_LAM:NEG_LAM + 1], in0=exps[:, 1:2], scalar=LAM_INIT,
                                         in1=exps[:, 0:1], op0=ALU.subtract, op1=ALU.subtract)
                dve.wait_ge(f["silued"].sem, f["silued"].value(1))
                dve.tensor_tensor(core.silu_c[:, :], par("c"), sig[:, :], ALU.mult)
                dve.wait_ge(f["products_done"].sem, f["products_done"].value(1))
                dve.tensor_copy(table_ac[:, :], core.psum[0:12, 0:2, :].rearrange("p a b -> p (a b)")[:, 0:TABLE])
                core.v_chain(dve, dve.tensor_copy(
                    table_b[:, :], core.psum[0:8, 2:4, :].rearrange("p a b -> p (a b)")[:, 0:TABLE]))
                dve.memset(table_ac[:, MASKED_FROM:TABLE], NEG)
                dve.memset(table_b[:, 0:S - WINDOW_B], NEG)
                dve.memset(table_b[:, MASKED_FROM:TABLE], NEG).then_inc(f["made"].sem, 1)

            @block.tensor
            def _(pe):
                pe.wait_ge(f["squared"].sem, f["squared"].value(1))
                pe.matmul(core.bank(4, P, 2), core.const("ones"), prod[:, :], start=True, stop=True)\
                    .then_inc(f["summed"].sem, 1)
                for b, (lo, hi) in enumerate(((0, 12), (12, 20))):
                    pe.matmul(core.bank(2 * b, hi - lo), rel[:, lo:hi], onehot[:, 0:512], start=True, stop=True)
                    last = pe.matmul(core.bank(2 * b + 1, hi - lo, TABLE - 512), rel[:, lo:hi],
                                     onehot[:, 512:TABLE], start=True, stop=True)
                last.then_inc(f["products_done"].sem, 1)

            @block.scalar
            def _(act):
                act.wait_ge(f["summed"].sem, f["summed"].value(1))
                act.activation(exps[:, :], core.bank(4, P, 2), ACT.Exp).then_inc(f["exped"].sem, 1)
                act.activation(sig[:, :], par("c"), ACT.Sigmoid).then_inc(f["silued"].sem, 1)
    for k in ("squared", "exped", "silued", "products_done", "summed", "made"):
        f[k].advance(1)


def modulation(core):
    nc, f = core.nc, core.flags
    with nc.sbuf_tensor("mod_row_tiles", [96, 2, P], F32) as R, nc.Block("modulation") as block:
        @block.sync
        def _(sp):
            for l in range(2):
                sp.dma_start(R[:, l, :], core.dram["mod_rows"][l].rearrange("v (m p) -> (v m) p", p=P))\
                    .then_inc(f["misc_loaded"].sem, 16)
            sp.wait_ge(f["late_loaded"].sem, 32)

        @block.tensor
        def _(pe):
            pe.wait_ge(f["misc_loaded"].sem, f["misc_loaded"].value(32))
            for l in range(2):
                last = pe.transpose(core.bank(0, P, 96, P * l), R[:, l, :], core.const("ident", 96)[:, 0:96])
            last.then_inc(f["turned"].sem, 1)

        @block.vector
        def _(dve):
            dve.wait_ge(f["turned"].sem, f["turned"].value(1))
            for l in range(2):
                for v in range(2):
                    dve.tensor_tensor(core.mods[:, l, :, v], core.bank(0, P, 48, P * l + 48 * v),
                                      core.param("mod_b", 48 * l, 48), ALU.add)
    f["misc_loaded"].advance(32)
    f["turned"].advance(1)

    with nc.Block("mod_gains") as block:
        @block.vector
        def _(dve):
            for l in range(2):
                for which, name in ((1, "norm_mix_2"), (4, "norm_ffn_2")):
                    for v in range(2):
                        dve.scalar_tensor_tensor(
                            out=core.mod_gain[:, l, which // 4, :, v], in0=core.mods[:, l, 8 * which:8 * which + 8, v],
                            scalar=1.0, in1=core.param(name, 8 * l, 8), op0=ALU.add, op1=ALU.mult)


def modulated_norm(core, name, l, ffn, parts):
    shift = 24 if ffn else 0
    normalise(core, name, parts, lambda k, p: core.mod_gain[:, l, ffn, k, p:p + 1],
              lambda k, p: core.mods[:, l, shift + k, p:p + 1])


def residual(core, name, chunks, src, parts, gate=None, beside=None):
    jobs, where = [], []
    for i, cname in enumerate(chunks):
        c, w = core.chunk(cname)
        tiles = w.shape[2] // P
        for j in range(tiles):
            for p, (t0, tn) in enumerate(parts):
                jobs.append((c, j == tiles - 1 and p == len(parts) - 1, P, tn,
                             [(w[:, k, j * P:(j + 1) * P], src(k, t0, tn)) for k in range(w.shape[1])]))
                where.append((i * tiles + j, p, t0, tn))

    def finish(dve, n, ps):
        m, p, t0, tn = where[n]
        x = core.X[:, m, t0:t0 + tn]
        if gate is None:
            return dve.tensor_tensor(x, x, ps, ALU.add)
        return dve.scalar_tensor_tensor(out=x, in0=ps, scalar=gate(m, p), in1=x, op0=ALU.mult, op1=ALU.add)
    dense(core, name, jobs, finish, both=False, beside=beside)


def feature_jobs(core, cname, parts, tiles=None, release=True):
    c, w = core.chunk(cname)
    tiles = range(w.shape[2] // P) if tiles is None else tiles
    jobs = []
    for j in tiles:
        for p, (t0, tn) in enumerate(parts):
            jobs.append((c, release and j == tiles[-1] and p == len(parts) - 1, P, tn,
                         [(w[:, k, j * P:(j + 1) * P], core.H[:, k, t0:t0 + tn]) for k in range(KD)]))
    return jobs


def token_jobs(core, cname, tokens, lo, hi, release=True):
    c, w = core.chunk(cname)
    return [(c, release and t == tokens - 1, P, hi - lo,
             [(core.H[:, k, t * P:(t + 1) * P], w[:, k, lo:hi]) for k in range(KD)]) for t in range(tokens)]


def load_compress(core, sp, CK, shifted, w2):
    f = core.flags
    w = core.dram["cmp_w2"].rearrange("v (k p) d -> p v k d", p=P)
    for half in range(2):
        for v in range(2):
            sp.dma_start(w2[:, v, :, 64 * half:64 * half + 64], w[:, v]).then_inc(f["misc_loaded"].sem, 16)
    for name in ("evacuated_v", "evacuated_s"):
        sp.wait_ge(f[name].sem, f[name].value(1))
    for g in range(2):
        sp.dma_start(shifted[0:64, :, g, :], CK[64 * g:64 * g + 64, :, :]).then_inc(f["misc_loaded"].sem, 16)
        sp.dma_start(shifted[64:128, :, g, 0:S - 1], CK[64 * g:64 * g + 64, :, 1:S]).then_inc(f["misc_loaded"].sem, 16)


def compress(core, shifted, w2, KC, VC, CG, CG0):
    nc, f, dram = core.nc, core.flags, core.dram
    N2 = 2 * NC_CMP
    with ExitStack() as stack:
        def sb(name, shape):
            return stack.enter_context(nc.sbuf_tensor(name, shape, F32))
        blocks = sb("cmp_blocks", [P, 2, 16, N2])
        x = sb("cmp_x", [P, 4 * N2])
        t = sb("cmp_t", [P, 4 * N2])
        root = sb("cmp_root", [P, N2])
        sq = sb("cmp_sq", [P, N2])
        for kv in range(2):
            core.used_up[core.plan[f"cmp{kv}"][0]] = (f["products_done"], f["products_done"].value(kv + 1))
        with nc.Block("compress") as block:
            @block.sync
            def _(sp):
                core.feed(sp, core.consumed + 2)

            @block.vector
            def _(dve):
                dve.wait_ge(f["misc_loaded"].sem, f["misc_loaded"].value(128))
                for kv in range(2):
                    for m in range(16):
                        last = dve.tensor_scalar(
                            blocks[:, kv, m, :].rearrange("p (g c) -> p g c", g=2),
                            shifted[:, kv, :, 2 * m:2 * m + 16 * (NC_CMP - 1) + 1:16],
                            core.param("cmp_pos", 16 * kv + m, 1), None, ALU.add)
                    last.then_inc(f["made"].sem, 1)
                dve.wait_ge(f["products_done"].sem, f["products_done"].value(2))
                core.v_chain(dve, dve.tensor_copy(x[:, :], core.bank(0, P, 4 * N2)))
                core.v_chain(dve, dve.tensor_tensor(t[:, :], x[:, :], x[:, :], ALU.mult))
                core.v_chain(dve, dve.tensor_scalar(t[:, :], t[:, :], 0.044715, 1.0, ALU.mult, ALU.add))
                dve.tensor_tensor(t[:, :], t[:, :], x[:, :], ALU.mult).then_inc(f["squared"].sem, 1)
                dve.wait_ge(f["exped"].sem, f["exped"].value(1))
                core.v_chain(dve, dve.tensor_scalar(t[:, :], t[:, :], 1.0, 0.5, ALU.add, ALU.mult))
                dve.tensor_tensor(x[:, :], t[:, :], x[:, :], ALU.mult).then_inc(f["made"].sem, 1)
                dve.wait_ge(f["summed"].sem, f["summed"].value(1))
                dve.tensor_copy(VC[:, :], core.bank(2, NC_CMP, P))
                dve.wait_ge(f["rooted"].sem, f["rooted"].value(1))
                dve.scalar_tensor_tensor(out=KC[:, :], in0=core.bank(1, P, N2), scalar=core.param("qk_gain", 5, 1),
                                         in1=root[:, :], op0=ALU.mult, op1=ALU.mult)
                dve.wait_ge(f["silued"].sem, f["silued"].value(1))
                for h in range(8):
                    last = dve.tensor_tensor(CG0[:, h:h + 1], CG[:, 0, 3 * h:3 * h + 1], core.param("valid31"),
                                             ALU.mult)

            @block.tensor
            def _(pe):
                for kv in range(2):
                    c, w = core.chunk(f"cmp{kv}")
                    core.await_chunk(pe, c)
                    pe.wait_ge(f["made"].sem, f["made"].value(kv + 1))
                    for ht in range(2):
                        last = products(pe, core.bank(0, P, N2, (2 * kv + ht) * N2),
                                        [(w[:, m, ht * P:(ht + 1) * P], blocks[:, kv, m, :]) for m in range(16)])
                    last.then_inc(f["products_done"].sem, 1)
                pe.wait_ge(f["made"].sem, f["made"].value(3))
                products(pe, core.bank(1, P, N2), [(w2[:, 0, ht, :], x[:, ht * N2:(ht + 1) * N2]) for ht in range(2)])
                for g in range(2):
                    last = products(pe, core.bank(2, NC_CMP, HD, g * HD),
                                    [(x[:, (2 + ht) * N2 + g * NC_CMP:(2 + ht) * N2 + (g + 1) * NC_CMP],
                                      w2[:, 1, ht, 0:HD]) for ht in range(2)])
                last.then_inc(f["summed"].sem, 1)
                pe.wait_ge(f["normed"].sem, f["normed"].value(1))
                pe.matmul(core.bank(3, P, N2), core.const("blocks"), sq[:, :], start=True, stop=True)\
                    .then_inc(f["turned"].sem, 1)

            @block.scalar
            def _(act):
                act.activation(CG[:, :, :], CG[:, :, :], ACT.Sigmoid).then_inc(f["silued"].sem, 1)
                act.wait_ge(f["squared"].sem, f["squared"].value(1))
                act.activation(t[:, :], t[:, :], ACT.Tanh, scale=math.sqrt(2 / math.pi)).then_inc(f["exped"].sem, 1)
                act.wait_ge(f["summed"].sem, f["summed"].value(1))
                act.activation(sq[:, :], core.bank(1, P, N2), ACT.Square).then_inc(f["normed"].sem, 1)
                act.wait_ge(f["turned"].sem, f["turned"].value(1))
                core.s_chain(act, act.activation(root[:, :], core.bank(3, P, N2), ACT.Ln, bias=core.eps[:, 0:1],
                                                 scale=1.0 / HD))
                act.activation(root[:, :], root[:, :], ACT.Exp, scale=-0.5).then_inc(f["rooted"].sem, 1)
    core.consumed += 2
    f["misc_loaded"].advance(128)
    f["made"].advance(3)
    f["products_done"].advance(2)
    for k in ("squared", "exped", "summed", "rooted", "silued", "normed", "turned"):
        f[k].advance(1)


def bias_tile(core, row, u0, n):
    whole = core.dram["bias"]
    return bass.AP(whole.tensor, row * P * TABLE + P - 1 + u0, [[TABLE - 1, P], [1, n]])


def first_block(core):
    nc, f = core.nc, core.flags
    normalise(core, "norm1", [LAT], lambda k, p: core.param("norm_mix", k, 1))
    with ExitStack() as stack:
        def sb(name, shape):
            return stack.enter_context(nc.sbuf_tensor(name, shape, F32))
        Q = sb("Q", [P, 12, S])
        YS = sb("YS", [P, KD, S])
        V = sb("V", [P, 4, 512 + 384])
        CG = sb("CG", [P, 4, 24])
        CG0 = sb("CG0", [P, 8])
        KC = sb("KC", [P, 2 * NC_CMP])
        VC = sb("VC", [NC_CMP, P])
        AQ, BQ, CQ = Q[:, 0:4, :], Q[:, 4:8, :], Q[:, 8:12, :]
        AK, KK = YS[:, 0:4, :], YS[:, 4:7, :]
        with ExitStack() as inner:
            def tmp(name, shape):
                return inner.enter_context(nc.sbuf_tensor(name, shape, F32))
            CK = tmp("CK", [P, 2, S])
            jobs = [j for i in range(4) for j in feature_jobs(core, f"proj{i}", [LAT])]
            jobs += feature_jobs(core, "proj4", [LAT], tiles=range(3), release=False)
            dests = [AQ[:, i, :] for i in range(4)] + [AK[:, i, :] for i in range(4)] + \
                    [BQ[:, i, :] for i in range(4)] + [CQ[:, i, :] for i in range(4)] + \
                    [KK[:, i, :] for i in range(3)]
            der = core.derived
            gains = [der[:, AQ_G:AQ_G + 1]] * 4 + [core.param("qk_gain", 1, 1)] * 4 + [der[:, BQ_G:BQ_G + 1]] * 4 + \
                    [der[:, CQ_G:CQ_G + 1]] * 4 + [core.param("qk_gain", i, 1) for i in (3, 6, 7)]
            with nc.sbuf_tensor("squares", [P, 2, 512], F32) as sq, nc.sbuf_tensor("roots", [P, 2, 512], F32) as rt:
                head_normed(core, "project_qk", jobs, (sq, rt), lambda n: dests[n], lambda n: gains[n], HD,
                            core.const("blocks"))
            jobs = feature_jobs(core, "proj4", [LAT], tiles=range(3, 4))
            jobs += feature_jobs(core, "proj5", [LAT], tiles=range(0, 1), release=False)
            to = [CK[:, 0, :], CK[:, 1, :]]
            jobs += token_jobs(core, "proj5", 4, P, 512)
            to += [V[:, t, 512:896] for t in range(4)]
            jobs += token_jobs(core, "proj6", 4, 0, 512)
            to += [V[:, t, 0:512] for t in range(4)]
            jobs += token_jobs(core, "proj7", 4, 0, 24)
            to += [CG[:, t, :] for t in range(4)]
            shifted = tmp("cmp_shifted", [P, 2, 2, S])
            w2 = tmp("cmp_w2", [P, 2, 2, P])
            dense(core, "project_v", jobs, copy_out(core, lambda n: to[n]),
                  loads=lambda sp: load_compress(core, sp, CK, shifted, w2))
            compress(core, shifted, w2, KC, VC, CG, CG0)

        with ExitStack() as inner:
            bias = inner.enter_context(nc.sbuf_tensor("bias_tiles", [P, 2, 512], F32))
            neg_lam = core.derived[:, NEG_LAM:NEG_LAM + 1]
            units, loads = [], []
            for h in range(4):
                loads.append((bias[:, h % 2, :], bias_tile(core, h, 0, 512), 8 * (h - 1) - 1 if h >= 2 else None))
                for i in range(4):
                    for c in range(2):
                        rows = slice(64 * c, 64 * c + 64)
                        units.append(unit(
                            AQ[rows, h, i * P:(i + 1) * P], [AK[rows, h, 0:(i + 1) * P]],
                            [V[:, t, h * P:(h + 1) * P] for t in range(i + 1)], h % 2, i * P, c == 0, c == 1,
                            bias=bias[:, h % 2, 384 - P * i:512], bias_load=h, coef=neg_lam if c else 1.0,
                            evac=(AQ[:, h, :], (0, P)) if (i, c) == (3, 1) else None))
            attention(core, "attn_a", plan_outputs(units), loads)

            units, loads = [], []
            for h in range(8):
                j, g = h % 4, h // 4
                rows = slice(64 * g, 64 * g + 64)
                loads.append((bias[:, h % 2, 0:256], bias_tile(core, 12 + h, 256, 256),
                              4 * (h - 1) - 1 if h >= 2 else None))
                for i in range(4):
                    lo = max(0, i - 1)
                    units.append(unit(
                        BQ[rows, j, i * P:(i + 1) * P], [KK[rows, 0, lo * P:(i + 1) * P]],
                        [V[:, t, 512:640] for t in range(lo, i + 1)], h % 2, i * P,
                        bias=bias[:, h % 2, 0 if i else P:256], bias_load=h, sink=core.param("sinks", h, 1),
                        evac=(BQ[rows, j, :], (64 * g, 64 * g + 64)) if i == 3 else None))
            attention(core, "attn_b", plan_outputs(units), loads)

            units, loads = [], []
            for h in range(8):
                j, g = h % 4, h // 4
                rows = slice(64 * g, 64 * g + 64)
                loads.append((bias[:, h % 2, :], bias_tile(core, 4 + h, 0, 512), 12 * (h - 1) - 1 if h >= 2 else None))
                for i in range(4):
                    q = CQ[rows, j, i * P:(i + 1) * P]
                    mask = core.const("cmask")[:, i * NC_CMP:(i + 1) * NC_CMP]
                    units.append(unit(q, [KC[rows, g * NC_CMP:(g + 1) * NC_CMP]], [VC[:, :]], h % 2, i * P, True, False,
                                      bias=mask, coef=CG[:, i, 3 * h:3 * h + 1] if i else CG0[:, h:h + 1]))
                    for b in range(2):
                        units.append(unit(
                            q, [KK[rows, 1 + b, 0:(i + 1) * P]],
                            [V[:, t, 640 + P * b:768 + P * b] for t in range(i + 1)], h % 2, i * P, False, b == 1,
                            bias=bias[:, h % 2, 384 - P * i:512], bias_load=h,
                            coef=CG[:, i, 3 * h + 1 + b:3 * h + 2 + b],
                            evac=(CQ[rows, j, :], (64 * g, 64 * g + 64)) if (i, b) == (3, 1) else None))
            attention(core, "attn_c", plan_outputs(units), loads)

        with ExitStack() as inner:
            def tmp(name, shape):
                return inner.enter_context(nc.sbuf_tensor(name, shape, F32))
            scratch = tmp("squares2", [P, 2, 512]), tmp("roots2", [P, 2, 512])
            head_normed(core, "norm_a", [(None, False, P, S, None)] * 4, scratch, lambda n: AQ[:, n, :],
                        lambda n: core.derived[:, SUBLN:SUBLN + 1], P, core.const("ones"),
                        sources=[AQ[:, n, :] for n in range(4)])
        branches(core, Q, YS)
        residual(core, "mix_out", ["out0", "out1"], lambda k, t0, tn: YS[:, k, t0:t0 + tn], [LAT])

    normalise(core, "norm_mlp", [LAT], lambda k, p: core.param("norm_mlp", k, 1))
    with nc.sbuf_tensor("hidden", [P, D_FF // P, S], F32) as HID:
        jobs = [j for i in range(8) for j in feature_jobs(core, f"up{i}", [LAT])]

        def squared_relu(eng, n, ps):
            if eng is nc.scalar:
                core.s_chain(eng, eng.activation(HID[:, n, :], ps, ACT.Relu))
                return eng.activation(HID[:, n, :], HID[:, n, :], ACT.Square)
            core.v_chain(eng, eng.tensor_scalar(HID[:, n, :], ps, 0.0, None, ALU.max))
            return eng.tensor_tensor(HID[:, n, :], HID[:, n, :], HID[:, n, :], ALU.mult)
        dense(core, "mlp_up", jobs, squared_relu, beside=MODS_BESIDE_UP)
        residual(core, "mlp_down", [f"down{i}" for i in range(8)], lambda k, t0, tn: HID[:, k, t0:t0 + tn], [LAT],
                 beside=MODS_BESIDE_DOWN)


def branches(core, Q, YS):
    nc, f = core.nc, core.flags
    with nc.sbuf_tensor("gates", [P, 2, S], F32) as SG, nc.sbuf_tensor("gated_y", [P, 2, S], F32) as GY:
        for n in range(3):
            for half in range(2):
                core.used_up[core.plan[f"mg{n}_{half}"][0]] = \
                    (f["products_done"], f["products_done"].value(8 * n + 4 * half + 4))
            core.used_up[core.plan[f"branch{n}"][0]] = (f["down_done"], f["down_done"].value(8 * n + 8))
        with nc.Block("branches") as block:
            @block.sync
            def _(sp):
                core.feed(sp, core.consumed + 9)

            @block.tensor
            def _(pe):
                for i in range(24):
                    n, m = i // 8, i % 8
                    if m % 4 == 0:
                        c, w = core.chunk(f"mg{n}_{m // 4}")
                        core.await_chunk(pe, c)
                    if i >= 2:
                        pe.wait_ge(f["silued"].sem, f["silued"].value(i - 1))
                    last = products(pe, core.bank(i % 2), [(w[:, k, (m % 4) * P:(m % 4 + 1) * P], core.H[:, k, 0:S])
                                                           for k in range(KD)])
                    last.then_inc(f["products_done"].sem, 1)
                    cb, wb = core.chunk(f"branch{n}")
                    if m == 0:
                        core.await_chunk(pe, cb)
                    if i >= 2:
                        pe.wait_ge(f["gated"].sem, f["gated"].value(i - 1))
                    last = products(pe, core.bank(2 + i % 2), [(wb[:, k, m * P:(m + 1) * P], Q[:, 4 * n + k, :])
                                                               for k in range(4)])
                    last.then_inc(f["down_done"].sem, 1)

            @block.scalar
            def _(act):
                for i in range(24):
                    act.wait_ge(f["products_done"].sem, f["products_done"].value(i + 1))
                    if i >= 2:
                        act.wait_ge(f["gated"].sem, f["gated"].value(i - 1))
                    act.activation(SG[:, i % 2, :], core.bank(i % 2), ACT.Sigmoid).then_inc(f["silued"].sem, 1)

            @block.vector
            def _(dve):
                for i in range(24):
                    m = i % 8
                    dve.wait_ge(f["silued"].sem, f["silued"].value(i + 1))
                    dve.wait_ge(f["down_done"].sem, f["down_done"].value(i + 1))
                    y = core.bank(2 + i % 2)
                    if i < 8:
                        dve.tensor_tensor(YS[:, m, :], SG[:, i % 2, :], y, ALU.mult).then_inc(f["gated"].sem, 1)
                    else:
                        core.v_chain(dve, dve.tensor_tensor(GY[:, i % 2, :], SG[:, i % 2, :], y, ALU.mult))
                        dve.tensor_tensor(YS[:, m, :], YS[:, m, :], GY[:, i % 2, :], ALU.add).then_inc(f["gated"].sem, 1)
    core.consumed += 9
    for k in ("products_done", "down_done", "silued", "gated"):
        f[k].advance(24)


def rotate(core, name, tiles, cos_sin):
    nc, f = core.nc, core.flags
    with nc.sbuf_tensor(name + "_turned", [P, 2, S], F32) as R, nc.Block(name) as block:
        @block.tensor
        def _(pe):
            for n, tile in enumerate(tiles):
                if n >= 2:
                    pe.wait_ge(f["normed"].sem, f["normed"].value(n - 1))
                pe.matmul(core.bank(n % 2), core.const("rot"), tile, start=True, stop=True)\
                    .then_inc(f["turned"].sem, 1)

        @block.vector
        def _(dve):
            for n, tile in enumerate(tiles):
                dve.wait_ge(f["turned"].sem, f["turned"].value(n + 1))
                dve.tensor_tensor(R[:, n % 2, :], core.bank(n % 2), cos_sin[:, 1, :], ALU.mult)
                core.v_chain(dve, dve.tensor_tensor(tile, tile, cos_sin[:, 0, :], ALU.mult))
                dve.tensor_tensor(tile, tile, R[:, n % 2, :], ALU.add).then_inc(f["normed"].sem, 1)
    f["turned"].advance(len(tiles))
    f["normed"].advance(len(tiles))


def over(ap, n):
    return ap.broadcast_to([ap.shape[0], ap.shape[1], n])


def gla_decays(core, z, GQ, GK, LR, gate_w, bufs, rates):
    nc, f = core.nc, core.flags
    CLIP = 40.0
    NCH = T // P
    B, G, EQ, EK0, EK1, QB, KE = (b[:, :] for b in bufs)
    GQf, GKf = (x[:, :, :].rearrange("p a t -> p (a t)") for x in (GQ, GK))
    parts = [LAT, CON]

    def by_chunk(x):
        return x.rearrange("p (c t) -> p c t", t=P)

    class Decays:

        @staticmethod
        def tensor(pe):
            for a in range(2):
                for p, (t0, tn) in enumerate(parts):
                    pe.matmul(core.bank(4 + 2 * a + p, P, tn), gate_w[:, z, a * P:(a + 1) * P], LR[:, t0:t0 + tn],
                              start=True, stop=True).then_inc(f["scored"].sem, 1)

        @staticmethod
        def vector(dve):
            def step(ins):
                core.v_chain(dve, ins)
            for a in range(2):
                for p, (t0, tn) in enumerate(parts):
                    dve.wait_ge(f["scored"].sem, f["scored"].value(4 * z + 2 * a + p + 1))
                    last = dve.tensor_scalar(G[:, a * T + t0:a * T + t0 + tn], core.bank(4 + 2 * a + p, P, tn),
                                             core.param("gla_b", 2 * z + a, 1), None, ALU.add)
            step(last)
            dve.scalar_tensor_tensor(out=B, in0=G, scalar=-1.0, in1=G, op0=ALU.mult, op1=ALU.max)\
                .then_inc(f["made"].sem, 1)
            dve.wait_ge(f["rooted"].sem, f["rooted"].value(z + 1))
            step(dve.scalar_tensor_tensor(out=G, in0=G, scalar=0.0, in1=B, op0=ALU.min, op1=ALU.subtract))
            step(dve.tensor_scalar(G, G, 1.0 / 16.0, None, ALU.mult))
            step(dve.memset(KE, 1.0))
            for c in range(2 * NCH):
                last = dve.tensor_tensor_scan(out=by_chunk(B)[:, c, :], data0=by_chunk(KE)[:, c, :],
                                              data1=by_chunk(G)[:, c, :], initial=0.0, op0=ALU.mult, op1=ALU.add)
            step(last)
            if z == 1:
                step(dve.tensor_tensor(G, G, B, ALU.subtract))
                step(dve.tensor_copy(rates[:, 0:1, :].rearrange("p a c -> p c a"), by_chunk(B)[:, :, P - 1:P]))
                step(dve.tensor_tensor(by_chunk(B), by_chunk(G),
                                       over(rates[:, 0:1, :].rearrange("p a c -> p c a"), P), ALU.add))
            end = P - 1 if z == 0 else 0
            total = by_chunk(B)[:, :, end:end + 1]
            step(dve.tensor_copy(rates[:, 1:2, :].rearrange("p a c -> p c a"), total))
            total = rates[:, 1:2, :].rearrange("p a c -> p c a")
            for half in range(2):
                mid = by_chunk(B)[:, :, 64 * half + 32:64 * half + 33]
                EK = (EK0, EK1)[half]
                step(dve.tensor_copy(rates[:, 2 + half:3 + half, :].rearrange("p a c -> p c a"), mid))
                mid = rates[:, 2 + half:3 + half, :].rearrange("p a c -> p c a")
                dve.tensor_tensor(by_chunk(EK), over(mid, P), by_chunk(B), ALU.subtract)
                t = slice(64 * half, 64 * half + 64)
                step(dve.tensor_tensor(by_chunk(EQ)[:, :, t], by_chunk(B)[:, :, t], over(mid, 64), ALU.subtract))
                step(dve.tensor_scalar(EK, EK, CLIP, None, ALU.min))
            step(dve.tensor_scalar(EQ, EQ, CLIP, None, ALU.min))
            step(dve.tensor_tensor(by_chunk(KE), over(total, P), by_chunk(B), ALU.subtract))
            dve.tensor_copy(QB, B).then_inc(f["made"].sem, 1)
            for n, (e, x) in enumerate(((EQ, GQf), (QB, GQf), (EK0, GKf), (EK1, GKf), (KE, GKf))):
                dve.wait_ge(f["exped"].sem, f["exped"].value(5 * z + n + 1))
                dve.tensor_tensor(e, e, x, ALU.mult)

        @staticmethod
        def scalar_softplus(act):
            act.wait_ge(f["made"].sem, f["made"].value(2 * z + 1))
            core.s_chain(act, act.activation(B, B, ACT.Exp, scale=-1.0))
            act.activation(B, B, ACT.Ln, bias=1.0).then_inc(f["rooted"].sem, 1)

        @staticmethod
        def scalar_exps(act):
            act.wait_ge(f["made"].sem, f["made"].value(2 * z + 2))
            for e in (EQ, QB, EK0, EK1, KE):
                act.activation(e, e, ACT.Exp).then_inc(f["exped"].sem, 1)
            act.activation(rates[:, 1, :], rates[:, 1, :], ACT.Exp)
    return Decays


def project_beside_decays(core, jobs, to, forward, backward):
    nc, f = core.nc, core.flags
    used = core.use_up(jobs)
    with nc.Block("project_gr_gv") as block:
        @block.sync
        def _(sp):
            core.feed(sp, used - 2)

        @block.tensor
        def _(pe):
            forward.tensor(pe)
            seen = None
            for n, (chunk, release, rows, cols, pairs) in enumerate(jobs):
                if chunk != seen:
                    core.await_chunk(pe, chunk)
                    seen = chunk
                if n == 8:
                    pe.wait_ge(f["made"].sem, f["made"].value(1))
                    backward.tensor(pe)
                if n >= 4:
                    pe.wait_ge(f["evacuated_s"].sem, f["evacuated_s"].value(n - 3))
                products(pe, core.bank(n % 4, rows, cols), pairs).then_inc(f["products_done"].sem, 1)

        @block.vector
        def _(dve):
            forward.vector(dve)
            dve.wait_ge(f["products_done"].sem, f["products_done"].value(8))
            backward.vector(dve)

        @block.scalar
        def _(act):
            for n, job in enumerate(jobs):
                act.wait_ge(f["products_done"].sem, f["products_done"].value(n + 1))
                act.activation(to[n], core.bank(n % 4, job[2], job[3]), ACT.Copy).then_inc(f["evacuated_s"].sem, 1)
                if n == 1:
                    forward.scalar_softplus(act)
                if n == 5:
                    forward.scalar_exps(act)
                if n == 8:
                    backward.scalar_softplus(act)
                if n == 11:
                    backward.scalar_exps(act)
    f["products_done"].advance(len(jobs))
    f["evacuated_s"].advance(len(jobs))
    core.consumed = used
    for name, count in (("scored", 8), ("made", 4), ("rooted", 2), ("exped", 10)):
        f[name].advance(count)


def gla_chunks(core, z, GV, GO, bufs, rates, state, keys, att):
    nc, f = core.nc, core.flags
    _, _, EQ, EK0, EK1, QB, KE = (b[:, :].rearrange("p (a t) -> p a t", a=2) for b in bufs)
    NCH = T // P
    order = [4, 5, 0, 1, 2, 3] if z == 0 else [5, 4, 3, 2, 1, 0]
    mask = core.const("causal_st") if z == 0 else core.const("anti_st")
    steps = [(n, c, h) for n, c in enumerate(order) for h in range(4)]

    with nc.Block(f"gla{z}") as block:
        @block.tensor
        def _(pe):
            def scores(i):
                n, c, h = steps[i]
                a, rows = h // 2, slice(64 * (h % 2), 64 * (h % 2) + 64)
                if i >= 2:
                    pe.wait_ge(f["weighted"].sem, f["weighted"].value(i - 1))
                for half, EK in enumerate((EK0, EK1)):
                    last = pe.matmul(core.bank(i % 2, P, 64, 64 * half), EK[rows, a, c * P:(c + 1) * P],
                                     EQ[rows, a, c * P + 64 * half:c * P + 64 * half + 64], start=True, stop=True)
                last.then_inc(f["scored"].sem, 1)
                if h % 2 == 0:
                    j = i // 2
                    if j >= 2:
                        pe.wait_ge(f["copied"].sem, f["copied"].value(j - 1))
                    pe.transpose(core.bank(2 + j % 2, P, P), KE[:, a, c * P:(c + 1) * P], core.const("ident"))\
                        .then_inc(f["turned"].sem, 1)

            def values(i):
                n, c, h = steps[i]
                a, rows = h // 2, slice(64 * (h % 2), 64 * (h % 2) + 64)
                v = GV[:, c, h * P:(h + 1) * P]
                pe.wait_ge(f["weighted"].sem, f["weighted"].value(i + 1))
                if i >= 2:
                    pe.wait_ge(f["emptied"].sem, f["emptied"].value(i - 1))
                last = pe.matmul(core.bank(4 + i % 2, P, P), v, att[:, i % 3, :], start=True, stop=n == 0)
                if n:
                    pe.wait_ge(f["added"].sem, f["added"].value(i - 3))
                    last = pe.matmul(core.bank(4 + i % 2, P, P), state[rows, h, :], QB[rows, a, c * P:(c + 1) * P],
                                     start=False, stop=True)
                last.then_inc(f["attended"].sem, 1)
                pe.wait_ge(f["copied"].sem, f["copied"].value(i // 2 + 1))
                if i >= 2:
                    pe.wait_ge(f["added"].sem, f["added"].value(i - 1))
                pe.matmul(core.bank(6 + i % 2, P, P), keys[:, (i // 2) % 2, :], v, start=True, stop=True)\
                    .then_inc(f["summed"].sem, 1)

            for i in range(len(steps) + 2):
                if i < len(steps):
                    scores(i)
                if i >= 2:
                    values(i - 2)

        @block.scalar
        def _(act):
            for j in range(len(steps) // 2):
                act.wait_ge(f["turned"].sem, f["turned"].value(j + 1))
                if j >= 2:
                    act.wait_ge(f["summed"].sem, f["summed"].value(2 * j - 2))
                act.activation(keys[:, j % 2, :], core.bank(2 + j % 2, P, P), ACT.Copy).then_inc(f["copied"].sem, 1)

        @block.vector
        def _(dve):
            def masked(i):
                dve.wait_ge(f["scored"].sem, f["scored"].value(i + 1))
                if i >= 3:
                    dve.wait_ge(f["attended"].sem, f["attended"].value(i - 2))
                dve.tensor_tensor(att[:, i % 3, :], mask, core.bank(i % 2, P, P), ALU.mult)\
                    .then_inc(f["weighted"].sem, 1)

            def out(i):
                n, c, h = steps[i]
                a, rows = h // 2, slice(64 * (h % 2), 64 * (h % 2) + 64)
                dve.wait_ge(f["attended"].sem, f["attended"].value(i + 1))
                dst, ps = GO[:, h, c * P:(c + 1) * P], core.bank(4 + i % 2, P, P)
                if z == 0:
                    last = dve.tensor_copy(dst, ps)
                else:
                    last = dve.tensor_tensor(dst, dst, ps, ALU.add)
                last.then_inc(f["emptied"].sem, 1)
                dve.wait_ge(f["summed"].sem, f["summed"].value(i + 1))
                u = core.psum[rows, 6 + i % 2, 0:P]
                if n == 0:
                    last = dve.tensor_copy(state[rows, h, :], u)
                else:
                    last = dve.scalar_tensor_tensor(out=state[rows, h, :], in0=state[rows, h, :],
                                                    scalar=rates[rows, 1, a * NCH + c:a * NCH + c + 1], in1=u,
                                                    op0=ALU.mult, op1=ALU.add)
                last.then_inc(f["added"].sem, 1)

            for i in range(len(steps) + 2):
                if i < len(steps):
                    masked(i)
                if i >= 2:
                    out(i - 2)
    N = len(steps)
    for k in ("scored", "weighted", "attended", "summed", "emptied", "added"):
        f[k].advance(N)
    f["turned"].advance(N // 2)
    f["copied"].advance(N // 2)


def even_layer(core):
    nc, f, dram = core.nc, core.flags, core.dram
    parts = [LAT, CON]
    modulated_norm(core, "norm_e", 0, 0, parts)
    with ExitStack() as stack:
        def sb(name, shape):
            return stack.enter_context(nc.sbuf_tensor(name, shape, F32))
        AQ = sb("eAQ", [P, 4, T])
        LR = sb("LR", [32, T])
        gate_w = sb("gate_w", [32, 2, 256])
        with ExitStack() as inner:
            def tmp(name, shape):
                return inner.enter_context(nc.sbuf_tensor(name, shape, F32))
            AK = tmp("eAK", [P, T])
            AV = tmp("eAV", [P, T // P, P])
            trig = tmp("trig", [P, 2, S])
            with nc.Block("load_trig") as block:
                @block.sync
                def _(sp):
                    sp.dma_start(trig[:, :, :], dram["trig"]).then_inc(f["misc_loaded"].sem, 16)
                    sp.dma_start(gate_w[:, :, :], dram["gate_w"]).then_inc(f["misc_loaded"].sem, 16)
                    sp.wait_ge(f["misc_loaded"].sem, f["misc_loaded"].value(32))
            f["misc_loaded"].advance(32)
            scratch = tmp("squares_e", [P, 2, 512]), tmp("roots_e", [P, 2, 512])
            jobs = feature_jobs(core, "ev0", parts)
            jobs += feature_jobs(core, "ev1", parts, tiles=range(1), release=False)
            dests = [AQ[:, j, t0:t0 + tn] for j in range(4) for t0, tn in parts] + [AK[:, t0:t0 + tn] for t0, tn in parts]
            head_normed(core, "project_eqk", jobs, scratch, lambda n: dests[n],
                        lambda n: core.derived[:, ATT_G:ATT_G + 1] if n < 8 else core.param("att_k"), HD,
                        core.const("blocks"))
            c, w = core.chunk("ev1")
            jobs = [(c, False, 32, tn, [(w[:, k, 256:288], core.H[:, k, t0:t0 + tn]) for k in range(KD)])
                    for t0, tn in parts]
            jobs += token_jobs(core, "ev1", T // P, P, 2 * P)
            to = [LR[:, t0:t0 + tn] for t0, tn in parts] + [AV[:, t, :] for t in range(T // P)]
            core.lent = 1
            dense(core, "project_ev", jobs, copy_out(core, lambda n: to[n]))
            rotate(core, "rope_e", [AQ[:, j, 0:S] for j in range(4)] + [AK[:, 0:S]], trig)
            units = []
            for h in range(8):
                j, g = h % 4, h // 4
                rows = slice(64 * g, 64 * g + 64)
                for t0, tn, keys in ((0, S, [(0, S), (S, CTX)]), (S, CTX, [(S, CTX)])):
                    tiles = [t for k0, kn in keys for t in range(k0 // P, (k0 + kn) // P)]
                    for i in range(tn // P):
                        last = i == tn // P - 1
                        units.append(unit(
                            AQ[rows, j, t0 + i * P:t0 + (i + 1) * P], [AK[rows, k0:k0 + kn] for k0, kn in keys],
                            [AV[:, t, :] for t in tiles], (0 if t0 == 0 else 1), i * P,
                            evac=(AQ[rows, j, t0:t0 + tn], (64 * g, 64 * g + 64)) if last else None))
            attention(core, "attn_e", plan_outputs(units))

        GQ, GK = sb("GQ", [P, 2, T]), sb("GK", [P, 2, T])
        GR = sb("GR", [P, 4, T])
        GV = sb("GV", [P, T // P, 512])
        jobs = feature_jobs(core, "ev2", parts)
        to = [x[:, a, t0:t0 + tn] for x in (GQ, GK) for a in range(2) for t0, tn in parts]

        def take_qk(eng, n, ps):
            scale = HD ** -0.5 if n < 4 else 1.0
            if eng is nc.scalar:
                return eng.activation(to[n], ps, ACT.Copy, scale=scale)
            return eng.tensor_scalar(to[n], ps, scale, None, ALU.mult)
        core.lent = 2
        dense(core, "project_gqk", jobs, take_qk)
        GO = sb("GO", [P, 4, T])
        with ExitStack() as inner:
            def tmp(name, shape):
                return inner.enter_context(nc.sbuf_tensor(name, shape, F32))
            n = 2 * T
            first_lent, spent = core.plan["ev_out0"][0] % RING, core.plan["ev3"][0] % RING
            assert first_lent < RING - 1
            lent = core.ring[:, first_lent:first_lent + 2, :].rearrange("p s n -> p (s n)")
            lent = [lent[:, i * n:(i + 1) * n] for i in range(5)]
            folded = [[tmp(name, [P, n]) for name in ("gEQ", "gEK0", "gEK1")] + lent[0:2],
                      lent[2:5] + [core.ring[:, spent, 0:n], core.ring[:, spent, n:2 * n]]]
            go_flat = GO[:, :, :].rearrange("p h t -> p (h t)")
            bufs = [[go_flat[:, 0:n], go_flat[:, n:2 * n]] + folded[z] for z in range(2)]
            rates = [tmp(f"rates{z}", [P, 4, 2 * T // P]) for z in range(2)]
            state = tmp("state", [P, 4, P])
            keys = tmp("keys", [P, 2, P])
            att = tmp("att", [P, 3, P])
            jobs = feature_jobs(core, "ev3", parts) + token_jobs(core, "ev4", T // P, 0, 512)
            to = [GR[:, a, t0:t0 + tn] for a in range(4) for t0, tn in parts] + [GV[:, t, :] for t in range(T // P)]
            project_beside_decays(core, jobs, to, *(gla_decays(core, z, GQ, GK, LR, gate_w, bufs[z], rates[z])
                                                    for z in range(2)))
            for z in range(2):
                gla_chunks(core, z, GV, GO, bufs[z], rates[z], state, keys, att)
            core.lent = 0
        with ExitStack() as inner:
            def tmp(name, shape):
                return inner.enter_context(nc.sbuf_tensor(name, shape, F32))
            scratch = core.H[:, 0:2, 0:512], core.H[:, 2:4, 0:512]
            tiles = [GO[:, h, t0:t0 + tn] for h in range(4) for t0, tn in parts]
            head_normed(core, "norm_g", [(None, False, P, t.shape[-1], None) for t in tiles], scratch,
                        lambda n: tiles[n], lambda n: core.param("gla_norm"), P, core.const("ones"), sources=tiles)
            with nc.Block("silu_r") as block:
                @block.scalar
                def _(act):
                    for h in range(4):
                        act.activation(core.H[:, h, :], GR[:, h, :], ACT.Sigmoid).then_inc(f["silued"].sem, 1)

                @block.vector
                def _(dve):
                    for h in range(4):
                        core.v_chain(dve, dve.tensor_tensor(GO[:, h, :], GO[:, h, :], GR[:, h, :], ALU.mult))
                        dve.wait_ge(f["silued"].sem, f["silued"].value(h + 1))
                        dve.tensor_tensor(GO[:, h, :], GO[:, h, :], core.H[:, h, :], ALU.mult)
            f["silued"].advance(4)
        residual(core, "even_out", ["ev_out0", "ev_out1"],
                 lambda k, t0, tn: (GO if k < 4 else AQ)[:, k % 4, t0:t0 + tn], parts,
                 gate=lambda m, p: core.mods[:, 0, 16 + m, p:p + 1])


def odd_layer(core):
    nc, f, dram = core.nc, core.flags, core.dram
    parts = [LAT, CON]
    modulated_norm(core, "norm_o", 1, 0, parts)
    with ExitStack() as stack:
        def sb(name, shape):
            return stack.enter_context(nc.sbuf_tensor(name, shape, F32))
        Q = sb("oQ", [P, 8, S])
        K = sb("oK", [P, T])
        V = sb("oV", [P, T // P, P])
        trig = sb("trig_o", [P, 2, S])
        masks = sb("masks_o", [P, 640 + 512])
        with nc.Block("load_trig_o") as block:
            @block.sync
            def _(sp):
                sp.dma_start(trig[:, :, :], dram["trig"]).then_inc(f["misc_loaded"].sem, 16)
                sp.dma_start(masks[:, :], dram["window"]).then_inc(f["misc_loaded"].sem, 16)
                sp.wait_ge(f["misc_loaded"].sem, f["misc_loaded"].value(32))
        f["misc_loaded"].advance(32)
        with ExitStack() as inner:
            scratch = [inner.enter_context(nc.sbuf_tensor(n, [P, 2, 512], F32)) for n in ("squares_o", "roots_o")]
            jobs = feature_jobs(core, "od0", [LAT]) + feature_jobs(core, "od1", [LAT])
            jobs += feature_jobs(core, "od2", parts, tiles=range(1), release=False)
            dests = [Q[:, j, :] for j in range(8)] + [K[:, t0:t0 + tn] for t0, tn in parts]
            head_normed(core, "project_oqk", jobs, scratch, lambda n: dests[n],
                        lambda n: core.derived[:, SWA_G:SWA_G + 1] if n < 8 else core.param("swa_k"), HD,
                        core.const("blocks"))
        dense(core, "project_ov", token_jobs(core, "od2", T // P, P, 2 * P), copy_out(core, lambda n: V[:, n, :]))
        rotate(core, "rope_o", [Q[:, j, :] for j in range(8)] + [K[:, 0:S]], trig)
        units = []
        for h in range(16):
            j, g = h % 8, h // 8
            rows = slice(64 * g, 64 * g + 64)
            for i in range(4):
                lo, hi = max(0, i - 1), min(3, i + 1)
                n = CTX + (hi - lo + 1) * P
                mask = masks[:, 0:n] if i else masks[:, 640:640 + n]
                units.append(unit(
                    Q[rows, j, i * P:(i + 1) * P], [K[rows, S:T], *split_keys(K, rows, lo, hi)],
                    [V[:, t, :] for t in (4, 5, *range(lo, hi + 1))], h % 2, i * P, bias=mask,
                    sink=core.param("swa_sink", h, 1),
                    evac=(Q[rows, j, :], (64 * g, 64 * g + 64)) if i == 3 else None))
        attention(core, "attn_o", plan_outputs(units))
        residual(core, "odd_out", ["od_out0", "od_out1"], lambda k, t0, tn: Q[:, k, t0:t0 + tn], [LAT],
                 gate=lambda m, p: core.mods[:, 1, 16 + m, p:p + 1])


def split_keys(K, rows, lo, hi):
    cut = min(lo + 2, hi + 1)
    return [K[rows, a * P:b * P] for a, b in ((lo, cut), (cut, hi + 1)) if b > a]


def expert_tiles(tokens):
    return (2 * tokens + N_EXP * (P - 1)) // P


def route(core, l, tokens, weight, posu, tile_slot, tile_ready, expert_end, load_first):
    nc, f, dram = core.nc, core.flags, core.dram
    NT = tokens // P
    TILES = expert_tiles(tokens)
    with ExitStack() as stack:
        def sb(name, shape, dtype=F32):
            return stack.enter_context(nc.sbuf_tensor(f"{name}{l}", shape, dtype))
        L = sb("logits", [P, NT, 20])
        one = sb("rt_one", [P, NT, 8])
        hot = sb("rt_hot", [P, NT, 12])
        tmp4 = sb("rt_tmp4", [P, NT, 4])
        esel = sb("rt_esel", [P, NT, 4])
        eall = sb("rt_eall", [P, NT, 16])
        taken = sb("rt_taken", [P, NT])
        first = sb("rt_first", [P, NT, 16])
        second = sb("rt_second", [P, NT, 16])
        both = sb("rt_both", [P, NT, 16])
        rank = sb("rt_rank", [P, NT, 16])
        before = sb("rt_before", [P, NT + 1, 16])
        count = sb("rt_count", [P, NT, 16])
        tiles = sb("rt_tiles", [P, 16])
        ends = sb("rt_ends", [P, 2, 16])
        start = sb("rt_start", [P, 1, 16])
        pos = sb("rt_pos", [P, 2, NT])
        passed = sb("rt_passed", [1, TILES, 16])
        index = sb("rt_index", [1, TILES, 1])
        turn = sb("rt_turn", [1, TILES, 1])
        no_token = sb("rt_no_token", [TILES, P], U32)
        token = sb("rt_token", [P, NT], U32)
        rows = sb("rt_rows", [P, 2, D])
        with nc.Block(f"route{l}") as block:
            @block.tensor
            def _(pe):
                for t in range(NT):
                    last = products(pe, core.bank(0, P, 20, 20 * t),
                                    [(core.H[:, k, t * P:(t + 1) * P], core.router[:, l, k, :]) for k in range(KD)])
                last.then_inc(f["products_done"].sem, 1)
                for t in range(NT):
                    if t >= 2:
                        pe.wait_ge(f["copied"].sem, f["copied"].value(t - 1))
                    for k in range(KD):
                        last = pe.transpose(core.bank(4 + 2 * (t % 2) + k // 4, P, P, P * (k % 4)),
                                            core.H[:, k, t * P:(t + 1) * P], core.const("ident"))
                    last.then_inc(f["rows_turned"].sem, 1)
                pe.wait_ge(f["made"].sem, f["made"].value(2))
                pe.matmul(core.bank(1, P, 16 * NT), core.const("causal_st"),
                          both[:, :, :].rearrange("p t e -> p (t e)"), start=True, stop=True)
                pe.matmul(core.bank(2, P, 16 * NT), core.const("ones"),
                          both[:, :, :].rearrange("p t e -> p (t e)"), start=True, stop=True)\
                    .then_inc(f["turned"].sem, 1)

            @block.vector
            def _(dve):
                def step(ins):
                    core.v_chain(dve, ins)

                def pick(best, scores, out):
                    step(dve.tensor_tensor(tmp4[:, :, :], scores, over(best, 4), ALU.is_equal))
                    step(dve.tensor_copy(out[:, :, 0], tmp4[:, :, 0]))
                    step(dve.tensor_copy(taken[:, :], tmp4[:, :, 0]))
                    for e in range(1, 4):
                        step(dve.tensor_tensor(out[:, :, e], tmp4[:, :, e], taken[:, :], ALU.is_gt))
                        if e < 3:
                            step(dve.tensor_tensor(taken[:, :], taken[:, :], tmp4[:, :, e], ALU.max))

                dve.memset(no_token[:, :], 0).then_inc(f["made"].sem, 1)
                dve.memset(before[:, 0, :], 0.0).then_inc(f["gate_up"].sem, 1)
                dve.memset(turn[:, :, :], 0.0).then_inc(f["down_done"].sem, 1)
                step(dve.tensor_copy(token[:, :], core.const("token_no")[:, 0:NT]))
                dve.wait_ge(f["products_done"].sem, f["products_done"].value(1))
                for t in range(NT):
                    last = dve.tensor_tensor(L[:, t, :], core.bank(0, P, 20, 20 * t),
                                             core.param("router_b", 20 * l, 20), ALU.add)
                step(last)
                G = L[:, :, 0:4]
                step(dve.tensor_reduce(one[:, :, 0:1], G, AX.X, ALU.max))
                pick(one[:, :, 0:1], G, hot[:, :, 0:4])
                step(dve.tensor_tensor(esel[:, :, :], G, over(one[:, :, 0:1], 4), ALU.subtract))
                dve.tensor_copy(tmp4[:, :, :], esel[:, :, :]).then_inc(f["weighted"].sem, 1)
                for g in range(4):
                    last = dve.tensor_tensor(eall[:, :, 4 * g:4 * g + 4], L[:, :, 4 + 4 * g:8 + 4 * g],
                                             over(hot[:, :, g:g + 1], 4), ALU.mult)
                step(last)
                for g in range(1, 4):
                    step(dve.tensor_tensor(eall[:, :, 0:4], eall[:, :, 0:4], eall[:, :, 4 * g:4 * g + 4], ALU.add))
                dve.wait_ge(f["exped"].sem, f["exped"].value(1))
                step(dve.tensor_reduce(one[:, :, 1:2], tmp4[:, :, :], AX.X, ALU.add))
                step(dve.reciprocal(one[:, :, 2:3], one[:, :, 1:2]))
                step(dve.tensor_copy(esel[:, :, :], eall[:, :, 0:4]))
                step(dve.tensor_reduce(one[:, :, 3:4], esel[:, :, :], AX.X, ALU.max))
                pick(one[:, :, 3:4], esel[:, :, :], hot[:, :, 4:8])
                step(dve.tensor_scalar(tmp4[:, :, :], hot[:, :, 4:8], NEG, None, ALU.mult))
                step(dve.tensor_tensor(esel[:, :, :], esel[:, :, :], tmp4[:, :, :], ALU.add))
                step(dve.tensor_reduce(one[:, :, 4:5], esel[:, :, :], AX.X, ALU.max))
                pick(one[:, :, 4:5], esel[:, :, :], hot[:, :, 8:12])
                for g in range(4):
                    dve.tensor_tensor(first[:, :, 4 * g:4 * g + 4], hot[:, :, 4:8], over(hot[:, :, g:g + 1], 4), ALU.mult)
                    last = dve.tensor_tensor(second[:, :, 4 * g:4 * g + 4], hot[:, :, 8:12],
                                             over(hot[:, :, g:g + 1], 4), ALU.mult)
                step(last)
                dve.tensor_tensor(both[:, :, :], first[:, :, :], second[:, :, :], ALU.add).then_inc(f["made"].sem, 1)
                dve.tensor_tensor(one[:, :, 6:7], one[:, :, 4:5], one[:, :, 3:4], ALU.subtract)\
                    .then_inc(f["weighted"].sem, 1)
                dve.wait_ge(f["turned"].sem, f["turned"].value(1))
                dve.tensor_copy(rank[:, :, :], core.bank(1, P, 16 * NT).rearrange("p (t e) -> p t e", e=16))
                step(dve.tensor_copy(count[:, :, :], core.bank(2, P, 16 * NT).rearrange("p (t e) -> p t e", e=16)))
                for t in range(NT):
                    step(dve.tensor_tensor(before[:, t + 1, :], before[:, t, :], count[:, t, :], ALU.add))
                step(dve.tensor_tensor(rank[:, :, :], rank[:, :, :], before[:, 0:NT, :], ALU.add))
                step(dve.tensor_scalar(tiles[:, :], before[:, NT, :], 0.0, None, ALU.is_gt))
                for m in range(1, NT):
                    step(dve.scalar_tensor_tensor(out=tiles[:, :], in0=before[:, NT, :], scalar=float(P * m),
                                                  in1=tiles[:, :], op0=ALU.is_gt, op1=ALU.add))
                step(dve.tensor_copy(ends[:, 0, :], tiles[:, :]))
                for n in range(4):
                    a, b, d = n % 2, (n + 1) % 2, 1 << n
                    dve.tensor_copy(ends[:, b, 0:d], ends[:, a, 0:d])
                    step(dve.tensor_tensor(ends[:, b, d:16], ends[:, a, d:16], ends[:, a, 0:16 - d], ALU.add))
                step(dve.tensor_tensor(start[:, 0, :], ends[:, 0, :], tiles[:, :], ALU.subtract))
                step(dve.tensor_scalar(start[:, 0, :], start[:, 0, :], float(P), -1.0, ALU.mult, ALU.add))
                step(dve.tensor_tensor(rank[:, :, :], rank[:, :, :], start[:, :, :].broadcast_to([P, NT, 16]), ALU.add))
                dve.tensor_tensor(first[:, :, :], first[:, :, :], rank[:, :, :], ALU.mult)
                step(dve.tensor_tensor(second[:, :, :], second[:, :, :], rank[:, :, :], ALU.mult))
                dve.tensor_reduce(pos[:, 0, :], first[:, :, :], AX.X, ALU.add)
                step(dve.tensor_reduce(pos[:, 1, :], second[:, :, :], AX.X, ALU.add))
                dve.tensor_copy(posu[:, :, :], pos[:, :, :]).then_inc(f["made"].sem, 1)
                step(dve.tensor_tensor(passed[:, :, :], ends[0:1, 0:1, :].broadcast_to([1, TILES, 16]),
                                       over(core.const("tile_no", 1)[:, 0:TILES].rearrange("p (t o) -> p t o", o=1), 16),
                                       ALU.is_le))
                step(dve.tensor_reduce(index[:, :, :], passed[:, :, :], AX.X, ALU.add))
                step(dve.tensor_scalar(index[:, :, :], index[:, :, :], float(N_EXP - 1), None, ALU.min))
                for m in range(U, N_EXP, U):
                    step(dve.scalar_tensor_tensor(out=turn[:, :, :], in0=index[:, :, :], scalar=float(m),
                                                  in1=turn[:, :, :], op0=ALU.is_ge, op1=ALU.add))
                step(dve.scalar_tensor_tensor(out=turn[:, :, :], in0=turn[:, :, :], scalar=-float(U),
                                              in1=index[:, :, :], op0=ALU.mult, op1=ALU.add))
                dve.tensor_copy(tile_slot[:, :], turn[:, :, :].rearrange("p t o -> p (t o)"))
                dve.tensor_scalar(tile_ready[:, :], index[:, :, :].rearrange("p t o -> p (t o)"), 1.0, None, ALU.add)
                dve.tensor_copy(expert_end[:, :], ends[0:1, 0, :]).then_inc(f["made"].sem, 1)
                dve.wait_ge(f["exped"].sem, f["exped"].value(2))
                step(dve.tensor_scalar(one[:, :, 5:6], one[:, :, 6:7], 1.0, None, ALU.add))
                step(dve.reciprocal(one[:, :, 7:8], one[:, :, 5:6]))
                step(dve.tensor_tensor(weight[:, 0, 0:NT], one[:, :, 7], one[:, :, 2], ALU.mult))
                dve.tensor_tensor(weight[:, 1, 0:NT], one[:, :, 6], weight[:, 0, 0:NT], ALU.mult)

            @block.scalar
            def _(act):
                for t in range(NT):
                    if t == 2:
                        act.wait_ge(f["weighted"].sem, f["weighted"].value(1))
                        act.activation(tmp4[:, :, :], tmp4[:, :, :], ACT.Exp).then_inc(f["exped"].sem, 1)
                    act.wait_ge(f["rows_turned"].sem, f["rows_turned"].value(t + 1))
                    if t >= 2:
                        act.wait_ge(f[f"rows_stored{t % 2}"].sem, f[f"rows_stored{t % 2}"].value(16 * (t // 2)))
                    act.activation(rows[:, t % 2, :], core.psum[:, 4 + 2 * (t % 2):6 + 2 * (t % 2), :]
                                   .rearrange("p a b -> p (a b)"), ACT.Copy).then_inc(f["copied"].sem, 1)
                act.wait_ge(f["weighted"].sem, f["weighted"].value(2))
                act.activation(one[:, :, 6:7], one[:, :, 6:7], ACT.Exp).then_inc(f["exped"].sem, 1)

            @block.sync
            def _(sp):
                sp.wait_ge(f["made"].sem, f["made"].value(1))
                sp.dma_start(dram["slot_token"][0:TILES * P, :].rearrange("(j p) o -> j (p o)", p=P), no_token[:, :])\
                    .then_inc(f["stored"].sem, 16)
                load_first(sp)
                for t in range(NT):
                    sp.wait_ge(f["copied"].sem, f["copied"].value(t + 1))
                    sp.dma_start(dram["h_rows"][t * P:(t + 1) * P, :], rows[:, t % 2, :])\
                        .then_inc(f[f"rows_stored{t % 2}"].sem, 16)
                for z in range(2):
                    sp.wait_ge(f[f"rows_stored{z}"].sem, f[f"rows_stored{z}"].value(16 * (NT // 2)))

            @block.gpsimd
            def _(pool):
                pool.wait_ge(f["stored"].sem, f["stored"].value(16))
                pool.wait_ge(f["made"].sem, f["made"].value(3))
                for z in range(2):
                    for t in range(NT):
                        pool.indirect_dma_start(dram["slot_token"][0:TILES * P, :],
                                                bass.IndirectOffsetOnAxis(ap=posu[:, z, t:t + 1], axis=0),
                                                token[:, t:t + 1], None).then_inc(f["scattered"].sem, 16)
                pool.wait_ge(f["scattered"].sem, f["scattered"].value(32 * NT))
    for k, n in (("products_done", 1), ("made", 4), ("turned", 1), ("weighted", 2), ("exped", 2), ("stored", 16),
                 ("rows_turned", NT), ("copied", NT), ("rows_stored0", 16 * (NT // 2)), ("rows_stored1", 16 * (NT // 2)),
                 ("scattered", 32 * NT), ("gate_up", 1), ("down_done", 1)):
        f[k].advance(n)


def experts(core, l, parts):
    nc, f, dram = core.nc, core.flags, core.dram
    tokens = sum(tn for _, tn in parts)
    NT = tokens // P
    TILES = expert_tiles(tokens)
    ROUNDS = (TILES + U - 1) // U

    def round_of(i, last=False):
        return [(i, u) for u in range(TILES - U * (ROUNDS - 1) if last else U)]

    def at(name, i, u, n=0):
        return i * U + f[name].value(u + n)

    def loaded(name, i, u, n=0):
        return i * 16 + f[f"{name}{(u + n) % U}"].value(16 * (1 + (u + n) // U))

    with ExitStack() as stack:
        def sb(name, shape, dtype=F32):
            return stack.enter_context(nc.sbuf_tensor(f"{name}{l}", shape, dtype))
        weight = sb("pair_weight", [P, 2, NT])
        posu = sb("pair_slot", [P, 2, NT], U32)
        tile_slot = sb("tile_slot", [1, TILES], I32)
        tile_ready = sb("tile_ready", [1, TILES], I32)
        expert_end = sb("expert_end", [1, N_EXP], I32)
        GU = sb("gate_up_w", [P, U * 4096])
        DN = sb("down_w", [P, U * 2048])

        def weight_row(i, u):
            return dram["experts"][bass.ds(i * U + (u + N_EXP * l), 1), :, :].rearrange("e p n -> p (e n)")

        def load_gate_up(sp, i, u):
            sp.dma_start(GU[:, 4096 * u:4096 * (u + 1)], weight_row(i, u)[:, 0:4096]).then_inc(f[f"gu_loaded{u}"].sem, 16)

        def load_down(sp, i, u):
            sp.dma_start(DN[:, 2048 * u:2048 * (u + 1)], weight_row(i, u)[:, 4096:6144]).then_inc(f[f"dn_loaded{u}"].sem, 16)

        def load_first(sp):
            for u in range(U):
                load_gate_up(sp, 0, u)
                load_down(sp, 0, u)
        route(core, l, tokens, weight, posu, tile_slot, tile_ready, expert_end, load_first)

        with ExitStack() as inner:
            def tile_sb(name, shape, dtype=F32):
                return inner.enter_context(nc.sbuf_tensor(f"{name}{l}", shape, dtype))
            IDX = tile_sb("slot_tokens", [P, U], U32)
            HR = tile_sb("h_gathered", [P, U, D])
            SL = tile_sb("silu_a", [P, 256])
            HID = tile_sb("hid", [P, 256])
            HIDT = tile_sb("hid_t", [P, 256])
            h_flat = core.H[:, :, :].rearrange("p k t -> p (k t)")
            HT = [h_flat[:, n * D:(n + 1) * D] for n in range(U)]
            Y = [h_flat[:, (U + n) * D:(U + n + 1) * D] for n in range(U)]

            with nc.Block(f"experts{l}") as block:
                @block.sync
                def _(sp):
                    def load(i, u):
                        end = sp.value_load(expert_end[0:1, bass.ds(i * U + (u - U), 1)], min_val=0, max_val=TILES)
                        sp.wait_ge(f["gate_up"].sem, end + f["gate_up"].value(0))
                        load_gate_up(sp, i, u)
                        sp.wait_ge(f["down_done"].sem, end + f["down_done"].value(0))
                        load_down(sp, i, u)

                    def ready(i, u, n=0):
                        k = (u + n) % U
                        for name in ("gu_loaded", "dn_loaded"):
                            sp.wait_ge(f[f"{name}{k}"].sem, loaded(name, i, u, n))
                        sp.sem_inc(f["experts_ready"].sem, 1)

                    for u in range(1, U):
                        ready(0, u, -1)
                    with sp.Fori(1, N_EXP // U) as r:
                        for u in range(U):
                            load(r, u)
                            ready(r, u, -1)
                    for u in range(N_EXP % U):
                        load(N_EXP // U, u)
                        ready(N_EXP // U, u, -1)
                    ready(N_EXP // U, N_EXP % U - 1)

                @block.gpsimd
                def _(pool):
                    def load_index(i, u, n=0):
                        k = (u + n) % U
                        pool.dma_start(IDX[:, k:k + 1], dram["slot_token"][bass.ds(i * (U * P) + (u + n) * P, P), :])\
                            .then_inc(f[f"idx_loaded{k}"].sem, 16)

                    def gather(i, u, first=False, last=False):
                        pool.wait_ge(f[f"idx_loaded{u}"].sem, loaded("idx_loaded", i, u))
                        if not first:
                            pool.wait_ge(f["rows_turned"].sem, at("rows_turned", i, u, 1 - U))
                        if not (first and u + 1 < U):
                            pool.wait_ge(f[f"gathered{(u + 1) % U}"].sem, loaded("gathered", i, u, 1 - U))
                        if not last:
                            load_index(i, u, 1)
                        pool.indirect_dma_start(HR[:, u, :], None, dram["h_rows"][0:tokens, :],
                                                bass.IndirectOffsetOnAxis(ap=IDX[:, u:u + 1], axis=0))\
                            .then_inc(f[f"gathered{u}"].sem, 16)

                    load_index(0, 0)
                    for i, u in round_of(0):
                        gather(i, u, first=True)
                    with pool.Fori(1, ROUNDS - 1) as r:
                        for i, u in round_of(r):
                            gather(i, u)
                    tail = round_of(ROUNDS - 1, True)
                    for i, u in tail:
                        gather(i, u, last=(i, u) == tail[-1])

                @block.tensor
                def _(pe):
                    def turn_rows(i, u, n, first=False):
                        k = (u + n) % U
                        pe.wait_ge(f[f"gathered{k}"].sem, loaded("gathered", i, u, n))
                        if not first:
                            for half in ("turned_v", "turned_s"):
                                pe.wait_ge(f[half].sem, at(half, i, u, n))
                        for m in range(KD):
                            last = pe.transpose(core.bank(m // 4, P, P, P * (m % 4)), HR[:, k, m * P:(m + 1) * P],
                                                core.const("ident"))
                        last.then_inc(f["rows_turned"].sem, 1)

                    def turn_hidden(i, u, n, second=False):
                        pe.wait_ge(f["hid_ready"].sem, at("hid_ready", i, u, n + 1))
                        if not second:
                            pe.wait_ge(f["hidT_ready"].sem, at("hidT_ready", i, u, n))
                        for m in range(2):
                            last = pe.transpose(core.bank(3, P, P, P * m), HID[:, m * P:(m + 1) * P], core.const("ident"))
                        last.then_inc(f["hid_turned"].sem, 1)

                    def slot_of(i, u, n=0):
                        return pe.value_load(tile_slot[0:1, bass.ds(i * U + (u + n), 1)], min_val=0, max_val=U - 1)

                    def gate_up(i, u, k, number):
                        pe.wait_ge(f["experts_ready"].sem, number + f["experts_ready"].value(0))
                        for half in ("turned_v", "turned_s"):
                            pe.wait_ge(f[half].sem, at(half, i, u, 1))
                        products(pe, core.bank(2), [(HT[u][:, m * P:(m + 1) * P], GU[:, bass.ds(k * 4096 + m * 512, 512)])
                                                    for m in range(KD)]).then_inc(f["gate_up"].sem, 1)

                    def down(i, u, n, k, second=False):
                        pe.wait_ge(f["hidT_ready"].sem, at("hidT_ready", i, u, n + 1))
                        if not second:
                            for half in ("y_v", "y_s"):
                                pe.wait_ge(f[half].sem, at(half, i, u, n))
                        for half in range(2):
                            last = products(pe, core.bank(4 + half),
                                            [(HIDT[:, m * P:(m + 1) * P],
                                              DN[:, bass.ds(k * 2048 + (1024 * m + 512 * half), 512)])
                                             for m in range(2)])
                        last.then_inc(f["down_done"].sem, 1)

                    def tile(i, u, number=None, last=False):
                        ready = pe.value_load(tile_ready[0:1, bass.ds(i * U + u, 1)], min_val=1, max_val=N_EXP)
                        k = slot_of(i, u)
                        if number != 0:
                            k_before = slot_of(i, u, -1)
                        if not last:
                            turn_rows(i, u, 1)
                        if number != 0:
                            turn_hidden(i, u, -1, second=number == 1)
                        gate_up(i, u, k, ready)
                        if number != 0:
                            down(i, u, -1, k_before, second=number == 1)

                    turn_rows(0, 0, 0, first=True)
                    for i, u in round_of(0):
                        tile(i, u, number=u)
                    with pe.Fori(1, ROUNDS - 1) as r:
                        for i, u in round_of(r):
                            tile(i, u)
                    tail = round_of(ROUNDS - 1, True)
                    for i, u in tail:
                        tile(i, u, last=(i, u) == tail[-1])
                    k = slot_of(i, u)
                    turn_hidden(i, u, 0)
                    down(i, u, 0, k)

                @block.vector
                def _(dve):
                    def turned(i, u, n, first=False):
                        k = (u + n) % U
                        dve.wait_ge(f["rows_turned"].sem, at("rows_turned", i, u, n + 1))
                        if not first:
                            dve.wait_ge(f["gate_up"].sem, at("gate_up", i, u, n + 1 - U))
                        dve.tensor_copy(HT[k][:, 0:512], core.bank(0)).then_inc(f["turned_v"].sem, 1)

                    def hidden(i, u, first=False):
                        dve.wait_ge(f["gate_up"].sem, at("gate_up", i, u, 1))
                        dve.wait_ge(f["silued"].sem, at("silued", i, u, 1))
                        if not first:
                            dve.wait_ge(f["hid_turned"].sem, at("hid_turned", i, u))
                        dve.tensor_tensor(HID[:, :], SL[:, :], core.bank(2, P, 256, 256), ALU.mult)\
                            .then_inc(f["hid_ready"].sem, 1)

                    def hidden_turned(i, u, n, second=False):
                        dve.wait_ge(f["hid_turned"].sem, at("hid_turned", i, u, n + 1))
                        if not second:
                            dve.wait_ge(f["down_done"].sem, at("down_done", i, u, n))
                        dve.tensor_copy(HIDT[:, :], core.bank(3, P, 256)).then_inc(f["hidT_ready"].sem, 1)

                    def y_half(i, u, n, first=False):
                        k = (u + n) % U
                        dve.wait_ge(f["down_done"].sem, at("down_done", i, u, n + 1))
                        if not first:
                            dve.wait_ge(f[f"y_stored{k}"].sem, loaded("y_stored", i, u, n - U))
                        dve.tensor_copy(Y[k][:, 0:512], core.bank(4)).then_inc(f["y_v"].sem, 1)

                    def tile(i, u, number=None, last=False):
                        if not last:
                            turned(i, u, 1, first=number in (0, 1))
                        if number != 0:
                            hidden_turned(i, u, -1, second=number == 1)
                        hidden(i, u, first=number == 0)
                        if number != 0:
                            y_half(i, u, -1, first=number in (1, 2, 3))

                    turned(0, 0, 0, first=True)
                    for i, u in round_of(0) + round_of(1):
                        tile(i, u, number=U * i + u)
                    with dve.Fori(2, ROUNDS - 1) as r:
                        for i, u in round_of(r):
                            tile(i, u)
                    tail = round_of(ROUNDS - 1, True)
                    for i, u in tail:
                        tile(i, u, last=(i, u) == tail[-1])
                    hidden_turned(i, u, 0)
                    y_half(i, u, 0)

                @block.scalar
                def _(act):
                    def turned(i, u, n, first=False):
                        k = (u + n) % U
                        act.wait_ge(f["rows_turned"].sem, at("rows_turned", i, u, n + 1))
                        if not first:
                            act.wait_ge(f["gate_up"].sem, at("gate_up", i, u, n + 1 - U))
                        act.activation(HT[k][:, 512:1024], core.bank(1), ACT.Copy).then_inc(f["turned_s"].sem, 1)

                    def y_half(i, u, n, first=False):
                        k = (u + n) % U
                        act.wait_ge(f["down_done"].sem, at("down_done", i, u, n + 1))
                        if not first:
                            act.wait_ge(f[f"y_stored{k}"].sem, loaded("y_stored", i, u, n - U))
                        act.activation(Y[k][:, 512:1024], core.bank(5), ACT.Copy).then_inc(f["y_s"].sem, 1)
                        for half in ("y_v", "y_s"):
                            act.wait_ge(f[half].sem, at(half, i, u, n + 1))
                        act.dma_start(dram["y_rows"][bass.ds(i * (U * P) + (u + n) * P, P), :], Y[k])\
                            .then_inc(f[f"y_stored{k}"].sem, 16)

                    def tile(i, u, number=None, last=False):
                        if not last:
                            turned(i, u, 1, first=number in (0, 1))
                        act.wait_ge(f["gate_up"].sem, at("gate_up", i, u, 1))
                        if number != 0:
                            act.wait_ge(f["hid_ready"].sem, at("hid_ready", i, u))
                        act.activation(SL[:, :], core.bank(2, P, 256), ACT.Silu).then_inc(f["silued"].sem, 1)
                        if number != 0:
                            y_half(i, u, -1, first=number in (1, 2, 3))

                    turned(0, 0, 0, first=True)
                    for i, u in round_of(0) + round_of(1):
                        tile(i, u, number=U * i + u)
                    with act.Fori(2, ROUNDS - 1) as r:
                        for i, u in round_of(r):
                            tile(i, u)
                    tail = round_of(ROUNDS - 1, True)
                    for i, u in tail:
                        tile(i, u, last=(i, u) == tail[-1])
                    y_half(i, u, 0)
                    for n in range(1 - U, 1):
                        act.wait_ge(f[f"y_stored{(u + n) % U}"].sem, loaded("y_stored", i, u, n))
        for name in ("rows_turned", "turned_v", "turned_s", "gate_up", "silued", "hid_ready", "hid_turned",
                     "hidT_ready", "down_done", "y_v", "y_s"):
            f[name].advance(TILES)
        f["experts_ready"].advance(N_EXP)
        for name, count in (("gu_loaded", N_EXP), ("dn_loaded", N_EXP), ("idx_loaded", TILES), ("gathered", TILES),
                            ("y_stored", TILES)):
            for u in range(U):
                f[f"{name}{u}"].advance(16 * ((count - u + U - 1) // U))
        combine_pairs(core, l, parts, weight, posu, GU)


def combine_pairs(core, l, parts, weight, posu, space):
    nc, f, dram = core.nc, core.flags, core.dram
    tokens = sum(tn for _, tn in parts)
    NT = tokens // P
    TILES = expert_tiles(tokens)
    YP = space[:, 0:4 * D].rearrange("p (s z d) -> p s z d", s=2, z=2)
    YS = space[:, 4 * D:6 * D].rearrange("p (s d) -> p s d", s=2)
    with nc.Block(f"combine{l}") as block:
        @block.gpsimd
        def _(pool):
            for t in range(NT):
                if t >= 2:
                    pool.wait_ge(f["made"].sem, f["made"].value(t - 1))
                for z in range(2):
                    pool.indirect_dma_start(YP[:, t % 2, z, :], None, dram["y_rows"][0:TILES * P, :],
                                            bass.IndirectOffsetOnAxis(ap=posu[:, z, t:t + 1], axis=0))\
                        .then_inc(f[f"pair{t % 2}{z}"].sem, 16)

        @block.tensor
        def _(pe):
            for t in range(NT):
                pe.wait_ge(f["made"].sem, f["made"].value(t + 1))
                if t >= 2:
                    pe.wait_ge(f["added"].sem, f["added"].value(t - 1))
                for k in range(KD):
                    last = pe.transpose(core.bank(2 * (t % 2) + k // 4, P, P, P * (k % 4)), YS[:, t % 2, k * P:(k + 1) * P],
                                        core.const("ident"))
                last.then_inc(f["turned"].sem, 1)

        @block.vector
        def _(dve):
            def weighted_sum(t):
                dve.wait_ge(f[f"pair{t % 2}0"].sem, f[f"pair{t % 2}0"].value(16 * (t // 2 + 1)))
                dve.wait_ge(f[f"pair{t % 2}1"].sem, f[f"pair{t % 2}1"].value(16 * (t // 2 + 1)))
                if t >= 2:
                    dve.wait_ge(f["turned"].sem, f["turned"].value(t - 1))
                core.v_chain(dve, dve.tensor_scalar(YS[:, t % 2, :], YP[:, t % 2, 0, :], weight[:, 0, t:t + 1], None,
                                                    ALU.mult))
                dve.scalar_tensor_tensor(out=YS[:, t % 2, :], in0=YP[:, t % 2, 1, :], scalar=weight[:, 1, t:t + 1],
                                         in1=YS[:, t % 2, :], op0=ALU.mult, op1=ALU.add).then_inc(f["made"].sem, 1)

            weighted_sum(0)
            for t in range(NT):
                if t + 1 < NT:
                    weighted_sum(t + 1)
                dve.wait_ge(f["turned"].sem, f["turned"].value(t + 1))
                p = 0 if t * P < S else 1
                for m in range(KD):
                    last = dve.scalar_tensor_tensor(
                        out=core.X[:, m, t * P:(t + 1) * P], in0=core.bank(2 * (t % 2) + m // 4, P, P, P * (m % 4)),
                        scalar=core.mods[:, l, 40 + m, p:p + 1], in1=core.X[:, m, t * P:(t + 1) * P],
                        op0=ALU.mult, op1=ALU.add)
                last.then_inc(f["added"].sem, 1)
    for name in ("made", "turned", "added"):
        f[name].advance(NT)
    for u in range(2):
        for z in range(2):
            f[f"pair{u}{z}"].advance(16 * (NT // 2))


def store(core):
    nc, f, dram = core.nc, core.flags, core.dram
    with nc.Block("store") as block:
        @block.sync
        def _(sp):
            sp.dma_start(dram["outT"].rearrange("(k p) t -> p k t", p=P), core.X[:, :, 0:S]).then_inc(f["out_stored"].sem, 16)
            sp.wait_ge(f["out_stored"].sem, 16)


def build_program(nc, dram, stages=99):
    with ExitStack() as ctx:
        core = Core(nc, ctx, dram)
        parts = [LAT, CON]

        def mix_ffn(l, tokens_of):
            modulated_norm(core, f"norm_f{l}", l, 1, tokens_of)
            experts(core, l, tokens_of)

        def first():
            with nc.sbuf_tensor("table_ac", [12, TABLE], F32) as core.table_ac, \
                 nc.sbuf_tensor("table_b", [8, TABLE], F32) as core.table_b:
                with nc.sbuf_tensor("onehot", [32, TABLE], F32) as onehot, nc.sbuf_tensor("rel", [32, 20], F32) as rel:
                    load_inputs(core, onehot, rel)
                    derive(core, onehot, rel)
                first_block(core)
        program = [first,
                   lambda: modulation(core), lambda: even_layer(core), lambda: mix_ffn(0, parts),
                   lambda: odd_layer(core), lambda: mix_ffn(1, [LAT]), lambda: store(core)]
        for stage in program[0:stages]:
            stage()


def shape_constants():
    con = {}
    con["ident"] = np.eye(P)
    con["ones"] = np.ones((P, P))
    con["blocks"] = np.kron(np.eye(2), np.ones((HD, HD)))
    rot = np.zeros((P, P))
    for b in range(0, P, 32):
        for d in range(16):
            rot[b + 16 + d, b + d] = -1.0
            rot[b + d, b + 16 + d] = 1.0
    con["rot"] = rot
    s, t = np.arange(P)[:, None], np.arange(P)[None, :]
    con["causal_st"] = s <= t
    con["anti_st"] = s >= t
    pos = np.arange(S)
    ends = np.arange(NC_CMP) * 16 + 31
    con["cmask"] = np.where(ends[None, :] <= pos[:, None], 0.0, NEG).reshape(4, P, NC_CMP).transpose(1, 0, 2)\
        .reshape(P, -1)
    con["token_no"] = s + P * np.arange(T // P)[None, :]
    con["tile_no"] = np.tile(np.arange(32)[None, :], (P, 1))
    con["pick_row"] = np.tile(np.eye(2).reshape(1, 4), (P, 1))
    packed = np.concatenate([np.asarray(con[n], np.float32).reshape(P, -1) for n, _ in CONSTS], 1)
    n = np.maximum(511 - np.arange(TABLE), 0)
    large = 16 + (np.log(np.maximum(n, 1).astype(np.float32) / np.float32(16)) / np.float32(math.log(128 / 16))
                  * np.float32(16)).astype(np.int32)
    bucket = np.where(n < 16, n, np.minimum(large, 31))
    onehot = (bucket[None, :] == np.arange(32)[:, None]).astype(np.float32)
    row, col = np.arange(S) // 64, np.arange(S) % 64
    inv = np.float32(10000.0) ** (-np.arange(0, 32, 2, dtype=np.float32) / np.float32(32))
    ang = np.stack([row[:, None].astype(np.float32) * inv, col[:, None].astype(np.float32) * inv], 1)
    ang = np.tile(np.repeat(ang[:, :, None, :], 2, 2).reshape(S, HD).T, (2, 1))
    trig = np.stack([np.cos(ang), np.sin(ang)], 1).astype(np.float32)
    near_before = np.where(t >= s, 0.0, NEG)
    near_behind = np.where(t <= s, 0.0, NEG)
    zero = np.zeros((P, P))
    window = np.concatenate([zero, zero, near_before, zero, near_behind, zero, zero, zero, near_behind], 1)
    return packed, onehot, trig, window.astype(np.float32)


def pairs(w, heads, axis):
    order = np.arange(heads).reshape(2, heads // 2).T.reshape(-1)
    w = np.moveaxis(np.asarray(w), axis, -1)
    w = w.reshape(w.shape[:-1] + (heads, HD))[..., order, :].reshape(w.shape)
    return np.moveaxis(w, -1, axis)


def laid_out(a):
    D1 = {k: np.asarray(v) for k, v in a.items()}
    w = D1["w_in"][0]
    sizes = [512, 512, 512, 512, 128, 128, 512, 768, 24, 3072]
    at = np.concatenate([[0], np.cumsum(sizes)])
    aq, ak, av, bq, bk, bv, cq, ckv, cg, mg = (w[:, at[i]:at[i + 1]] for i in range(10))
    kv = [ckv[:, 128 * i:128 * i + 128] for i in range(6)]
    ev = D1["ev_w_in_2"][0]
    at = np.concatenate([[0], np.cumsum([256, 256, 512, 512, 32, 512, 128, 128])])
    gq, gk, gv, gr, lr, eq, ek, evv = (ev[:, at[i]:at[i + 1]] for i in range(8))
    od = D1["od_w_in_2"][0]
    ev_out = D1["ev_w_out_2"][0]
    ev_out = np.concatenate([ev_out[0:512], pairs(ev_out[512:1024], 8, 0)], 0)
    od_out = pairs(D1["od_w_out_2"][0], 16, 0)
    odq = pairs(od[:, 0:1024], 16, 1)
    wb = D1["w_branch"][0]
    wb = [wb[0], pairs(wb[1], 8, 0), pairs(wb[2], 8, 0)]
    src = {"proj0": aq, "proj1": ak, "proj2": pairs(bq, 8, 1), "proj3": pairs(cq, 8, 1),
           "proj4": np.concatenate([bk, kv[2], kv[4], kv[0]], 1), "proj5": np.concatenate([kv[1], bv, kv[3], kv[5]], 1),
           "proj6": av, "proj7": cg, "cmp0": D1["cmp_w1"][0, 0], "cmp1": D1["cmp_w1"][0, 1],
           "ev0": pairs(eq, 8, 1), "ev1": np.concatenate([ek, evv, lr], 1), "ev2": np.concatenate([gq, gk], 1),
           "ev3": gr, "ev4": gv, "od0": odq[:, 0:512], "od1": odq[:, 512:1024], "od2": od[:, 1024:1280]}
    for n in range(3):
        src[f"branch{n}"] = wb[n]
        for h in range(2):
            src[f"mg{n}_{h}"] = mg[:, 1024 * n + 512 * h:1024 * n + 512 * h + 512]
    for i in range(2):
        c = slice(512 * i, 512 * i + 512)
        src[f"out{i}"], src[f"ev_out{i}"], src[f"od_out{i}"] = D1["w_out"][0][:, c], ev_out[:, c], od_out[:, c]
    for i in range(8):
        src[f"up{i}"] = D1["w_up"][0][:, 512 * i:512 * i + 512]
        src[f"down{i}"] = D1["w_down"][0][:, P * i:P * i + P]
    experts = np.zeros((2 * N_EXP, P, 6144), np.float32)
    for l in range(2):
        for i in range(12):
            src[f"mod{12 * l + i}"] = D1["mod_w_2"][l][:, 512 * i:512 * i + 512]
        gate, up, down = (D1[n][l].reshape((N_EXP,) + D1[n].shape[3:]) for n in
                          ("exp_w_gate_2", "exp_w_up_2", "exp_w_down_2"))
        for e in range(N_EXP):
            gate_up = np.concatenate([gate[e], up[e]], 1)
            experts[N_EXP * l + e] = np.concatenate(
                [gate_up.reshape(KD, P, 512).transpose(1, 0, 2).reshape(P, 4096),
                 down[e].reshape(2, P, D).transpose(1, 0, 2).reshape(P, 2048)], 1)
    plan = plan_weights()
    weights = np.zeros((len(plan), P, 4096), np.float32)
    for c, (name, kt, n) in enumerate(plan):
        weights[c, :, 0:kt * n] = src[name].reshape(kt, P, n).transpose(1, 0, 2).reshape(P, kt * n)

    def column(v):
        return v.reshape(-1, P).T

    def twice(v):
        return np.tile(v, 2)[:, None]

    def rows(v):
        return np.tile(v.reshape(1, -1), (P, 1))

    lam = np.zeros((P, 4), np.float32)
    lam[0:HD] = D1["diff_lambda"][0].T
    par = {
        "norm_mix": column(D1["norm_mix"][0]), "norm_mlp": column(D1["norm_mlp"][0]),
        "qk_gain": np.concatenate([twice(D1["qk_gain"][0, i]) for i in range(8)], 1),
        "subln": D1["diff_subln"][0][:, None], "mod_b": column(D1["mod_b_2"].reshape(-1)),
        "norm_mix_2": column(D1["norm_mix_2"].reshape(-1)), "norm_ffn_2": column(D1["norm_ffn_2"].reshape(-1)),
        "gla_b": column(D1["gla_gate_b_2"][0].reshape(-1)), "gla_norm": D1["gla_out_norm_2"][0][:, None],
        "att_q": twice(D1["att_q_norm_2"][0]), "att_k": twice(D1["att_k_norm_2"][0]),
        "swa_q": twice(D1["swa_q_norm_2"][0]), "swa_k": twice(D1["swa_k_norm_2"][0]),
        "c": np.stack([column(D1["c_2"][0]), column(D1["c_ctx_2"])], 2).reshape(P, 16),
        "sinks": rows(D1["sinks"][0]), "swa_sink": rows(D1["swa_sink_2"][0]),
        "router_b": rows(np.concatenate([D1["router_group_b_2"], D1["router_expert_b_2"]], 1)),
        "cmp_pos": D1["cmp_pos"][0].reshape(2, 16, P).transpose(2, 0, 1).reshape(P, 32),
        "lambda": lam, "valid31": (np.arange(P) >= 31)[:, None].astype(np.float32),
    }
    router = np.concatenate([D1["router_group_w_2"], D1["router_expert_w_2"]], 2)
    gate_w = np.zeros((32, 2, 256), np.float32)
    for z in range(2):
        gate_w[16 * z:16 * z + 16, z] = D1["gla_gate_w_2"][0, z]
    rel = D1["rel_bias"]
    packed, onehot, trig, window = shape_constants()
    return {
        "xT": D1["x"][0].T, "ctxT": D1["ctx_2"][0].T, "weights": weights, "experts": experts,
        "par": np.concatenate([par[n].reshape(P, -1) for n, _ in PARAMS], 1), "con": packed,
        "router": router.reshape(2, KD, P, 20).transpose(2, 0, 1, 3), "gate_w": gate_w,
        "rel": np.concatenate([rel[:, 0:4], rel[:, 12:20], rel[:, 4:12]], 1), "onehot": onehot,
        "trig": trig, "window": window, "cmp_w2": D1["cmp_w2"][0],
    }


def kernel(**inputs):
    import concourse.bacc as _bacc
    from concourse.bass_utils import run_bass_kernel_spmd as _run

    nc = _bacc.Bacc("TRN2", target_bir_lowering=False, num_devices=1)
    arrays, dram = {}, {}
    for name, a in laid_out(inputs).items():
        a = np.ascontiguousarray(a)
        arrays[f"in_{name}"] = a
        dram[name] = nc.dram_tensor(f"in_{name}", a.shape, mybir.dt.from_np(a.dtype), kind="ExternalInput").ap()
    dram["bias"] = nc.dram_tensor("bias_tables", [20, P, TABLE], F32, kind="Internal").ap()
    dram["mod_rows"] = nc.dram_tensor("mod_rows", [2, 2, 6 * D], F32, kind="Internal").ap()
    dram["h_rows"] = nc.dram_tensor("h_rows", [T, D], F32, kind="Internal").ap()
    dram["slot_token"] = nc.dram_tensor("slot_token", [P * expert_tiles(T), 1], U32, kind="Internal").ap()
    dram["y_rows"] = nc.dram_tensor("y_rows", [P * expert_tiles(T), D], F32, kind="Internal").ap()
    dram["outT"] = nc.dram_tensor("outT", [D, S], F32, kind="ExternalOutput").ap()
    build_program(nc, dram)
    r = _run(nc, [arrays], core_ids=[0])
    return np.ascontiguousarray(r.results[0]["outT"].T)[None]
```
